# Optimizing a Trainium2 kernel written in Bass

```python
import math
import jax, jax.numpy as jnp
from jax import lax
import numpy as np

D_MODEL = 1024
BATCH = 1
SEQ = 2048
DEPTH = 1
DEC_BATCH = 8
DEC_SEQ = 4
PAST_LEN = 2048
PAGE_SIZE = 128

W_GROUP = D_MODEL // 4
D_MIX = 4 * W_GROUP
N_HEADS = 4
HEAD_DIM = W_GROUP // N_HEADS
N_IN_COLS = 9 * W_GROUP
CONV_A = 4
CONV_B = 3
RGLRU_C = 8.0
POOL_WINDOWS = (2, 4, 8, 16)
POOL_BUF = max(POOL_WINDOWS) - 1
POOL_GROUP = W_GROUP // len(POOL_WINDOWS)
D_FF = 4 * D_MODEL
Q_BLOCK = 128
SB_BIAS_INIT = -7.0
ALPHA = (2.0 * DEPTH) ** 0.25
BETA = (8.0 * DEPTH) ** -0.25
LN_EPS = 1e-5

kernel_name = "hybrid_parallel_heads_decode_step"

def layer_norm(x, g, b):
    xf = x.astype(jnp.float32)
    mu = jnp.mean(xf, -1, keepdims=True)
    var = jnp.mean(jnp.square(xf - mu), -1, keepdims=True)
    return ((xf - mu) * lax.rsqrt(var + LN_EPS) * g + b).astype(x.dtype)

def causal_conv(u, buf, w):
    width = w.shape[0]
    T = u.shape[1]
    ext = jnp.concatenate([buf.astype(u.dtype), u], axis=1)
    y = sum(w[j] * ext[:, j:j + T] for j in range(width))
    return y, ext[:, -(width - 1):]

def rglru(xc, h0, wa, ba, wx, bx, lam):
    B, T, _ = xc.shape
    xh = xc.reshape(B, T, N_HEADS, HEAD_DIM)
    r = jax.nn.sigmoid(jnp.einsum('bthi,hij->bthj', xh, wa).reshape(B, T, W_GROUP) + ba)
    i = jax.nn.sigmoid(jnp.einsum('bthi,hij->bthj', xh, wx).reshape(B, T, W_GROUP) + bx)
    log_a = -RGLRU_C * r.astype(jnp.float32) * jax.nn.softplus(-lam.astype(jnp.float32))
    a = jnp.exp(log_a)
    b = jnp.sqrt(-jnp.expm1(2.0 * log_a)) * (i * xc).astype(jnp.float32)

    def combine(c1, c2):
        a1, b1 = c1
        a2, b2 = c2
        return a1 * a2, a2 * b1 + b2

    a_cum, b_cum = lax.associative_scan(combine, (a, b), axis=1)
    h = a_cum * h0.astype(jnp.float32)[:, None, :] + b_cum
    return h.astype(xc.dtype), h[:, -1].astype(xc.dtype)

def pool_mixer(p, buf, p0, w_pool, scale):
    B, T, _ = p.shape
    ext = jnp.concatenate([buf.astype(p.dtype), p], axis=1)
    extf = ext.astype(jnp.float32)
    cs = jnp.concatenate([jnp.zeros_like(extf[:, :1]), jnp.cumsum(extf, axis=1)], axis=1)
    upper = cs[:, POOL_BUF + 1:]
    pos = p0 + jnp.arange(T)
    outs = []
    for g, w in enumerate(POOL_WINDOWS):
        sl = slice(g * POOL_GROUP, (g + 1) * POOL_GROUP)
        lower = cs[:, POOL_BUF + 1 - w:POOL_BUF + 1 - w + T, sl]
        cnt = jnp.minimum(w, pos + 1).astype(jnp.float32)[None, :, None]
        outs.append((upper[..., sl] - lower) / cnt)
    pooled = jnp.concatenate(outs, axis=-1)
    d = (pooled - p.astype(jnp.float32)).astype(p.dtype).reshape(B, T, len(POOL_WINDOWS), POOL_GROUP)
    y = jnp.einsum('btgi,gij->btgj', d, w_pool).reshape(B, T, W_GROUP) * scale
    return y, ext[:, -POOL_BUF:]

def sb_block(q, k, v, q_start, sb_bias):
    Tq, Tk = q.shape[1], k.shape[1]
    z = jnp.einsum('bqhd,bkhd->bhqk', q.astype(jnp.float32), k.astype(jnp.float32)) * (HEAD_DIM ** -0.5)
    z = z + sb_bias.astype(jnp.float32)[None, :, None, None]
    qpos = q_start + jnp.arange(Tq)
    kpos = jnp.arange(Tk)
    mask = kpos[None, :] < qpos[:, None]
    l = jnp.where(mask, jax.nn.log_sigmoid(-z), 0.0)
    later = jnp.flip(jnp.cumsum(jnp.flip(l, -1), -1), -1) - l
    w = jnp.where(mask, jnp.exp(jax.nn.log_sigmoid(z) + later), 0.0)
    return jnp.einsum('bhqk,bkhd->bqhd', w, v.astype(jnp.float32)).astype(q.dtype)

def stick_breaking(q, k_all, v_all, p0, sb_bias):
    T = q.shape[1]
    outs = []
    for qs in range(0, T, Q_BLOCK):
        qe = min(T, qs + Q_BLOCK)
        outs.append(sb_block(q[:, qs:qe], k_all[:, :p0 + qe], v_all[:, :p0 + qe], p0 + qs, sb_bias))
    return jnp.concatenate(outs, axis=1)

def mixer_layer(x, past_k, past_v, h0, buf_a, buf_b, buf_p, p0,
                w_in, conv_a_w, conv_a_b, lru_wa, lru_ba, lru_wx, lru_bx, lru_lambda,
                conv_b_w, sb_bias, pool_w, pool_scale, w_out):
    B, T, _ = x.shape
    proj = x @ w_in
    xa, ga, xb, gb, gc, q, k, v, xp = jnp.split(proj, 9, axis=-1)
    xc, new_buf_a = causal_conv(xa, buf_a, conv_a_w)
    xc = xc + conv_a_b
    ha, new_h = rglru(xc, h0, lru_wa, lru_ba, lru_wx, lru_bx, lru_lambda)
    ya = ha * jax.nn.gelu(ga)
    uc, new_buf_b = causal_conv(gc * xb, buf_b, conv_b_w)
    yb = gb * uc
    qh = q.reshape(B, T, N_HEADS, HEAD_DIM)
    kh = k.reshape(B, T, N_HEADS, HEAD_DIM)
    vh = v.reshape(B, T, N_HEADS, HEAD_DIM)
    if past_k is None:
        k_all, v_all = kh, vh
    else:
        k_all = jnp.concatenate([past_k.astype(kh.dtype), kh], axis=1)
        v_all = jnp.concatenate([past_v.astype(vh.dtype), vh], axis=1)
    yc = stick_breaking(qh, k_all, v_all, p0, sb_bias).reshape(B, T, W_GROUP)
    yd, new_buf_p = pool_mixer(xp, buf_p, p0, pool_w, pool_scale)
    out = jnp.concatenate([ya, yb, yc, yd], axis=-1) @ w_out
    return out, (kh, vh, new_h, new_buf_a, new_buf_b, new_buf_p)

def sq_relu_mlp(x, w1, w2):
    return jnp.square(jax.nn.relu(x @ w1)) @ w2

def trunk(x, p0, cache_k, cache_v, page_table, states, weights):
    (ln_in_g, ln_in_b, w_in, conv_a_w, conv_a_b, lru_wa, lru_ba, lru_wx, lru_bx, lru_lambda,
     conv_b_w, sb_bias, pool_w, pool_scale, w_out, ln1_g, ln1_b, w_ff1, w_ff2, ln2_g, ln2_b) = weights
    h_s, a_s, b_s, p_s = states
    x = layer_norm(x, ln_in_g, ln_in_b)
    new = []
    for l in range(DEPTH):
        if page_table is None:
            pk = pv = None
        else:
            nb, npg = page_table.shape
            pk = cache_k[l][page_table].reshape(nb, npg * PAGE_SIZE, N_HEADS, HEAD_DIM)
            pv = cache_v[l][page_table].reshape(nb, npg * PAGE_SIZE, N_HEADS, HEAD_DIM)
        mix, st = mixer_layer(x, pk, pv, h_s[l], a_s[l], b_s[l], p_s[l], p0,
                              w_in[l], conv_a_w[l], conv_a_b[l], lru_wa[l], lru_ba[l], lru_wx[l],
                              lru_bx[l], lru_lambda[l], conv_b_w[l], sb_bias[l], pool_w[l], pool_scale[l],
                              w_out[l])
        x = layer_norm(ALPHA * x + mix, ln1_g[l], ln1_b[l])
        x = layer_norm(ALPHA * x + sq_relu_mlp(x, w_ff1[l], w_ff2[l]), ln2_g[l], ln2_b[l])
        new.append(st)
    stacked = [jnp.stack([s[j] for s in new]) for j in range(6)]
    return x, stacked

def setup_inputs(seed: int = 0) -> dict:
    key = jax.random.key(seed)
    ks = iter(jax.random.split(key, 48))

    def nrm(shape, s):
        return jax.random.normal(next(ks), shape, jnp.float32) * s

    n_pages = PAST_LEN // PAGE_SIZE
    n_pool = (DEC_BATCH * n_pages * 5) // 4
    page_table = jax.random.permutation(next(ks), n_pool)[:DEC_BATCH * n_pages]
    page_table = page_table.reshape(DEC_BATCH, n_pages).astype(jnp.int32)
    u = jax.random.uniform(next(ks), (DEPTH, W_GROUP), jnp.float32, 0.9, 0.999)
    lru_lambda = jnp.log(u) - jnp.log1p(-u)
    return {
        "x_prompt": nrm((BATCH, SEQ, D_MODEL), 1.0),
        "x_sample": nrm((DEC_BATCH, DEC_SEQ, D_MODEL), 1.0),
        "cache_k": nrm((DEPTH, n_pool, PAGE_SIZE, N_HEADS, HEAD_DIM), 1.0),
        "cache_v": nrm((DEPTH, n_pool, PAGE_SIZE, N_HEADS, HEAD_DIM), 1.0),
        "state_rglru_h": nrm((DEPTH, DEC_BATCH, W_GROUP), 0.5),
        "state_conv_a": nrm((DEPTH, DEC_BATCH, CONV_A - 1, W_GROUP), 1.0),
        "state_conv_b": nrm((DEPTH, DEC_BATCH, CONV_B - 1, W_GROUP), 1.0),
        "state_pool": nrm((DEPTH, DEC_BATCH, POOL_BUF, W_GROUP), 1.0),
        "page_table": page_table,
        "ln_in_g": 1.0 + nrm((D_MODEL,), 0.02),
        "ln_in_b": nrm((D_MODEL,), 0.02),
        "w_in": nrm((DEPTH, D_MODEL, N_IN_COLS), D_MODEL ** -0.5),
        "conv_a_w": nrm((DEPTH, CONV_A, W_GROUP), CONV_A ** -0.5),
        "conv_a_b": nrm((DEPTH, W_GROUP), 0.01),
        "lru_wa": nrm((DEPTH, N_HEADS, HEAD_DIM, HEAD_DIM), HEAD_DIM ** -0.5),
        "lru_ba": nrm((DEPTH, W_GROUP), 0.01),
        "lru_wx": nrm((DEPTH, N_HEADS, HEAD_DIM, HEAD_DIM), HEAD_DIM ** -0.5),
        "lru_bx": nrm((DEPTH, W_GROUP), 0.01),
        "lru_lambda": lru_lambda,
        "conv_b_w": nrm((DEPTH, CONV_B, W_GROUP), CONV_B ** -0.5),
        "sb_bias": SB_BIAS_INIT + nrm((DEPTH, N_HEADS), 0.1),
        "pool_w": nrm((DEPTH, len(POOL_WINDOWS), POOL_GROUP, POOL_GROUP), POOL_GROUP ** -0.5),
        "pool_scale": 1.0 + nrm((DEPTH, W_GROUP), 0.02),
        "w_out": nrm((DEPTH, D_MIX, D_MODEL), BETA * D_MIX ** -0.5),
        "ln1_g": 1.0 + nrm((DEPTH, D_MODEL), 0.02),
        "ln1_b": nrm((DEPTH, D_MODEL), 0.02),
        "w_ff1": nrm((DEPTH, D_MODEL, D_FF), BETA * D_MODEL ** -0.5),
        "w_ff2": nrm((DEPTH, D_FF, D_MODEL), BETA * D_FF ** -0.5),
        "ln2_g": 1.0 + nrm((DEPTH, D_MODEL), 0.02),
        "ln2_b": nrm((DEPTH, D_MODEL), 0.02),
    }

def reference(x_prompt, x_sample, cache_k, cache_v, state_rglru_h, state_conv_a, state_conv_b, state_pool,
              page_table, ln_in_g, ln_in_b, w_in, conv_a_w, conv_a_b, lru_wa, lru_ba, lru_wx, lru_bx,
              lru_lambda, conv_b_w, sb_bias, pool_w, pool_scale, w_out, ln1_g, ln1_b, w_ff1, w_ff2, ln2_g, ln2_b):
    weights = (ln_in_g, ln_in_b, w_in, conv_a_w, conv_a_b, lru_wa, lru_ba, lru_wx, lru_bx, lru_lambda,
               conv_b_w, sb_bias, pool_w, pool_scale, w_out, ln1_g, ln1_b, w_ff1, w_ff2, ln2_g, ln2_b)
    B = x_prompt.shape[0]
    dt = x_prompt.dtype
    prompt_states = (jnp.zeros((DEPTH, B, W_GROUP), dt),
                     jnp.zeros((DEPTH, B, CONV_A - 1, W_GROUP), dt),
                     jnp.zeros((DEPTH, B, CONV_B - 1, W_GROUP), dt),
                     jnp.zeros((DEPTH, B, POOL_BUF, W_GROUP), dt))
    y_prompt, sp = trunk(x_prompt, 0, None, None, None, prompt_states, weights)
    sample_states = (state_rglru_h, state_conv_a, state_conv_b, state_pool)
    past_len = page_table.shape[1] * PAGE_SIZE
    y_sample, ss = trunk(x_sample, past_len, cache_k, cache_v, page_table, sample_states, weights)
    return (y_prompt, y_sample, sp[0], sp[1], ss[0], ss[1], sp[2], ss[2], sp[3], ss[3], sp[4], ss[4], sp[5], ss[5])


_drawn_inputs = setup_inputs


def setup_inputs(seed=0):
    import zlib

    import numpy as np

    out = dict(_drawn_inputs(seed))
    spreads = {}
    factors = {'cache_k': 6.439,
     'cache_v': 5.132,
     'lru_ba': 22.691,
     'lru_bx': 8.0,
     'sb_bias': 8.0,
     'pool_scale': 27.862,
     'ln1_g': 7.765,
     'ln1_b': 7.541,
     'ln2_g': 7.448,
     'ln2_b': 7.98}
    for name, (base, spread) in spreads.items():
        noise = np.random.default_rng([zlib.crc32(name.encode()), seed]).standard_normal(out[name].shape)
        drawn = base * np.exp(spread * noise) if base else spread * noise
        out[name] = __import__('jax').numpy.asarray(drawn.astype(out[name].dtype))
    for name, factor in factors.items():
        out[name] = (out[name] * factor).astype(out[name].dtype)
    return out
```

```python
from contextlib import ExitStack, contextmanager

import numpy as np
import concourse.bass as bass
from concourse import mybir

F32 = mybir.dt.float32
F32R = mybir.dt.float32r
I32 = mybir.dt.int32
ACT = mybir.ActivationFunctionType
ALU = mybir.AluOpType

P = 128
D = 1024
KT = D // P
SEQ = 2048
DECB, DECT = 8, 4
SMP = DECB * DECT
TOK = SEQ + SMP
BLK = 416
NB = TOK // BLK
ROW = 104
NR = BLK // ROW
NC_IN = 18
FT = 32
STEPS = KT + FT + KT * (FT // KT)
HD = 64
NH = 4
PAGE = 128
NPG = 16
PAST = NPG * PAGE
QT = SEQ // P
CHW = 512
ALPHA = 2.0 ** 0.25
EPS = 1e-5
RC = 8.0
BUFA, BUFB, BUFP = 3, 2, 15
WINDOWS = (2, 4, 8, 16)
XA, GA, XB, GB, GC, Q, K, V, XP = range(9)
ORDER = [(g, c) for g in (XA, GA, XB, GC, GB, XP, K, V, Q) for c in (0, 1)]
AT = {gc: n for n, gc in enumerate(ORDER)}
K0 = AT[K, 0]
PCW, PCB, PBA, PBX, PLAM, PBW, PSC, PINV, NPV = 0, 4, 5, 6, 7, 8, 11, 12, 13
SO_H, SO_A, SO_B, SO_P = 0, 1 + DECB, 1 + DECB + BUFA * (1 + DECB), 1 + DECB + (BUFA + BUFB) * (1 + DECB)
SO_N = (1 + DECB) * (1 + BUFA + BUFB + BUFP)


NAT0 = NR
CONST_ALL = 16 * 18


def ext_of(tile, halo):
    a = SEQ + halo
    return tile[:, a:a + DECB * (halo + DECT)].rearrange("p (b t) -> p b t", b=DECB)


def new_of(tile):
    return tile[:, SEQ:TOK].rearrange("p (b t) -> p b t", b=DECB)


def rev(ap):
    return ap[:, ::-1]


def groups_until(n):
    return sum(-(-(m % QT + 1) // 4) for m in range(n))


def build(nc, x_all, w_all, pvec, lnp, rows2, gates_a, gates_x, poolw, sbh, sbr, masks, ident_d, ck, cv, ptab,
          st_h, st_a, st_b, st_p, y_out, kv_out, so_out):
    ctx = ExitStack()
    with ctx:
        def sb(name, shape, dt=F32, stack=ctx):
            return stack.enter_context(nc.sbuf_tensor(name, shape, dt))

        def sem(name):
            return ctx.enter_context(nc.semaphore(name))

        proj_d = nc.dram_tensor("proj_scratch", (NC_IN, P, TOK), F32, kind="Internal").ap()
        x1_d = nc.dram_tensor("x1_scratch", (KT, P, TOK), F32, kind="Internal").ap()
        y_d = nc.dram_tensor("mixed_scratch", (KT, P, TOK), F32, kind="Internal").ap()
        vn_d = nc.dram_tensor("vnew_scratch", (SMP, 2 * P), F32, kind="Internal").ap()

        PS = ctx.enter_context(nc.psum_tensor("PS", [P, 8, 512], F32))

        ident = sb("ident", [P, P])
        raw = sb("w_raw", [P, 2, KT * P])
        wh = sb("w_hi", [P, 2, KT * P], F32R)
        wl = sb("w_lo", [P, 2, KT * P], F32R)
        pv = sb("pv", [P, 2, NPV])
        ln_gb = sb("ln_gb", [P, 4, KT])
        mask = sb("mask", [P, DECT + 32])
        hs = sb("hs", [P, 2, DECB])
        bias_h = sb("bias_h", [P, NH + 1])
        nbias_h = sb("nbias_h", [P, NH + 1])
        bn = sb("bn", [P, 4, 2, 6])
        mv = sb("mv", [P, 4, 2])
        var = sb("var", [P, 4])
        std = sb("std", [P, 4])
        rstd = sb("rstd", [P, 4])
        nmr = sb("nmr", [P, 4])
        gsel = sb("gsel", [P, 2, 3, P])
        lam = sb("lam", [P, 2, 8])
        so = sb("so", [P, 2, SO_N])

        with ExitStack() as e1:
            xh = sb("x_hi", [P, KT, TOK], F32R, e1)
            xl = sb("x_lo", [P, KT, TOK], F32R, e1)
            with ExitStack() as e:
                xin = sb("xin", [P, NR, D], F32, e)
                nat1 = sb("nat1", [P, NR, D], F32, e)
                t1 = sb("t1", [P, KT, BLK], F32, e)
            with ExitStack() as e:
                stage = sb("stage", [P, 2, TOK], F32, e)
        with ExitStack() as e:
            MW = SEQ + BUFP + DECB * (BUFP + DECT)
            mx = [sb(f"mx{n}", [P, MW], F32, e) for n in range(8)]
            qbd = sb("qbd", [P, 2368], F32, e)
            kqs = sb("kqs", [P, 6, SMP], F32, e)
            kpg = sb("kpg", [P, 2, 4, 2 * P], F32, e)
            kts = sb("kts", [P, 2, 2, CHW], F32, e)
            vpg = sb("vpg", [P, 2, 4, 2 * P], F32, e)
            vnew = sb("vnew", [DECT, 2 * P], F32, e)
            vnat = sb("vnat", [SMP, 2 * P], F32, e)
            sS = sb("sS", [P, PAST + DECT], F32, e)
            nS = sb("nS", [P, PAST + DECT], F32, e)
            pS = sb("pS", [P, PAST + DECT + 1], F32, e)
            wtS = sb("wtS", [P, NPG, P], F32, e)
            wtN = sb("wtN", [DECT, P], F32, e)
            ycs = sb("ycs", [P, 2, SMP], F32, e)
            ptb = sb("ptb", [1, DECB * NPG], I32, e)
        with ExitStack() as e:
            qT = sb("qT", [P, SEQ], F32, e)
            kT = sb("kT", [P, SEQ], F32, e)
            vT = sb("vT", [P, SEQ], F32, e)
            vN = sb("vN", [P, QT, P], F32, e)
            sP = sb("sP", [P, 2, SEQ], F32, e)
            nP = sb("nP", [P, 2, SEQ], F32, e)
            pP = sb("pP", [P, SEQ + 1], F32, e)
            wtP = sb("wtP", [P, 2, CHW], F32, e)
            ycT = sb("ycT", [P, SEQ], F32, e)
        with ExitStack() as e:
            hh = sb("h_hi", [P, FT, BLK], F32R, e)
            hl = sb("h_lo", [P, FT, BLK], F32R, e)
            ah = sb("a_hi", [P, KT, BLK], F32R, e)
            al = sb("a_lo", [P, KT, BLK], F32R, e)
            t3 = sb("t3", [P, KT, BLK], F32, e)
            nat3 = sb("nat3", [P, NR * D], F32, e)
            rbuf = sb("rbuf", [P, 2, BLK], F32, e)
            hf = sb("hf", [P, BLK], F32, e)
            gb2 = sb("gb2", [P, 2, D], F32, e)
        nat3t = nat3[:, :].rearrange("p (j d) -> p j d", j=NR)
        yin = nat3[:, 0:KT * BLK].rearrange("p (k t) -> p k t", k=KT)

        s_const = sem("const_in")
        s_raw = [sem("raw_in0"), sem("raw_in1")]
        s_wh, s_wl = sem("w_hi_made"), sem("w_lo_made")
        s_xin, s_t1st = sem("xin_in"), sem("x1_stored")
        s_ve, s_std, s_nmr = sem("var_made"), sem("std_made"), sem("nmr_made")
        s_nat = sem("tile_normalised")
        s_bt = sem("back_transposed")
        s_xh, s_xf, s_xl = sem("x_hi_made"), sem("x_full_made"), sem("x_lo_made")
        s_grp, s_ev1 = sem("proj_group_done"), sem("proj_evacuated")
        s_stg = [sem("stage_stored0"), sem("stage_stored1")]
        s_act, s_dve, s_pool = sem("act_own"), sem("dve_own"), sem("pool_own")
        s_mld = [sem("mix_loaded_a"), sem("mix_loaded_b"), sem("mix_loaded_d")]
        s_mzero = sem("mix_halo_zeroed")
        s_xc, s_gps, s_gev = sem("xc_made"), sem("gate_product_done"), sem("gate_evacuated")
        s_mxa, s_mxv = sem("mix_act_made"), sem("mix_dve_made")
        s_mst = [sem("ya_stored"), sem("yb_stored"), sem("yd_stored")]
        s_scan = sem("scan_done")
        s_lam = sem("lambda_step")
        s_mfree = sem("mix_tiles_free")
        s_qz, s_qbd, s_kqs = sem("qbd_zeroed"), sem("qbd_made"), sem("kqs_in")
        s_pt = sem("page_table_in")
        s_kin = [sem("k_pages_in0"), sem("k_pages_in1")]
        s_ktr, s_kte, s_kmm = sem("k_transposed"), sem("kT_evacuated"), sem("k_product_done")
        s_zs, s_sns, s_zn = sem("z_sample_done"), sem("sn_sample_made"), sem("z_new_done")
        s_ws, s_wtr, s_wte = sem("w_sample_made"), sem("w_sample_transposed"), sem("wT_sample_made")
        s_vin = [sem("v_pages_in0"), sem("v_pages_in1")]
        s_vuse, s_vnin, s_vnuse = sem("v_pages_used"), sem("v_new_in"), sem("v_new_used")
        s_vnt, s_vnat, s_vnst = sem("v_new_transposed"), sem("v_new_natural"), sem("v_new_stored")
        s_yse, s_yst = sem("yc_sample_made"), sem("yc_stored")
        s_qkv, s_pair, s_vtr, s_vnp = sem("qkv_in"), sem("pair_done"), sem("v_transposed"), sem("v_natural")
        s_z, s_sn, s_msk, s_w = sem("z_done"), sem("sn_made"), sem("diag_masked"), sem("w_made")
        s_tr, s_wt, s_av, s_yc = sem("w_transposed"), sem("wT_made"), sem("av_group_done"), sem("yc_made")
        s_ycs = sem("yc_prompt_stored")
        s_yin, s_x1in = sem("y_in"), sem("x1_in")
        s_yh, s_yl = sem("y_hi_made"), sem("y_lo_made")
        s_step, s_oev, s_ft = sem("step_done"), sem("outproj_evacuated"), sem("forward_transposed")
        s_r, s_hh, s_hf, s_hl = sem("relu_made"), sem("h_hi_made"), sem("h_full_made"), sem("h_lo_made")
        s_fev = sem("mlp_evacuated")
        s_row, s_out, s_so = sem("row_scaled"), sem("y_stored"), sem("state_stored")
        s_rowfree = sem("nat3_free")

        def wait_apart(eng, sem, value):
            eng.wait_ge(sem, value)
            eng.nop(nofuse=True)

        class Tally:

            def __init__(self, eng, sem):
                self.eng, self.sem, self.base, self.n = eng, sem, 0, 0

            def up(self, ins):
                ins.then_inc(self.sem, 1)
                self.n += 1

            def sync(self):
                wait_apart(self.eng, self.sem, self.base + self.n)

            def op(self, ins):
                self.up(ins)
                self.sync()

            @contextmanager
            def loop(self, count, per):
                base, n = self.base, self.n
                with self.eng.Fori(0, count) as i:
                    self.base, self.n = base + n + i * per, 0
                    yield i
                    assert self.n == per, (self.n, per)
                self.base, self.n = base, n + count * per

        block = ctx.enter_context(nc.Block())

        @block.sync
        def _(sp):
            n_const = [0]

            def const(dst, src):
                sp.dma_start(dst, src).then_inc(s_const, 16)
                n_const[0] += 16

            def load_raw(slot, tile):
                sp.dma_start(raw[:, slot, :], w_all[bass.ds(tile, 1)].rearrange("o p n -> p (o n)")).then_inc(
                    s_raw[slot], 16)

            sp.sem_inc(s_nat, NAT0)
            sp.sem_inc(s_vnuse, 1)
            sp.sem_inc(s_pair, 1)
            const(ident[:, :], ident_d)
            const(ln_gb[:, :, :], lnp)
            load_raw(0, 0)
            load_raw(1, 1)
            with sp.Fori(0, NB) as b:
                sp.wait_ge(s_nat, b * NR + NAT0)
                sp.dma_start(xin[0:ROW], x_all[bass.ds(b * BLK, BLK)].rearrange("(j p) d -> p j d", p=ROW)).then_inc(
                    s_xin, 16)
            const(pv[:, :, :], pvec)
            const(mask[:, :], masks)
            const(bias_h[:, 0:NH], sbh)
            const(bias_h[:, NH:NH + 1], sbr)
            sp.wait_ge(s_mzero, 1)
            for c in range(2):
                for n, src in enumerate((gates_a, gates_x, poolw)):
                    for h in range(2):
                        const(gsel[HD * h:HD * h + HD, c, n, HD * h:HD * h + HD], src[2 * c + h])
            assert n_const[0] == CONST_ALL

            def proj_steps(first, last, dst):
                with sp.Fori(first // 2, last // 2) as i:
                    for u in range(2):
                        sp.wait_ge(s_wl, i * 2 + (u + 1))
                        load_raw(u, i * 2 + (u + 2))
                        sp.wait_ge(s_ev1, i * 10 + (5 * u + 10))
                        sp.dma_start(dst[bass.ds(i * 2 + (u - (first if dst is kv_out else 0)), 1)].rearrange(
                            "o p t -> p (o t)"), stage[:, u, :]).then_inc(s_stg[u], 16)

            proj_steps(0, K0, proj_d)
            proj_steps(K0, K0 + 4, kv_out)
            proj_steps(K0 + 4, NC_IN, proj_d)
            for u in range(2):
                sp.wait_ge(s_stg[u], 16 * (NC_IN // 2) + 16)

            for c in range(2):
                if c:
                    sp.wait_ge(s_mfree, 3 * c)
                for dst, t in ((mx[0][:, BUFA:BUFA + SEQ], XA), (mx[1][:, 0:SEQ], GA)):
                    sp.dma_start(dst, proj_d[AT[t, c], :, 0:SEQ]).then_inc(s_mld[0], 16)
                sp.dma_start(ext_of(mx[0], BUFA)[:, :, BUFA:], new_of(proj_d[AT[XA, c]])).then_inc(s_mld[0], 16)
                sp.dma_start(ext_of(mx[0], BUFA)[:, :, 0:BUFA], st_a[c]).then_inc(s_mld[0], 16)
                sp.dma_start(mx[1][:, SEQ:TOK], proj_d[AT[GA, c], :, SEQ:TOK]).then_inc(s_mld[0], 16)
                sp.dma_start(hs[:, c, :], st_h[c]).then_inc(s_mld[0], 16)
                sp.wait_ge(s_mxv, 2 * c + 1)
                sp.dma_start(y_d[0 + c], mx[6][:, 0:TOK]).then_inc(s_mst[0], 16)
                sp.wait_ge(s_mfree, 3 * c + 1)
                sp.dma_start(mx[0][:, 0:TOK], proj_d[AT[XB, c]]).then_inc(s_mld[1], 16)
                sp.dma_start(mx[1][:, 0:TOK], proj_d[AT[GC, c]]).then_inc(s_mld[1], 16)
                sp.dma_start(mx[2][:, 0:TOK], proj_d[AT[GB, c]]).then_inc(s_mld[1], 16)
                sp.dma_start(ext_of(mx[3], BUFB)[:, :, 0:BUFB], st_b[c]).then_inc(s_mld[1], 16)
                sp.wait_ge(s_mxv, 2 * c + 2)
                sp.dma_start(y_d[2 + c], mx[4][:, 0:TOK]).then_inc(s_mst[1], 16)
                sp.wait_ge(s_mfree, 3 * c + 2)
                sp.dma_start(mx[0][:, BUFP:BUFP + SEQ], proj_d[AT[XP, c], :, 0:SEQ]).then_inc(s_mld[2], 16)
                sp.dma_start(ext_of(mx[0], BUFP)[:, :, BUFP:], new_of(proj_d[AT[XP, c]])).then_inc(s_mld[2], 16)
                sp.dma_start(ext_of(mx[0], BUFP)[:, :, 0:BUFP], st_p[c]).then_inc(s_mld[2], 16)
                sp.wait_ge(s_mxa, c + 1)
                sp.dma_start(y_d[6 + c], mx[6][:, 0:TOK]).then_inc(s_mst[2], 16)
            sp.wait_ge(s_mfree, 6)
            sp.dma_start(so_out, so[:, :, :]).then_inc(s_so, 16)

            sp.dma_start(ptb[:, :], ptab).then_inc(s_pt, 16)
            for c in range(2):
                for n, (src, t) in enumerate(((proj_d, AT[Q, 0]), (kv_out, 0), (kv_out, 2))):
                    sp.dma_start(kqs[:, 2 * n + c, :], src[t + c, :, SEQ:TOK]).then_inc(s_kqs, 16)
            sp.wait_ge(s_pt, 16)
            with sp.Fori(0, NPG // 4) as c:
                for b in range(DECB):
                    ids = [sp.value_load(ptb[0:1, bass.ds(c * 4 + (b * NPG + g), 1)], min_val=0, max_val=ck.shape[0] - 1)
                           for g in range(4)]
                    sp.wait_ge(s_ktr, c * DECB + (b + 1))
                    for g in range(4):
                        sp.dma_start(kpg[:, b % 2, g, :], ck[bass.ds(ids[g], 1)].rearrange("o p n -> p (o n)")).then_inc(
                            s_kin[b % 2], 16)
            sp.wait_ge(s_vnat, 2)
            sp.dma_start(vn_d, vnat[:, :]).then_inc(s_vnst, 16)
            sp.wait_ge(s_vnst, 16)
            with sp.Fori(0, DECB) as b:
                sp.wait_ge(s_vnuse, b + 1)
                sp.dma_start(vnew[:, :], vn_d[bass.ds(b * DECT, DECT)]).then_inc(s_vnin, 16)
                for c in range(4):
                    ids = [sp.value_load(ptb[0:1, bass.ds(b * NPG + (c * 4 + g), 1)], min_val=0, max_val=ck.shape[0] - 1)
                           for g in range(4)]
                    sp.wait_ge(s_vuse, b * 4 + (c + 1))
                    for g in range(4):
                        sp.dma_start(vpg[:, c % 2, g, :], cv[bass.ds(ids[g], 1)].rearrange("o p n -> p (o n)")).then_inc(
                            s_vin[c % 2], 16)
            sp.wait_ge(s_yse, 4)
            for c in range(2):
                sp.dma_start(y_d[4 + c, :, SEQ:TOK], ycs[:, c, :]).then_inc(s_yst, 16)
            sp.wait_ge(s_yst, 32)
            for m in s_mst:
                sp.wait_ge(m, 32)
            sp.wait_ge(s_so, 16)

            with sp.Fori(0, 2) as hp:
                sp.wait_ge(s_pair, hp + 1)
                sp.dma_start(qT[:, :], proj_d[bass.ds(hp + AT[Q, 0], 1), :, 0:SEQ].rearrange("o p t -> p (o t)")).then_inc(s_qkv, 16)
                sp.dma_start(kT[:, :], kv_out[bass.ds(hp, 1), :, 0:SEQ].rearrange("o p t -> p (o t)")).then_inc(s_qkv, 16)
                sp.dma_start(vT[:, :], kv_out[bass.ds(hp + 2, 1), :, 0:SEQ].rearrange("o p t -> p (o t)")).then_inc(s_qkv, 16)
                sp.wait_ge(s_yc, hp * 32 + 32)
                sp.dma_start(y_d[bass.ds(hp + 4, 1), :, 0:SEQ].rearrange("o p t -> p (o t)"), ycT[:, :]).then_inc(s_ycs, 16)

            sp.wait_ge(s_pair, 3)
            sp.wait_ge(s_ycs, 48)
            const(gb2[:, :, :], rows2)
            with sp.Fori(0, NB) as b:
                with sp.Fori(0, (STEPS - 2) // 2) as i:
                    for u in range(2):
                        sp.wait_ge(s_wl, b * STEPS + i * 2 + (NC_IN + u + 1))
                        load_raw(u, i * 2 + (NC_IN + 2 + u))
                for u in range(2):
                    sp.wait_ge(s_wl, b * STEPS + (NC_IN + STEPS - 2 + u + 1))
                    load_raw(u, NC_IN + u)
            sp.wait_ge(s_out, 16 * NR * NB)

        @block.tensor
        def _(pe):
            def back(b, base):
                nat = nat1 if base == 0 else nat3t
                for k in range(KT):
                    if k >= 4:
                        pe.wait_ge(s_xf, b * KT + (base + k - 3))
                    for j in range(NR):
                        ins = pe.transpose(PS[:, 4 + k % 4, j * ROW:(j + 1) * ROW], nat[0:ROW, j, k * P:(k + 1) * P],
                                           ident[0:ROW, 0:ROW])
                    ins.then_inc(s_bt, 1)

            def step(slot, out, moving, first, last):
                for k in range(KT):
                    mh, ml = moving(k)
                    w_h, w_l = wh[:, slot, k * P:(k + 1) * P], wl[:, slot, k * P:(k + 1) * P]
                    pe.matmul(out, w_h, mh, start=(first and k == 0), stop=False)
                    pe.matmul(out, w_h, ml, start=False, stop=False)
                    ins = pe.matmul(out, w_l, mh, start=False, stop=(last and k == KT - 1))
                return ins

            pe.wait_ge(s_const, 32)
            with pe.Fori(0, NB) as b:
                pe.wait_ge(s_nat, b * NR + (NAT0 + NR))
                back(b, 0)
            pe.wait_ge(s_xh, NB * KT)
            pe.wait_ge(s_xl, NB * KT)
            with pe.Fori(0, NC_IN // 2) as i:
                for u in range(2):
                    pe.wait_ge(s_wh, i * 2 + (u + 1))
                    pe.wait_ge(s_wl, i * 2 + (u + 1))
                    for b in range(NB):
                        pe.wait_ge(s_ev1, i * 10 + (5 * u + b + 1))
                        cols = slice(b * BLK, (b + 1) * BLK)
                        step(u, PS[:, b, 0:BLK], lambda k: (xh[:, k, cols], xl[:, k, cols]), True, True).then_inc(s_grp, 1)

            pe.wait_ge(s_const, CONST_ALL)
            pe.wait_ge(s_ev1, NB * NC_IN + NB)
            n = 0
            for c in range(2):
                for what in range(3):
                    pe.wait_ge(s_xc, 2 * c + (1 if what < 2 else 2))
                    src = mx[2] if what < 2 else mx[5]
                    for a in range(0, TOK, CHW):
                        w = min(CHW, TOK - a)
                        if n >= 4:
                            pe.wait_ge(s_gev, n - 3)
                        pe.matmul(PS[:, n % 4, 0:w], gsel[:, c, what, :], src[:, a:a + w], start=True, stop=True).then_inc(s_gps, 1)
                        n += 1

            def qsel(b, h):
                return qbd[:, (2 * b + h) * P:(2 * b + h + 1) * P]

            pe.wait_ge(s_gev, n)
            pe.wait_ge(s_kqs, 96)
            for c in range(2):
                pe.transpose(PS[0:SMP, 6 + c, 0:P], kqs[:, 4 + c, :], ident[:, :]).then_inc(s_vnt, 1)
            pe.wait_ge(s_qbd, 4)
            pe.sem_inc(s_ktr, 2)
            pe.sem_inc(s_kmm, 2)
            pe.sem_inc(s_sns, 1)
            for b in range(DECB):
                for h in range(2):
                    ins = pe.matmul(PS[:, 5, 0:DECT], qsel(b, h), kqs[:, 2 + h, b * DECT:(b + 1) * DECT],
                                    start=(b == 0 and h == 0), stop=(b == DECB - 1 and h == 1))
            ins.then_inc(s_zn, 1)
            with pe.Fori(0, NPG // 4) as c:
                for b in range(DECB + 1):
                    if b < DECB:
                        pe.wait_ge(s_kin[b % 2], c * (64 * DECB // 2) + 64 * (b // 2 + 1))
                        pe.wait_ge(s_kte, c * DECB + (b + 1))
                        for h in range(2):
                            for g in range(4):
                                ins = pe.transpose(PS[:, 2 * (b % 2) + h, g * P:(g + 1) * P],
                                                   kpg[:, b % 2, g, h * P:(h + 1) * P], ident[:, :])
                        ins.then_inc(s_ktr, 1)
                    if b >= 1:
                        d = b - 1
                        if d == 0:
                            pe.wait_ge(s_sns, c + 1)
                        pe.wait_ge(s_kte, c * DECB + (d + 3))
                        for h in range(2):
                            ins = pe.matmul(PS[:, 4, :], qsel(d, h), kts[:, d % 2, h, :],
                                            start=(d == 0 and h == 0), stop=(d == DECB - 1 and h == 1))
                        ins.then_inc(s_kmm, 1)
            pe.wait_ge(s_ws, 1)
            for g in range(4):
                for j in range(4):
                    t = 4 * g + j
                    ins = pe.transpose(PS[:, g, j * P:(j + 1) * P], sS[:, t * P:(t + 1) * P], ident[:, :])
                ins.then_inc(s_wtr, 1)
            pe.wait_ge(s_sns, 6)
            pe.transpose(PS[0:DECT, 5, 0:P], sS[:, PAST:PAST + DECT], ident[:, :]).then_inc(s_wtr, 1)
            pe.sem_inc(s_vuse, 2)
            pe.wait_ge(s_wte, 5)
            pe.wait_ge(s_vnat, 2)
            with pe.Fori(0, DECB) as b:
                for c in range(4):
                    pe.wait_ge(s_vin[c % 2], b * 128 + 64 * (c // 2 + 1))
                    for g in range(4):
                        for h in range(2):
                            ins = pe.matmul(PS[:, 6 + h, bass.ds(b * 8, 8)], vpg[:, c % 2, g, h * P:(h + 1) * P],
                                            wtS[:, 4 * c + g, bass.ds(b * 16 + 8 * h, 8)],
                                            start=(c == 0 and g == 0), stop=False)
                    ins.then_inc(s_vuse, 1)
                pe.wait_ge(s_vnin, b * 16 + 16)
                for h in range(2):
                    ins = pe.matmul(PS[:, 6 + h, bass.ds(b * 8, 8)], vnew[:, h * P:(h + 1) * P],
                                    wtN[:, bass.ds(b * 16 + 8 * h, 8)], start=False, stop=True)
                ins.then_inc(s_vnuse, 1)
            pe.wait_ge(s_yse, 4)

            with pe.Fori(0, 2) as hp:
                pe.wait_ge(s_qkv, hp * 48 + 48)
                for g in range(4):
                    for j in range(4):
                        t = 4 * g + j
                        ins = pe.transpose(PS[:, 4 + g, j * P:(j + 1) * P], vT[:, t * P:(t + 1) * P], ident[:, :])
                    ins.then_inc(s_vtr, 1)
                pe.wait_ge(s_vnp, hp * 4 + 4)
                cc = tg = 0

                def scores(n):
                    nonlocal cc
                    hl_, qt = divmod(n, QT)
                    rows = slice(HD * hl_, HD * hl_ + HD)
                    W = (qt + 1) * P
                    for a in range(0, W, CHW):
                        w = min(CHW, W - a)
                        if cc >= 4:
                            pe.wait_ge(s_sn, hp * 80 + (cc - 3))
                        pe.matmul(PS[:, cc % 4, 0:w], qT[rows, qt * P:(qt + 1) * P], kT[rows, a:a + w],
                                  start=True, stop=True).then_inc(s_z, 1)
                        cc += 1

                scores(0)
                for n in range(2 * QT):
                    if n + 1 < 2 * QT:
                        scores(n + 1)
                    hl_, qt = divmod(n, QT)
                    pe.wait_ge(s_w, hp * 32 + (n + 2))
                    if n >= 2:
                        pe.wait_ge(s_yc, hp * 32 + (n - 1))
                    groups = [list(range(a, min(a + 4, qt + 1))) for a in range(0, qt + 1, 4)]

                    def values(g, at):
                        pe.wait_ge(s_wt, hp * 80 + (at + 1))
                        for j, t in enumerate(groups[g]):
                            ins = pe.matmul(PS[HD * hl_:HD * hl_ + HD, 6 + n % 2, 0:P], vN[:, t, HD * hl_:HD * hl_ + HD],
                                            wtP[:, at % 2, j * P:(j + 1) * P], start=(t == 0), stop=(t == qt))
                        ins.then_inc(s_av, 1)

                    for g, ts in enumerate(groups):
                        if tg >= 2:
                            pe.wait_ge(s_wt, hp * 80 + (tg - 1))
                        for j, t in enumerate(ts):
                            ins = pe.transpose(PS[:, 4 + tg % 2, j * P:(j + 1) * P], sP[:, n % 2, t * P:(t + 1) * P], ident[:, :])
                        ins.then_inc(s_tr, 1)
                        if g:
                            values(g - 1, tg - 1)
                        tg += 1
                    values(len(groups) - 1, tg - 1)
                pe.wait_ge(s_yc, hp * 32 + 32)
                pe.sem_inc(s_pair, 1)

            with pe.Fori(0, NB) as b:
                pe.wait_ge(s_yh, b * 2 + 2)
                pe.wait_ge(s_yl, b * 2 + 2)
                for s in range(KT):
                    pe.wait_ge(s_wh, b * STEPS + (NC_IN + s + 1))
                    pe.wait_ge(s_wl, b * STEPS + (NC_IN + s + 1))
                    if s >= 4:
                        pe.wait_ge(s_oev, b * KT + (s - 3))
                    step(s % 2, PS[:, s % 4, 0:BLK], lambda k: (ah[:, k, :], al[:, k, :]), True, True).then_inc(s_step, 1)

                def forward(pair, done):
                    pe.wait_ge(s_nat, done)
                    for jj in range(2):
                        j = 2 * pair + jj
                        for k in range(KT):
                            ins = pe.transpose(PS[0:ROW, 4 + 2 * jj + k // 4, (k % 4) * P:(k % 4 + 1) * P],
                                               t3[:, k, j * ROW:(j + 1) * ROW], ident[:, :])
                    ins.then_inc(s_ft, 1)

                pe.wait_ge(s_oev, b * KT + KT)
                for pair in range(2):
                    forward(pair, b * 8 + (NAT0 + NR * NB + 2 * pair))
                pe.wait_ge(s_nat, b * 8 + (NAT0 + NR * NB + 4))
                back(b, NB * KT)
                pe.wait_ge(s_xh, b * KT + (NB * KT + KT))
                wait_apart(pe, s_xl, b * KT + (NB * KT + KT))
                with pe.Fori(0, FT // 4) as i:
                    for u in range(4):
                        pe.wait_ge(s_wh, b * STEPS + i * 4 + (NC_IN + KT + u + 1))
                        pe.wait_ge(s_wl, b * STEPS + i * 4 + (NC_IN + KT + u + 1))
                        pe.wait_ge(s_r, b * FT + i * 4 + (u + 1))
                        step(u % 2, PS[:, u, 0:BLK], lambda k: (ah[:, k, :], al[:, k, :]), True, True).then_inc(s_step, 1)
                pe.wait_ge(s_hh, b * FT + FT)
                wait_apart(pe, s_hl, b * FT + (FT + 1))
                with pe.Fori(0, KT // 2) as i:
                    for u in range(2):
                        pe.wait_ge(s_fev, b * KT + i * 2 + (u + 1))
                        for q in range(4):
                            s = 4 * u + q
                            pe.wait_ge(s_wh, b * STEPS + i * 8 + (NC_IN + KT + FT + s + 1))
                            pe.wait_ge(s_wl, b * STEPS + i * 8 + (NC_IN + KT + FT + s + 1))
                            step(s % 2, PS[:, u, 0:BLK], lambda k: (hh[:, 8 * q + k, :], hl[:, 8 * q + k, :]),
                                 q == 0, q == 3).then_inc(s_step, 1)
                pe.wait_ge(s_fev, b * KT + (KT + 2))
                for pair in range(2):
                    forward(pair, b * 8 + (NAT0 + NR * NB + 4 + 2 * pair))

        @block.scalar
        def _(act):
            own = Tally(act, s_act)

            def split_hi(slot, uses):
                act.wait_ge(s_raw[slot], uses * 16)
                act.activation(wh[:, slot, :], raw[:, slot, :], ACT.Copy).then_inc(s_wh, 1)

            def norm(src, dst, j, col):
                act.activation(dst, src, ACT.Identity, bias=nmr[0:ROW, col:col + 1], scale=rstd[0:ROW, col:col + 1]).then_inc(s_nat, 1)

            def back_hi(b, base, full, hi):
                for k in range(KT):
                    wait_apart(act, s_xf, b * KT + (base + k + 1))
                    act.activation(hi(k), full[:, k, :], ACT.Copy).then_inc(s_xh, 1)

            act.wait_ge(s_const, 32)
            split_hi(0, 1)
            split_hi(1, 1)
            with act.Fori(0, NB) as b:
                act.wait_ge(s_ve, b + 1)
                act.activation(std[0:ROW, :], var[0:ROW, :], ACT.Sqrt).then_inc(s_std, 1)
                act.wait_ge(s_nmr, b + 1)
                for j in range(NR):
                    norm(xin[0:ROW, j, :], nat1[0:ROW, j, :], j, j)
                back_hi(b, 0, t1, lambda k: xh[:, k, bass.ds(b * BLK, BLK)])
                act.wait_ge(s_xf, b * KT + KT)
                act.dma_start(x1_d[:, :, bass.ds(b * BLK, BLK)].rearrange("k p t -> p k t"), t1[:, :, :]).then_inc(s_t1st, 16)
            act.sem_inc(s_ev1, 5)
            act.sem_inc(s_stg[0], 16)
            act.sem_inc(s_stg[1], 16)
            act.wait_ge(s_t1st, 16 * NB + 16)
            with act.Fori(0, NC_IN // 2) as i:
                for u in range(2):
                    act.wait_ge(s_stg[u], i * 16 + 16)
                    for b in range(NB):
                        act.wait_ge(s_grp, i * 10 + (5 * u + b + 1))
                        act.activation(stage[:, u, b * BLK:(b + 1) * BLK], PS[:, b, 0:BLK], ACT.Copy).then_inc(s_ev1, 1)
                    split_hi(u, i + 2)

            def gates(n0, c, dst, func, bias, scale=1.0):
                n = n0
                for a in range(0, TOK, CHW):
                    w = min(CHW, TOK - a)
                    act.wait_ge(s_gps, n + 1)
                    act.activation(dst[:, a:a + w], PS[:, n % 4, 0:w], func, bias=bias, scale=scale).then_inc(s_gev, 1)
                    n += 1
                return n

            n = 0
            act.wait_ge(s_const, CONST_ALL)
            act.wait_ge(s_lam, 1)
            own.up(act.activation(lam[:, :, 1], lam[:, :, 0], ACT.Exp, scale=-1.0))
            act.wait_ge(s_lam, 2)
            own.up(act.activation(lam[:, :, 3], lam[:, :, 2], ACT.Ln))
            for c in range(2):
                act.wait_ge(s_lam, 3)
                act.wait_ge(s_mst[1], 16 * c)
                n = gates(n, c, mx[3], ACT.Sigmoid, pv[:, c, PBA:PBA + 1])
                n = gates(n, c, mx[4], ACT.Sigmoid, pv[:, c, PBX:PBX + 1])
                act.wait_ge(s_gev, n)
                own.up(act.activation(mx[3][:, 0:TOK], mx[3][:, 0:TOK], ACT.Tanh, scale=lam[:, c, 7:8]))
                own.sync()
                own.up(act.activation(mx[5][:, 0:TOK], mx[3][:, 0:TOK], ACT.Sqrt))
                act.wait_ge(s_mld[0], (c + 1) * 96)
                own.up(act.activation(mx[1][:, 0:TOK], mx[1][:, 0:TOK], ACT.Gelu_apprx_tanh))
                act.wait_ge(s_mst[0], 16 * (c + 1))
                n = gates(n, c, mx[6], ACT.Copy, 0.0, pv[:, c, PSC:PSC + 1])
                act.wait_ge(s_gev, n)
                act.sem_inc(s_mxa, 1)

            act.wait_ge(s_vnt, 2)
            for c in range(2):
                act.activation(vnat[:, c * P:(c + 1) * P], PS[0:SMP, 6 + c, 0:P], ACT.Copy).then_inc(s_vnat, 1)
            act.sem_inc(s_kte, 2)
            with act.Fori(0, NPG // 4) as c:
                for b in range(DECB):
                    act.wait_ge(s_ktr, c * DECB + (b + 3))
                    act.wait_ge(s_kmm, c * DECB + (b + 1))
                    act.activation(kts[:, b % 2, :, :], PS[:, 2 * (b % 2):2 * (b % 2) + 2, :], ACT.Copy).then_inc(s_kte, 1)
                wait_apart(act, s_kmm, c * DECB + (DECB + 2))
                own_c = bass.ds(c * CHW, CHW)
                act.activation(sS[:, own_c], PS[:, 4, :], ACT.Sigmoid, bias=bias_h[:, NH:NH + 1], scale=HD ** -0.5)
                act.activation(nS[:, own_c], PS[:, 4, :], ACT.Sigmoid, bias=nbias_h[:, NH:NH + 1], scale=-HD ** -0.5).then_inc(s_sns, 1)
            act.wait_ge(s_zn, 1)
            act.activation(sS[:, PAST:PAST + DECT], PS[:, 5, 0:DECT], ACT.Sigmoid, bias=bias_h[:, NH:NH + 1], scale=HD ** -0.5)
            act.activation(nS[:, PAST:PAST + DECT], PS[:, 5, 0:DECT], ACT.Sigmoid, bias=nbias_h[:, NH:NH + 1],
                           scale=-HD ** -0.5).then_inc(s_sns, 1)
            for g in range(4):
                act.wait_ge(s_wtr, g + 1)
                act.activation(wtS[:, 4 * g:4 * g + 4, :].rearrange("p a b -> p (a b)"), PS[:, g, :], ACT.Copy).then_inc(s_wte, 1)
            act.wait_ge(s_wtr, 5)
            act.activation(wtN[:, :], PS[0:DECT, 5, 0:P], ACT.Copy).then_inc(s_wte, 1)

            with act.Fori(0, 2) as hp:
                for g in range(4):
                    act.wait_ge(s_vtr, hp * 4 + (g + 1))
                    act.activation(vN[:, 4 * g:4 * g + 4, :].rearrange("p a b -> p (a b)"), PS[:, 4 + g, :], ACT.Copy).then_inc(s_vnp, 1)
                cc = tg = 0

                def sig(n):
                    nonlocal cc
                    hl_, qt = divmod(n, QT)
                    W = (qt + 1) * P
                    if n >= 2:
                        act.wait_ge(s_tr, hp * 80 + groups_until(n - 1))
                    for a in range(0, W, CHW):
                        w = min(CHW, W - a)
                        wait_apart(act, s_z, hp * 80 + (cc + 1))
                        act.activation(sP[:, n % 2, a:a + w], PS[:, cc % 4, 0:w], ACT.Sigmoid, scale=HD ** -0.5,
                                       bias=bias_h[:, bass.ds(hp * 2 + hl_, 1)])
                        act.activation(nP[:, n % 2, a:a + w], PS[:, cc % 4, 0:w], ACT.Sigmoid, scale=-HD ** -0.5,
                                       bias=nbias_h[:, bass.ds(hp * 2 + hl_, 1)]).then_inc(s_sn, 1)
                        cc += 1

                sig(0)
                for n in range(2 * QT):
                    if n + 1 < 2 * QT:
                        sig(n + 1)
                    qt = n % QT
                    for a in range(0, qt + 1, 4):
                        w = min(4, qt + 1 - a) * P
                        act.wait_ge(s_tr, hp * 80 + (tg + 1))
                        if tg >= 2:
                            act.wait_ge(s_av, hp * 80 + (tg - 1))
                        act.activation(wtP[:, tg % 2, 0:w], PS[:, 4 + tg % 2, 0:w], ACT.Copy).then_inc(s_wt, 1)
                        tg += 1

            act.wait_ge(s_pair, 3)
            act.wait_ge(s_ycs, 48)
            act.wait_ge(s_yst, 32)
            for m in s_mst:
                act.wait_ge(m, 32)
            act.sem_inc(s_r, 4)
            act.sem_inc(s_rowfree, 1)
            act.sem_inc(s_ft, 1)
            with act.Fori(0, NB) as b:
                def hi_after(s, off):
                    act.wait_ge(s_step, b * STEPS + s + (off + 1))
                    slot = off % 2
                    act.wait_ge(s_raw[slot], b * (STEPS * 8) + s * 8 + (NC_IN * 8 + 16 + (off - slot) * 8 + 16))
                    act.activation(wh[:, slot, :], raw[:, slot, :], ACT.Copy).then_inc(s_wh, 1)

                act.wait_ge(s_rowfree, b + 1)
                act.wait_ge(s_ft, b * 4 + 1)
                cols = bass.ds(b * BLK, BLK)
                act.dma_start(yin, y_d[:, :, cols].rearrange("k p t -> p k t")).then_inc(s_yin, 16)
                act.dma_start(t3[:, :, :], x1_d[:, :, cols].rearrange("k p t -> p k t")).then_inc(s_x1in, 16)
                act.wait_ge(s_yin, b * 16 + 16)
                for g in range(2):
                    act.activation(ah[:, 4 * g:4 * g + 4, :], yin[:, 4 * g:4 * g + 4, :], ACT.Copy).then_inc(s_yh, 1)
                for s in range(KT):
                    hi_after(0, s)

                def ln_scale(seq, dsts):
                    for pair in range(2):
                        act.wait_ge(s_ve, b * 4 + (NB + seq + pair + 1))
                        act.activation(std[0:ROW, 0:2], var[0:ROW, 0:2], ACT.Sqrt).then_inc(s_std, 1)
                        act.wait_ge(s_nmr, b * 4 + (NB + seq + pair + 1))
                        for jj in range(2):
                            j = 2 * pair + jj
                            norm(PS[0:ROW, 4 + 2 * jj:6 + 2 * jj, :].rearrange("p a b -> p (a b)"), nat3t[0:ROW, j, :], j, jj)

                act.wait_ge(s_yl, b * 2 + 2)
                ln_scale(0, None)
                back_hi(b, NB * KT, t3, lambda k: ah[:, k, :])
                with act.Fori(0, FT // 4) as i:
                    for u in range(4):
                        hi_after(i * 4, KT + u)
                        act.wait_ge(s_hf, b * FT + i * 4 + (u + 1))
                        act.activation(rbuf[:, u % 2, :], PS[:, u, 0:BLK], ACT.Relu).then_inc(s_r, 1)
                        wait_apart(act, s_r, b * FT + i * 4 + (u + 5))
                        act.activation(hh[:, bass.ds(i * 4 + u, 1), :].rearrange("p o t -> p (o t)"), rbuf[:, u % 2, :],
                                       ACT.Square).then_inc(s_hh, 1)
                with act.Fori(0, KT // 2) as i:
                    for s in range(8):
                        hi_after(i * 8, KT + FT + s)
                ln_scale(2, None)

        @block.vector
        def _(dve):
            own = Tally(dve, s_dve)

            def split_lo(slot, n_hi):
                dve.wait_ge(s_wh, n_hi)
                dve.tensor_tensor(wl[:, slot, :], raw[:, slot, :], wh[:, slot, :].bitcast(F32), ALU.subtract).then_inc(s_wl, 1)

            def moments(srcs, width, seq):
                for j, src in enumerate(srcs):
                    for h in range(2):
                        ins = dve.bn_stats(bn[0:ROW, j, h, :], src[:, h * 512:(h + 1) * 512])
                own.up(ins)
                own.sync()
                for j in range(width):
                    ins = dve.bn_aggr(mv[0:ROW, j, :], bn[0:ROW, j, :, :])
                own.up(ins)
                own.sync()
                dve.tensor_scalar(var[0:ROW, 0:width], mv[0:ROW, 0:width, 1], EPS, None, ALU.add).then_inc(s_ve, 1)
                dve.wait_ge(s_std, seq + 1)
                own.up(dve.reciprocal(rstd[0:ROW, 0:width], std[0:ROW, 0:width]))
                own.sync()
                dve.scalar_tensor_tensor(out=nmr[0:ROW, 0:width], in0=mv[0:ROW, 0:width, 0], scalar=-1.0,
                                         in1=rstd[0:ROW, 0:width], op0=ALU.mult, op1=ALU.mult).then_inc(s_nmr, 1)

            def back_lo(b, base, full, hi, lo, which):
                for n in range(KT + 1):
                    if n < KT:
                        dve.wait_ge(s_bt, b * KT + (base + n + 1))
                        dve.tensor_scalar(full(n), PS[:, 4 + n % 4, 0:BLK], ln_gb[:, which, n:n + 1], ln_gb[:, which + 1, n:n + 1],
                                          ALU.mult, ALU.add).then_inc(s_xf, 1)
                    if n:
                        k = n - 1
                        dve.wait_ge(s_xf, b * KT + (base + k + 1))
                        dve.wait_ge(s_xh, b * KT + (base + k + 1))
                        dve.tensor_tensor(lo(k), full(k), hi(k).bitcast(F32), ALU.subtract).then_inc(s_xl, 1)

            dve.memset(gsel[:, :, :, :], 0.0).then_inc(s_mzero, 1)
            dve.sem_inc(s_t1st, 16)
            dve.wait_ge(s_const, 32)
            split_lo(0, 1)
            split_lo(1, 2)
            with own.loop(NB, 3) as b:
                dve.wait_ge(s_xin, b * 16 + 16)
                moments([xin[0:ROW, j, :] for j in range(NR)], NR, b)
                dve.wait_ge(s_t1st, b * 16 + 16)
                cols = bass.ds(b * BLK, BLK)
                back_lo(b, 0, lambda k: t1[:, k, :], lambda k: xh[:, k, cols], lambda k: xl[:, k, cols], 0)
            with dve.Fori(0, NC_IN // 2) as i:
                for u in range(2):
                    dve.wait_ge(s_grp, i * 10 + (5 * u + 5))
                    split_lo(u, i * 2 + (u + 3))

            def op(ins):
                own.up(ins)
                own.sync()

            def conv(dst, src, c, col, taps, halo, bias):
                ext = ext_of(src, halo)
                dst_s = dst[:, SEQ:TOK].rearrange("p (b t) -> p b t", b=DECB)
                for j in range(taps):
                    for d_, s_ in ((dst[:, 0:SEQ], src[:, j:j + SEQ]), (dst_s, ext[:, :, j:j + DECT])):
                        if j == 0:
                            own.up(dve.tensor_scalar(d_, s_, pv[:, c, col:col + 1], bias, ALU.mult, ALU.add))
                        else:
                            own.up(dve.scalar_tensor_tensor(out=d_, in0=s_, scalar=pv[:, c, col + j:col + j + 1], in1=d_,
                                                            op0=ALU.mult, op1=ALU.add))
                    own.sync()

            dve.wait_ge(s_const, CONST_ALL)
            op(dve.tensor_scalar(nbias_h[:, :], bias_h[:, :], -1.0, None, ALU.mult))
            L = lambda n: lam[:, :, n]
            lamv = pv[:, :, PLAM]
            op(dve.tensor_scalar(L(4), lamv, -1.0, None, ALU.mult))
            dve.tensor_tensor(L(0), lamv, L(4), ALU.max).then_inc(s_lam, 1)
            dve.wait_ge(s_act, 1)
            dve.tensor_scalar(L(2), L(1), 1.0, None, ALU.add).then_inc(s_lam, 1)
            dve.wait_ge(s_lam, 2)
            op(dve.tensor_scalar(L(5), L(2), -1.0, None, ALU.add))
            op(dve.tensor_scalar(L(6), L(5), 0.0, None, ALU.is_equal))
            op(dve.tensor_tensor(L(5), L(5), L(6), ALU.add))
            op(dve.reciprocal(L(5), L(5)))
            dve.wait_ge(s_act, 2)
            op(dve.tensor_tensor(L(5), L(5), L(3), ALU.mult))
            op(dve.tensor_tensor(L(5), L(5), L(6), ALU.add))
            op(dve.tensor_tensor(L(5), L(5), L(1), ALU.mult))
            op(dve.scalar_tensor_tensor(out=L(5), in0=L(4), scalar=0.0, in1=L(5), op0=ALU.max, op1=ALU.add))
            dve.tensor_scalar(L(7), L(5), RC / 2, None, ALU.mult).then_inc(s_lam, 1)

            for c in range(2):
                dve.wait_ge(s_mld[0], (c + 1) * 96)
                op(dve.memset(mx[0][:, 0:BUFA], 0.0))
                conv(mx[2], mx[0], c, PCW, 4, BUFA, pv[:, c, PCB:PCB + 1])
                dve.sem_inc(s_xc, 1)
                nb = 1 + DECB
                own.up(dve.tensor_copy(so[:, c, SO_A:SO_A + BUFA], mx[0][:, SEQ:SEQ + BUFA]))
                op(dve.tensor_copy(so[:, c, SO_A + BUFA:SO_A + BUFA * nb].rearrange("p (b t) -> p b t", b=DECB),
                                   ext_of(mx[0], BUFA)[:, :, DECT:]))
                dve.wait_ge(s_act, 4 + 3 * c)
                T = lambda n: mx[n][:, 0:TOK]
                op(dve.tensor_scalar(T(7), T(3), 1.0, None, ALU.add))
                op(dve.reciprocal(T(7), T(7)))
                own.up(dve.tensor_scalar(T(3), T(7), 2.0, -1.0, ALU.mult, ALU.add))
                own.up(dve.scalar_tensor_tensor(out=T(5), in0=T(5), scalar=2.0, in1=T(7), op0=ALU.mult, op1=ALU.mult))
                op(dve.tensor_tensor(T(4), T(4), T(2), ALU.mult))
                op(dve.tensor_tensor(T(5), T(5), T(4), ALU.mult))
                dve.wait_ge(s_mst[2], 16 * c)
                own.up(dve.tensor_tensor_scan(mx[6][:, 0:SEQ], mx[3][:, 0:SEQ], mx[5][:, 0:SEQ], 0.0, ALU.mult, ALU.add))
                for b in range(DECB):
                    ts = slice(SEQ + b * DECT, SEQ + (b + 1) * DECT)
                    own.up(dve.tensor_tensor_scan(mx[6][:, ts], mx[3][:, ts], mx[5][:, ts], hs[:, c, b:b + 1], ALU.mult, ALU.add))
                own.sync()
                own.up(dve.tensor_copy(so[:, c, SO_H:SO_H + 1], mx[6][:, SEQ - 1:SEQ]))
                op(dve.tensor_copy(so[:, c, SO_H + 1:SO_H + nb], mx[6][:, SEQ:TOK].rearrange("p (b t) -> p b t", b=DECB)[:, :, DECT - 1]))
                dve.wait_ge(s_act, 5 + 3 * c)
                dve.tensor_tensor(T(6), T(6), T(1), ALU.mult).then_inc(s_mxv, 1)
                dve.wait_ge(s_mxv, 2 * c + 1)
                dve.sem_inc(s_mfree, 1)
                dve.wait_ge(s_mld[1], (c + 1) * 64)
                u_s = ext_of(mx[3], BUFB)
                own.up(dve.memset(mx[3][:, 0:BUFB], 0.0))
                own.up(dve.tensor_tensor(mx[3][:, BUFB:BUFB + SEQ], mx[0][:, 0:SEQ], mx[1][:, 0:SEQ], ALU.mult))
                s3 = lambda t: t[:, SEQ:TOK].rearrange("p (b t) -> p b t", b=DECB)
                op(dve.tensor_tensor(u_s[:, :, BUFB:], s3(mx[0]), s3(mx[1]), ALU.mult))
                own.up(dve.tensor_copy(so[:, c, SO_B:SO_B + BUFB], mx[3][:, SEQ:SEQ + BUFB]))
                own.up(dve.tensor_copy(so[:, c, SO_B + BUFB:SO_B + BUFB * nb].rearrange("p (b t) -> p b t", b=DECB), u_s[:, :, DECT:]))
                conv(mx[4], mx[3], c, PBW, 3, BUFB, 0.0)
                dve.tensor_tensor(T(4), T(4), T(2), ALU.mult).then_inc(s_mxv, 1)
                dve.wait_ge(s_mxv, 2 * c + 2)
                dve.sem_inc(s_mfree, 1)
                dve.wait_ge(s_mld[2], (c + 1) * 48)
                own.up(dve.memset(mx[0][:, 0:BUFP], 0.0))
                ext = ext_of(mx[0], BUFP)
                own.sync()
                own.up(dve.tensor_copy(so[:, c, SO_P:SO_P + BUFP], mx[0][:, SEQ:SEQ + BUFP]))
                own.up(dve.tensor_copy(so[:, c, SO_P + BUFP:SO_P + BUFP * nb].rearrange("p (b t) -> p b t", b=DECB), ext[:, :, DECT:]))

                def wider(dst, src, half, rows):
                    a = 2 * half - 1
                    own.up(dve.tensor_tensor(dst[rows, a:BUFP + SEQ], src[rows, a:BUFP + SEQ],
                                             src[rows, a - half:BUFP + SEQ - half], ALU.add))
                    d_, s_ = ext_of(dst, BUFP)[rows], ext_of(src, BUFP)[rows]
                    op(dve.tensor_tensor(d_[:, :, a:], s_[:, :, a:], s_[:, :, a - half:BUFP + DECT - half], ALU.add))

                every, low, high = slice(0, P), slice(0, HD), slice(HD, P)
                wider(mx[1], mx[0], 1, every)
                if c == 0:
                    wider(mx[2], mx[1], 2, high)
                    lo_t, hi_t = mx[1], mx[2]
                else:
                    wider(mx[2], mx[1], 2, every)
                    wider(mx[1], mx[2], 4, every)
                    wider(mx[2], mx[1], 8, high)
                    lo_t, hi_t = mx[1], mx[2]
                for rows, t in ((low, lo_t), (high, hi_t)):
                    own.up(dve.scalar_tensor_tensor(out=mx[5][rows, 0:SEQ], in0=t[rows, BUFP:BUFP + SEQ], scalar=pv[rows, c, PINV:PINV + 1],
                                                    in1=mx[0][rows, BUFP:BUFP + SEQ], op0=ALU.mult, op1=ALU.subtract))
                    own.up(dve.scalar_tensor_tensor(out=s3(mx[5])[rows], in0=ext_of(t, BUFP)[rows][:, :, BUFP:], scalar=pv[rows, c, PINV:PINV + 1],
                                                    in1=ext[rows][:, :, BUFP:], op0=ALU.mult, op1=ALU.subtract))
                own.sync()
                cnt = lambda rows: mask[rows, DECT + 16 * c:DECT + 16 * c + 16]
                for rows, t in ((low, lo_t), (high, hi_t)):
                    own.up(dve.tensor_tensor(mx[5][rows, 0:16], t[rows, BUFP:BUFP + 16], cnt(rows), ALU.mult))
                own.sync()
                op(dve.tensor_tensor(mx[5][:, 0:16], mx[5][:, 0:16], mx[0][:, BUFP:BUFP + 16], ALU.subtract))
                dve.sem_inc(s_xc, 1)
                dve.sem_inc(s_mfree, 1)

            op(dve.memset(qbd[:, :], 0.0))
            dve.wait_ge(s_kqs, 96)
            for h in range(NH):
                rows = slice(HD * (h % 2), HD * (h % 2) + HD)
                a = (h // 2) * P + h * DECT
                dst = qbd[rows, a:a + DECB * 272].rearrange("p (b s) -> p b s", s=272)[:, :, 0:DECT]
                dve.tensor_copy(dst, kqs[rows, h // 2, :].rearrange("p (b t) -> p b t", b=DECB)).then_inc(s_qbd, 1)
            dve.wait_ge(s_sns, 6)
            new = slice(PAST, PAST + DECT)
            own.up(dve.tensor_tensor(sS[:, new], sS[:, new], mask[:, 0:DECT], ALU.mult))
            op(dve.scalar_tensor_tensor(out=nS[:, new], in0=nS[:, new], scalar=-1.0, in1=mask[:, 0:DECT], op0=ALU.add, op1=ALU.mult))
            op(dve.tensor_scalar(nS[:, new], nS[:, new], 1.0, None, ALU.add))
            W = PAST + DECT
            own.up(dve.memset(pS[:, W:W + 1], 1.0))
            op(dve.tensor_tensor_scan(rev(pS[:, 0:W]), rev(nS[:, :]), rev(nS[:, :]), 1.0, ALU.mult, ALU.bypass))
            dve.tensor_tensor(sS[:, :], sS[:, :], pS[:, 1:W + 1], ALU.mult).then_inc(s_ws, 1)
            dve.wait_ge(s_vnuse, DECB + 1)
            for h in range(NH):
                rows = slice(HD * (h % 2), HD * (h % 2) + HD)
                src = PS[rows, 6 + h // 2, 0:DECB * 8].rearrange("p (b s) -> p b s", s=8)[:, :, DECT * (h % 2):DECT * (h % 2) + DECT]
                dve.tensor_copy(ycs[rows, h // 2, :].rearrange("p (b t) -> p b t", b=DECB), src).then_inc(s_yse, 1)

            dve.wait_ge(s_yst, 32)
            for m in s_mst:
                dve.wait_ge(m, 32)
            op(dve.memset(pP[:, SEQ:SEQ + 1], 1.0))
            dve.sem_inc(s_ycs, 16)
            dve.sem_inc(s_w, 1)
            with dve.Fori(0, 2) as hp:
                def result(n):
                    hl_, qt = divmod(n, QT)
                    rows = slice(HD * hl_, HD * hl_ + HD)
                    if n == 0:
                        dve.wait_ge(s_ycs, hp * 16 + 16)
                    dve.wait_ge(s_av, hp * 80 + groups_until(n + 1))
                    dve.tensor_copy(ycT[rows, qt * P:(qt + 1) * P], PS[rows, 6 + n % 2, 0:P]).then_inc(s_yc, 1)

                for n in range(2 * QT):
                    W = (n % QT + 1) * P
                    dve.wait_ge(s_msk, hp * 32 + (n + 1))
                    dve.wait_ge(s_w, hp * 32 + (n + 1))
                    dve.tensor_tensor_scan(rev(pP[:, SEQ - W:SEQ]), rev(nP[:, n % 2, 0:W]), rev(nP[:, n % 2, 0:W]), 1.0,
                                           ALU.mult, ALU.bypass).then_inc(s_scan, 1)
                    dve.wait_ge(s_scan, hp * 32 + (n + 1))
                    dve.tensor_tensor(sP[:, n % 2, 0:W], sP[:, n % 2, 0:W], pP[:, SEQ - W + 1:SEQ + 1], ALU.mult).then_inc(s_w, 1)
                    if n >= 1:
                        result(n - 1)
                result(2 * QT - 1)

            dve.wait_ge(s_pair, 3)
            dve.wait_ge(s_ycs, 48)
            dve.sem_inc(s_hf, 2)
            dve.sem_inc(s_fev, 2)
            dve.sem_inc(s_hl, 1)
            with own.loop(NB, 12) as b:
                def lo_after(s, off):
                    dve.wait_ge(s_step, b * STEPS + s + (off + 1))
                    split_lo(off % 2, b * STEPS + s + (NC_IN + off + 3))

                dve.wait_ge(s_yin, b * 16 + 16)
                for g in range(2):
                    dve.wait_ge(s_yh, b * 2 + (g + 1))
                    dve.tensor_tensor(al[:, 4 * g:4 * g + 4, :], yin[:, 4 * g:4 * g + 4, :], ah[:, 4 * g:4 * g + 4, :].bitcast(F32),
                                      ALU.subtract).then_inc(s_yl, 1)
                dve.wait_ge(s_x1in, b * 16 + 16)
                for s in range(KT):
                    lo_after(0, s)
                    dve.scalar_tensor_tensor(out=t3[:, s, :], in0=t3[:, s, :], scalar=ALPHA, in1=PS[:, s % 4, 0:BLK],
                                             op0=ALU.mult, op1=ALU.add).then_inc(s_oev, 1)

                def ln_moments(seq):
                    for pair in range(2):
                        dve.wait_ge(s_ft, b * 4 + (seq + pair + 2))
                        moments([PS[0:ROW, 4 + 2 * jj:6 + 2 * jj, :].rearrange("p a b -> p (a b)") for jj in range(2)], 2,
                                b * 4 + (NB + seq + pair))

                ln_moments(0)
                back_lo(b, NB * KT, lambda k: t3[:, k, :], lambda k: ah[:, k, :], lambda k: al[:, k, :], 2)
                with dve.Fori(0, FT // 4) as i:
                    for u in range(4):
                        lo_after(i * 4, KT + u)
                        dve.wait_ge(s_r, b * FT + i * 4 + (u + 5))
                        dve.wait_ge(s_hl, b * FT + i * 4 + (u + 1))
                        dve.tensor_tensor(hf[:, :], rbuf[:, u % 2, :], rbuf[:, u % 2, :], ALU.mult).then_inc(s_hf, 1)
                        dve.wait_ge(s_hf, b * FT + i * 4 + (u + 3))
                        dve.wait_ge(s_hh, b * FT + i * 4 + (u + 1))
                        f = bass.ds(i * 4 + u, 1)
                        dve.tensor_tensor(hl[:, f, :].rearrange("p o t -> p (o t)"), hf[:, :],
                                          hh[:, f, :].rearrange("p o t -> p (o t)").bitcast(F32), ALU.subtract).then_inc(s_hl, 1)
                with dve.Fori(0, KT // 2) as i:
                    for u in range(2):
                        for q in range(4):
                            lo_after(i * 8, KT + FT + 4 * u + q)
                        tk = t3[:, bass.ds(i * 2 + u, 1), :].rearrange("p o t -> p (o t)")
                        dve.scalar_tensor_tensor(out=tk, in0=tk, scalar=ALPHA, in1=PS[:, u, 0:BLK],
                                                 op0=ALU.mult, op1=ALU.add).then_inc(s_fev, 1)
                ln_moments(2)

        @block.gpsimd
        def _(pool):
            own = Tally(pool, s_pool)
            with pool.Fori(0, 2) as hp:
                for n in range(2 * QT):
                    W = (n % QT + 1) * P
                    wait_apart(pool, s_sn, hp * 80 + groups_until(n + 1))
                    for t, fill in ((sP, 0.0), (nP, 1.0)):
                        diag = t[:, n % 2, W - P:W]
                        ins = pool.affine_select(out=diag, in_=diag, compare_op=ALU.is_gt, fill=fill, base=0,
                                                 pattern=[[-1, P]], channel_multiplier=1)
                    ins.then_inc(s_msk, 1)
            pool.wait_ge(s_const, CONST_ALL + 16)
            with own.loop(NB, NR) as b:
                for j in range(NR):
                    pool.wait_ge(s_nat, b * 8 + (NAT0 + NR * NB + 4 + j + 1))
                    row = nat3t[0:ROW, j, :]
                    own.up(pool.tensor_tensor(row, row, gb2[0:ROW, 0, :], ALU.mult))
                    own.sync()
                    pool.tensor_tensor(row, row, gb2[0:ROW, 1, :], ALU.add).then_inc(s_row, 1)
                    pool.wait_ge(s_row, b * NR + (j + 1))
                    pool.dma_start(y_out[bass.ds(b * BLK + j * ROW, ROW)], row).then_inc(s_out, 16)
                pool.wait_ge(s_out, b * (16 * NR) + 16 * NR)
                pool.sem_inc(s_rowfree, 1)


def _tiles(w, rows, cols):
    a = w.reshape(rows, KT, P, cols, P)
    return a.transpose(3, 0, 2, 1, 4).reshape(cols * rows, P, KT * P)


def _channels(a):
    a = np.moveaxis(a, -1, 0)
    return np.ascontiguousarray(a.reshape((2, P) + a.shape[1:]))


def kernel(**inputs):
    import concourse.bacc as bacc
    from concourse.bass_utils import run_bass_kernel_spmd

    f = {k: np.asarray(v) for k, v in inputs.items()}
    w_in = _tiles(f["w_in"][0], 1, NC_IN)[[2 * g + c for g, c in ORDER]]
    w_all = np.concatenate([w_in, _tiles(f["w_out"][0], 1, KT), _tiles(f["w_ff1"][0], 1, FT), _tiles(f["w_ff2"][0], 4, KT)])
    per_channel = [f["conv_a_w"][0].T, f["conv_a_b"][0][:, None], f["lru_ba"][0][:, None], f["lru_bx"][0][:, None],
                   f["lru_lambda"][0][:, None], f["conv_b_w"][0].T, f["pool_scale"][0][:, None],
                   np.repeat(np.float32(1.0) / np.array(WINDOWS, np.float32), HD)[:, None]]
    pvec = np.concatenate(per_channel, 1).reshape(2, P, NPV).transpose(1, 0, 2)
    lnp = np.stack([f[k].reshape(KT, P) for k in ("ln_in_g", "ln_in_b", "ln1_g", "ln1_b")]).transpose(2, 0, 1)
    rows2 = np.broadcast_to(np.stack([f["ln2_g"][0], f["ln2_b"][0]]), (P, 2, D))
    masks = np.zeros((P, DECT + 32), np.float32)
    masks[:, :DECT] = np.arange(DECT)[None] < (np.arange(P) % DECT)[:, None]
    for c in range(2):
        w = np.repeat(WINDOWS[2 * c:2 * c + 2], HD)[:, None]
        masks[:, DECT + 16 * c:DECT + 16 * c + 16] = 1.0 / np.minimum(w, np.arange(16)[None] + 1)
    n_pool = f["cache_k"].shape[1]
    arrays = {
        "x_all": np.concatenate([f["x_prompt"].reshape(SEQ, D), f["x_sample"].reshape(SMP, D)]),
        "w_all": w_all, "pvec": pvec, "lnp": lnp, "rows2": rows2,
        "gates_a": f["lru_wa"][0], "gates_x": f["lru_wx"][0], "poolw": f["pool_w"][0],
        "sbh": np.broadcast_to(f["sb_bias"][0], (P, NH)),
        "sbr": np.tile(np.repeat(f["sb_bias"][0], DECT), DECB)[:, None],
        "masks": masks, "ident_d": np.eye(P, dtype=np.float32),
        "ck": f["cache_k"].reshape(n_pool, PAGE, 2 * P), "cv": f["cache_v"].reshape(n_pool, PAGE, 2 * P),
        "ptab": f["page_table"].reshape(1, DECB * NPG),
        "st_h": _channels(f["state_rglru_h"][0]), "st_a": _channels(f["state_conv_a"][0]),
        "st_b": _channels(f["state_conv_b"][0]), "st_p": _channels(f["state_pool"][0]),
    }
    arrays = {k: np.ascontiguousarray(v) for k, v in arrays.items()}
    outs = {"y_out": (TOK, D), "kv_out": (4, P, TOK), "so_out": (P, 2, SO_N)}
    nc = bacc.Bacc("TRN2", target_bir_lowering=False, num_devices=1)
    args = [nc.dram_tensor(k, a.shape, mybir.dt.from_np(a.dtype), kind="ExternalInput").ap() for k, a in arrays.items()]
    args += [nc.dram_tensor(k, s, F32, kind="ExternalOutput").ap() for k, s in outs.items()]
    build(nc, *args)
    got = run_bass_kernel_spmd(nc, [arrays], core_ids=[0]).results[0]
    y, kv, so = got["y_out"], got["kv_out"], got["so_out"]
    kv = kv.reshape(2, 2 * P, TOK).transpose(0, 2, 1)

    def prompt(a):
        return np.ascontiguousarray(a[:SEQ].reshape(1, 1, SEQ, NH, HD))

    def sample(a):
        return np.ascontiguousarray(a[SEQ:].reshape(1, DECB, DECT, NH, HD))

    so = so.transpose(1, 0, 2).reshape(2 * P, SO_N).T

    def state(at, rows):
        return (np.ascontiguousarray(so[at:at + rows].reshape(1, 1, rows, 2 * P)),
                np.ascontiguousarray(so[at + rows:at + rows * (1 + DECB)].reshape(1, DECB, rows, 2 * P)))

    h_p, h_s = state(SO_H, 1)
    a_p, a_s = state(SO_A, BUFA)
    b_p, b_s = state(SO_B, BUFB)
    p_p, p_s = state(SO_P, BUFP)
    return (y[:SEQ].reshape(1, SEQ, D), y[SEQ:].reshape(DECB, DECT, D), prompt(kv[0]), prompt(kv[1]), sample(kv[0]), sample(kv[1]),
            h_p.reshape(1, 1, 2 * P), h_s.reshape(1, DECB, 2 * P), a_p, a_s, b_p, b_s, p_p, p_s)
```

```python
from contextlib import ExitStack, contextmanager

import numpy as np
import concourse.bass as bass
from concourse import mybir

F32 = mybir.dt.float32
F32R = mybir.dt.float32r
I32 = mybir.dt.int32
ACT = mybir.ActivationFunctionType
ALU = mybir.AluOpType

P = 128
D = 1024
KT = D // P
SEQ = 2048
DECB, DECT = 8, 4
SMP = DECB * DECT
TOK = SEQ + SMP
BLK = 416
NB = TOK // BLK
ROW = 104
NR = BLK // ROW
NC_IN = 18
FT = 32
HF = FT // 2
NN = 8
D1 = 4
PRO = KT + NN
SA_, SB_ = 0, HF - NN
SC_ = SB_ + HF
SD_ = SC_ + HF
SE_ = SD_ + D1
SD2 = SE_ + KT
SN_ = SD2 + HF - D1
STEPS = SN_ + NN
LAST = STEPS - KT - NN
TOTAL = PRO + (NB - 1) * STEPS + LAST
HD = 64
NH = 4
PAGE = 128
NPG = 16
PAST = NPG * PAGE
QT = SEQ // P
CHW = 512
ALPHA = 2.0 ** 0.25
EPS = 1e-5
RC = 8.0
BUFA, BUFB, BUFP = 3, 2, 15
WINDOWS = (2, 4, 8, 16)
XA, GA, XB, GB, GC, Q, K, V, XP = range(9)
ORDER = [(g, c) for g in (XA, GA, XB, GC, GB, XP, K, V, Q) for c in (0, 1)]
AT = {gc: n for n, gc in enumerate(ORDER)}
K0 = AT[K, 0]
PCW, PCB, PBA, PBX, PLAM, PBW, PSC, PINV, NPV = 0, 4, 5, 6, 7, 8, 11, 12, 13
SO_H, SO_A, SO_B, SO_P = 0, 1 + DECB, 1 + DECB + BUFA * (1 + DECB), 1 + DECB + (BUFA + BUFB) * (1 + DECB)
SO_N = (1 + DECB) * (1 + BUFA + BUFB + BUFP)


NAT0 = NR
NATB = NAT0 + NR * NB
CONST_ALL = 16 * 18


def ext_of(tile, halo):
    a = SEQ + halo
    return tile[:, a:a + DECB * (halo + DECT)].rearrange("p (b t) -> p b t", b=DECB)


def new_of(tile):
    return tile[:, SEQ:TOK].rearrange("p (b t) -> p b t", b=DECB)


def tile_of(t, k):
    return t[:, bass.ds(k, 1), :].rearrange("p o t -> p (o t)")


def rev(ap):
    return ap[:, ::-1]


def groups_until(n):
    return sum(-(-(m % QT + 1) // 4) for m in range(n))


def build(nc, x_all, w_all, pvec, lnp, rows2, gates_a, gates_x, poolw, sbh, sbr, masks, ident_d, ck, cv, ptab,
          st_h, st_a, st_b, st_p, y_out, kv_out, so_out):
    ctx = ExitStack()
    with ctx:
        def sb(name, shape, dt=F32, stack=ctx):
            return stack.enter_context(nc.sbuf_tensor(name, shape, dt))

        def sem(name):
            return ctx.enter_context(nc.semaphore(name))

        proj_d = nc.dram_tensor("proj_scratch", (NC_IN, P, TOK), F32, kind="Internal").ap()
        x1_d = nc.dram_tensor("x1_scratch", (KT, P, TOK), F32, kind="Internal").ap()
        y_d = nc.dram_tensor("mixed_scratch", (KT, P, TOK), F32, kind="Internal").ap()
        vn_d = nc.dram_tensor("vnew_scratch", (SMP, 2 * P), F32, kind="Internal").ap()

        PS = ctx.enter_context(nc.psum_tensor("PS", [P, 8, 512], F32))

        ident = sb("ident", [P, P])
        raw = sb("w_raw", [P, 2, KT * P])
        wh = sb("w_hi", [P, 2, KT * P], F32R)
        wl = sb("w_lo", [P, 2, KT * P], F32R)
        pv = sb("pv", [P, 2, NPV])
        ln_gb = sb("ln_gb", [P, 4, KT])
        mask = sb("mask", [P, DECT + 32])
        hs = sb("hs", [P, 2, DECB])
        bias_h = sb("bias_h", [P, NH + 1])
        nbias_h = sb("nbias_h", [P, NH + 1])
        bn = sb("bn", [P, 4, 2, 6])
        mv = sb("mv", [P, 4, 2])
        var = sb("var", [P, 4])
        std = sb("std", [P, 4])
        rstd = sb("rstd", [P, 4])
        nmr = sb("nmr", [P, 4])
        gsel = sb("gsel", [P, 2, 3, P])
        lam = sb("lam", [P, 2, 8])
        so = sb("so", [P, 2, SO_N])

        with ExitStack() as e1:
            xh = sb("x_hi", [P, KT, TOK], F32R, e1)
            xl = sb("x_lo", [P, KT, TOK], F32R, e1)
            with ExitStack() as e:
                xin = sb("xin", [P, NR, D], F32, e)
                nat1 = sb("nat1", [P, NR, D], F32, e)
                t1 = sb("t1", [P, KT, BLK], F32, e)
            with ExitStack() as e:
                stage = sb("stage", [P, 2, TOK], F32, e)
        with ExitStack() as e:
            MW = SEQ + BUFP + DECB * (BUFP + DECT)
            mx = [sb(f"mx{n}", [P, MW], F32, e) for n in range(8)]
            qbd = sb("qbd", [P, 2368], F32, e)
            kqs = sb("kqs", [P, 6, SMP], F32, e)
            kpg = sb("kpg", [P, 2, 4, 2 * P], F32, e)
            kts = sb("kts", [P, 2, 2, CHW], F32, e)
            vpg = sb("vpg", [P, 2, 4, 2 * P], F32, e)
            vnew = sb("vnew", [DECT, 2 * P], F32, e)
            vnat = sb("vnat", [SMP, 2 * P], F32, e)
            sS = sb("sS", [P, PAST + DECT], F32, e)
            nS = sb("nS", [P, PAST + DECT], F32, e)
            pS = sb("pS", [P, PAST + DECT + 1], F32, e)
            wtS = sb("wtS", [P, NPG, P], F32, e)
            wtN = sb("wtN", [DECT, P], F32, e)
            ycs = sb("ycs", [P, 2, SMP], F32, e)
            ptb = sb("ptb", [1, DECB * NPG], I32, e)
        with ExitStack() as e:
            qT = sb("qT", [P, SEQ], F32, e)
            kT = sb("kT", [P, SEQ], F32, e)
            vT = sb("vT", [P, SEQ], F32, e)
            vN = sb("vN", [P, QT, P], F32, e)
            sP = sb("sP", [P, 2, SEQ], F32, e)
            nP = sb("nP", [P, 2, SEQ], F32, e)
            pP = sb("pP", [P, SEQ + 1], F32, e)
            wtP = sb("wtP", [P, 2, CHW], F32, e)
            ycT = sb("ycT", [P, SEQ], F32, e)
        with ExitStack() as e:
            hh = sb("h_hi", [P, HF, BLK], F32R, e)
            hl = sb("h_lo", [P, HF, BLK], F32R, e)
            ah = sb("a_hi", [P, KT, BLK], F32R, e)
            al = sb("a_lo", [P, KT, BLK], F32R, e)
            xr = sb("x_residual", [P, KT, BLK], F32, e)
            acc = sb("mlp_sum", [P, KT, BLK], F32, e)
            nat3 = sb("nat3", [P, NR, D], F32, e)
            yin = sb("y_block", [P, KT, BLK], F32, e)
            rbuf = sb("rbuf", [P, 2, BLK], F32, e)
            hf = sb("hf", [P, BLK], F32, e)
            gb2 = sb("gb2", [P, 2, D], F32, e)

        s_const = sem("const_in")
        s_raw = [sem("raw_in0"), sem("raw_in1")]
        s_wh, s_wl = sem("w_hi_made"), sem("w_lo_made")
        s_xin, s_t1st = sem("xin_in"), sem("x1_stored")
        s_ve, s_std, s_nmr = sem("var_made"), sem("std_made"), sem("nmr_made")
        s_nat = sem("tile_normalised")
        s_bt = sem("back_transposed")
        s_xh, s_xf, s_xl = sem("x_hi_made"), sem("x_full_made"), sem("x_lo_made")
        s_grp, s_ev1 = sem("proj_group_done"), sem("proj_evacuated")
        s_stg = [sem("stage_stored0"), sem("stage_stored1")]
        s_act, s_dve, s_pool = sem("act_own"), sem("dve_own"), sem("pool_own")
        s_mld = [sem("mix_loaded_a"), sem("mix_loaded_b"), sem("mix_loaded_d")]
        s_mzero = sem("mix_halo_zeroed")
        s_xc, s_gps, s_gev = sem("xc_made"), sem("gate_product_done"), sem("gate_evacuated")
        s_mxa, s_mxv = sem("mix_act_made"), sem("mix_dve_made")
        s_mst = [sem("ya_stored"), sem("yb_stored"), sem("yd_stored")]
        s_scan = sem("scan_done")
        s_lam = sem("lambda_step")
        s_mfree = sem("mix_tiles_free")
        s_qz, s_qbd, s_kqs = sem("qbd_zeroed"), sem("qbd_made"), sem("kqs_in")
        s_pt = sem("page_table_in")
        s_kin = [sem("k_pages_in0"), sem("k_pages_in1")]
        s_ktr, s_kte, s_kmm = sem("k_transposed"), sem("kT_evacuated"), sem("k_product_done")
        s_zs, s_sns, s_zn = sem("z_sample_done"), sem("sn_sample_made"), sem("z_new_done")
        s_ws, s_wtr, s_wte = sem("w_sample_made"), sem("w_sample_transposed"), sem("wT_sample_made")
        s_vin = [sem("v_pages_in0"), sem("v_pages_in1")]
        s_vuse, s_vnin, s_vnuse = sem("v_pages_used"), sem("v_new_in"), sem("v_new_used")
        s_vnt, s_vnat, s_vnst = sem("v_new_transposed"), sem("v_new_natural"), sem("v_new_stored")
        s_yse, s_yst = sem("yc_sample_made"), sem("yc_stored")
        s_qkv, s_pair, s_vtr, s_vnp = sem("qkv_in"), sem("pair_done"), sem("v_transposed"), sem("v_natural")
        s_z, s_sn, s_msk, s_w = sem("z_done"), sem("sn_made"), sem("diag_masked"), sem("w_made")
        s_tr, s_wt, s_av, s_yc = sem("w_transposed"), sem("wT_made"), sem("av_group_done"), sem("yc_made")
        s_ycs = sem("yc_prompt_stored")
        s_yin, s_x1in = sem("y_in"), sem("x1_in")
        s_yh, s_yl = sem("y_hi_made"), sem("y_lo_made")
        s_step, s_oev, s_ft = sem("step_done"), sem("outproj_evacuated"), sem("forward_transposed")
        s_r, s_hh, s_hf, s_hl = sem("relu_made"), sem("h_hi_made"), sem("h_full_made"), sem("h_lo_made")
        s_fev = sem("mlp_evacuated")
        s_row, s_out, s_so = sem("row_scaled"), sem("y_stored"), sem("state_stored")
        s_rowfree = sem("nat3_free")

        def wait_apart(eng, sem, value):
            eng.wait_ge(sem, value)
            eng.nop(nofuse=True)

        class Tally:

            def __init__(self, eng, sem):
                self.eng, self.sem, self.base, self.n = eng, sem, 0, 0

            def up(self, ins):
                ins.then_inc(self.sem, 1)
                self.n += 1

            def sync(self):
                wait_apart(self.eng, self.sem, self.base + self.n)

            def op(self, ins):
                self.up(ins)
                self.sync()

            @contextmanager
            def loop(self, count, per):
                base, n = self.base, self.n
                with self.eng.Fori(0, count) as i:
                    self.base, self.n = base + n + i * per, 0
                    yield i
                    assert self.n == per, (self.n, per)
                self.base, self.n = base, n + count * per

        block = ctx.enter_context(nc.Block())

        @block.sync
        def _(sp):
            n_const = [0]

            def const(dst, src):
                sp.dma_start(dst, src).then_inc(s_const, 16)
                n_const[0] += 16

            def load_raw(slot, tile):
                sp.dma_start(raw[:, slot, :], w_all[bass.ds(tile, 1)].rearrange("o p n -> p (o n)")).then_inc(
                    s_raw[slot], 16)

            sp.sem_inc(s_nat, NAT0)
            sp.sem_inc(s_vnuse, 1)
            sp.sem_inc(s_pair, 1)
            const(ident[:, :], ident_d)
            const(ln_gb[:, :, :], lnp)
            load_raw(0, 0)
            load_raw(1, 1)
            with sp.Fori(0, NB) as b:
                sp.wait_ge(s_nat, b * NR + NAT0)
                sp.dma_start(xin[0:ROW], x_all[bass.ds(b * BLK, BLK)].rearrange("(j p) d -> p j d", p=ROW)).then_inc(
                    s_xin, 16)
            const(pv[:, :, :], pvec)
            const(mask[:, :], masks)
            const(bias_h[:, 0:NH], sbh)
            const(bias_h[:, NH:NH + 1], sbr)
            sp.wait_ge(s_mzero, 1)
            for c in range(2):
                for n, src in enumerate((gates_a, gates_x, poolw)):
                    for h in range(2):
                        const(gsel[HD * h:HD * h + HD, c, n, HD * h:HD * h + HD], src[2 * c + h])
            assert n_const[0] == CONST_ALL

            def proj_steps(first, last, dst):
                with sp.Fori(first // 2, last // 2) as i:
                    for u in range(2):
                        sp.wait_ge(s_wl, i * 2 + (u + 1))
                        load_raw(u, i * 2 + (u + 2))
                        sp.wait_ge(s_ev1, i * 10 + (5 * u + 10))
                        sp.dma_start(dst[bass.ds(i * 2 + (u - (first if dst is kv_out else 0)), 1)].rearrange(
                            "o p t -> p (o t)"), stage[:, u, :]).then_inc(s_stg[u], 16)

            proj_steps(0, K0, proj_d)
            proj_steps(K0, K0 + 4, kv_out)
            proj_steps(K0 + 4, NC_IN, proj_d)
            for u in range(2):
                sp.wait_ge(s_stg[u], 16 * (NC_IN // 2) + 16)

            for c in range(2):
                if c:
                    sp.wait_ge(s_mfree, 3 * c)
                for dst, t in ((mx[0][:, BUFA:BUFA + SEQ], XA), (mx[1][:, 0:SEQ], GA)):
                    sp.dma_start(dst, proj_d[AT[t, c], :, 0:SEQ]).then_inc(s_mld[0], 16)
                sp.dma_start(ext_of(mx[0], BUFA)[:, :, BUFA:], new_of(proj_d[AT[XA, c]])).then_inc(s_mld[0], 16)
                sp.dma_start(ext_of(mx[0], BUFA)[:, :, 0:BUFA], st_a[c]).then_inc(s_mld[0], 16)
                sp.dma_start(mx[1][:, SEQ:TOK], proj_d[AT[GA, c], :, SEQ:TOK]).then_inc(s_mld[0], 16)
                sp.dma_start(hs[:, c, :], st_h[c]).then_inc(s_mld[0], 16)
                sp.wait_ge(s_mxv, 2 * c + 1)
                sp.dma_start(y_d[0 + c], mx[6][:, 0:TOK]).then_inc(s_mst[0], 16)
                sp.wait_ge(s_mfree, 3 * c + 1)
                sp.dma_start(mx[0][:, 0:TOK], proj_d[AT[XB, c]]).then_inc(s_mld[1], 16)
                sp.dma_start(mx[1][:, 0:TOK], proj_d[AT[GC, c]]).then_inc(s_mld[1], 16)
                sp.dma_start(mx[2][:, 0:TOK], proj_d[AT[GB, c]]).then_inc(s_mld[1], 16)
                sp.dma_start(ext_of(mx[3], BUFB)[:, :, 0:BUFB], st_b[c]).then_inc(s_mld[1], 16)
                sp.wait_ge(s_mxv, 2 * c + 2)
                sp.dma_start(y_d[2 + c], mx[4][:, 0:TOK]).then_inc(s_mst[1], 16)
                sp.wait_ge(s_mfree, 3 * c + 2)
                sp.dma_start(mx[0][:, BUFP:BUFP + SEQ], proj_d[AT[XP, c], :, 0:SEQ]).then_inc(s_mld[2], 16)
                sp.dma_start(ext_of(mx[0], BUFP)[:, :, BUFP:], new_of(proj_d[AT[XP, c]])).then_inc(s_mld[2], 16)
                sp.dma_start(ext_of(mx[0], BUFP)[:, :, 0:BUFP], st_p[c]).then_inc(s_mld[2], 16)
                sp.wait_ge(s_mxa, c + 1)
                sp.dma_start(y_d[6 + c], mx[6][:, 0:TOK]).then_inc(s_mst[2], 16)
            sp.wait_ge(s_mfree, 6)
            sp.dma_start(so_out, so[:, :, :]).then_inc(s_so, 16)

            sp.dma_start(ptb[:, :], ptab).then_inc(s_pt, 16)
            for c in range(2):
                for n, (src, t) in enumerate(((proj_d, AT[Q, 0]), (kv_out, 0), (kv_out, 2))):
                    sp.dma_start(kqs[:, 2 * n + c, :], src[t + c, :, SEQ:TOK]).then_inc(s_kqs, 16)
            sp.wait_ge(s_pt, 16)
            with sp.Fori(0, NPG // 4) as c:
                for b in range(DECB):
                    ids = [sp.value_load(ptb[0:1, bass.ds(c * 4 + (b * NPG + g), 1)], min_val=0, max_val=ck.shape[0] - 1)
                           for g in range(4)]
                    sp.wait_ge(s_ktr, c * DECB + (b + 1))
                    for g in range(4):
                        sp.dma_start(kpg[:, b % 2, g, :], ck[bass.ds(ids[g], 1)].rearrange("o p n -> p (o n)")).then_inc(
                            s_kin[b % 2], 16)
            sp.wait_ge(s_vnat, 2)
            sp.dma_start(vn_d, vnat[:, :]).then_inc(s_vnst, 16)
            sp.wait_ge(s_vnst, 16)
            with sp.Fori(0, DECB) as b:
                sp.wait_ge(s_vnuse, b + 1)
                sp.dma_start(vnew[:, :], vn_d[bass.ds(b * DECT, DECT)]).then_inc(s_vnin, 16)
                for c in range(4):
                    ids = [sp.value_load(ptb[0:1, bass.ds(b * NPG + (c * 4 + g), 1)], min_val=0, max_val=ck.shape[0] - 1)
                           for g in range(4)]
                    sp.wait_ge(s_vuse, b * 4 + (c + 1))
                    for g in range(4):
                        sp.dma_start(vpg[:, c % 2, g, :], cv[bass.ds(ids[g], 1)].rearrange("o p n -> p (o n)")).then_inc(
                            s_vin[c % 2], 16)
            sp.wait_ge(s_yse, 4)
            for c in range(2):
                sp.dma_start(y_d[4 + c, :, SEQ:TOK], ycs[:, c, :]).then_inc(s_yst, 16)
            sp.wait_ge(s_yst, 32)
            for m in s_mst:
                sp.wait_ge(m, 32)
            sp.wait_ge(s_so, 16)

            with sp.Fori(0, 2) as hp:
                sp.wait_ge(s_pair, hp + 1)
                sp.dma_start(qT[:, :], proj_d[bass.ds(hp + AT[Q, 0], 1), :, 0:SEQ].rearrange("o p t -> p (o t)")).then_inc(s_qkv, 16)
                sp.dma_start(kT[:, :], kv_out[bass.ds(hp, 1), :, 0:SEQ].rearrange("o p t -> p (o t)")).then_inc(s_qkv, 16)
                sp.dma_start(vT[:, :], kv_out[bass.ds(hp + 2, 1), :, 0:SEQ].rearrange("o p t -> p (o t)")).then_inc(s_qkv, 16)
                sp.wait_ge(s_yc, hp * 32 + 32)
                sp.dma_start(y_d[bass.ds(hp + 4, 1), :, 0:SEQ].rearrange("o p t -> p (o t)"), ycT[:, :]).then_inc(s_ycs, 16)

            sp.wait_ge(s_pair, 3)
            sp.wait_ge(s_ycs, 48)
            const(gb2[:, :, :], rows2)

            def load_step(n, tile, u):
                sp.wait_ge(s_wl, n + (NC_IN - 1))
                load_raw(u, tile)

            W0 = NC_IN + PRO
            with sp.Fori(1, PRO // 2) as i:
                for u in range(2):
                    load_step(i * 2 + u, i * 2 + (NC_IN + u), u)
            with sp.Fori(0, NB - 1) as b:
                with sp.Fori(0, STEPS // 2) as i:
                    for u in range(2):
                        load_step(b * STEPS + i * 2 + (PRO + u), i * 2 + (W0 + u), u)
            for first, count, skip in ((0, SE_, 0), (SE_, LAST - SE_, KT)):
                with sp.Fori(0, count // 2) as i:
                    for u in range(2):
                        load_step(i * 2 + (PRO + (NB - 1) * STEPS + first + u), i * 2 + (W0 + first + skip + u), u)
            sp.wait_ge(s_out, 16 * NR * NB)

        @block.tensor
        def _(pe):
            def back(b, base, nat, ks=range(KT)):
                for k in ks:
                    if k >= 4:
                        pe.wait_ge(s_xf, b * KT + (base + k - 3))
                    for j in range(NR):
                        ins = pe.transpose(PS[:, 4 + k % 4, j * ROW:(j + 1) * ROW], nat[0:ROW, j, k * P:(k + 1) * P],
                                           ident[0:ROW, 0:ROW])
                    ins.then_inc(s_bt, 1)

            def step(slot, out, moving, first, last):
                for k in range(KT):
                    mh, ml = moving(k)
                    w_h, w_l = wh[:, slot, k * P:(k + 1) * P], wl[:, slot, k * P:(k + 1) * P]
                    pe.matmul(out, w_h, mh, start=(first and k == 0), stop=False)
                    pe.matmul(out, w_h, ml, start=False, stop=False)
                    ins = pe.matmul(out, w_l, mh, start=False, stop=(last and k == KT - 1))
                return ins

            pe.wait_ge(s_const, 32)
            with pe.Fori(0, NB) as b:
                pe.wait_ge(s_nat, b * NR + (NAT0 + NR))
                back(b, 0, nat1)
            pe.wait_ge(s_xh, NB * KT)
            pe.wait_ge(s_xl, NB * KT)
            with pe.Fori(0, NC_IN // 2) as i:
                for u in range(2):
                    pe.wait_ge(s_wh, i * 2 + (u + 1))
                    pe.wait_ge(s_wl, i * 2 + (u + 1))
                    for b in range(NB):
                        pe.wait_ge(s_ev1, i * 10 + (5 * u + b + 1))
                        cols = slice(b * BLK, (b + 1) * BLK)
                        step(u, PS[:, b, 0:BLK], lambda k: (xh[:, k, cols], xl[:, k, cols]), True, True).then_inc(s_grp, 1)

            pe.wait_ge(s_const, CONST_ALL)
            pe.wait_ge(s_ev1, NB * NC_IN + NB)
            n = 0
            for c in range(2):
                for what in range(3):
                    pe.wait_ge(s_xc, 2 * c + (1 if what < 2 else 2))
                    src = mx[2] if what < 2 else mx[5]
                    for a in range(0, TOK, CHW):
                        w = min(CHW, TOK - a)
                        if n >= 4:
                            pe.wait_ge(s_gev, n - 3)
                        pe.matmul(PS[:, n % 4, 0:w], gsel[:, c, what, :], src[:, a:a + w], start=True, stop=True).then_inc(s_gps, 1)
                        n += 1

            def qsel(b, h):
                return qbd[:, (2 * b + h) * P:(2 * b + h + 1) * P]

            pe.wait_ge(s_gev, n)
            pe.wait_ge(s_kqs, 96)
            for c in range(2):
                pe.transpose(PS[0:SMP, 6 + c, 0:P], kqs[:, 4 + c, :], ident[:, :]).then_inc(s_vnt, 1)
            pe.wait_ge(s_qbd, 4)
            pe.sem_inc(s_ktr, 2)
            pe.sem_inc(s_kmm, 2)
            pe.sem_inc(s_sns, 1)
            for b in range(DECB):
                for h in range(2):
                    ins = pe.matmul(PS[:, 5, 0:DECT], qsel(b, h), kqs[:, 2 + h, b * DECT:(b + 1) * DECT],
                                    start=(b == 0 and h == 0), stop=(b == DECB - 1 and h == 1))
            ins.then_inc(s_zn, 1)
            with pe.Fori(0, NPG // 4) as c:
                for b in range(DECB + 1):
                    if b < DECB:
                        pe.wait_ge(s_kin[b % 2], c * (64 * DECB // 2) + 64 * (b // 2 + 1))
                        pe.wait_ge(s_kte, c * DECB + (b + 1))
                        for h in range(2):
                            for g in range(4):
                                ins = pe.transpose(PS[:, 2 * (b % 2) + h, g * P:(g + 1) * P],
                                                   kpg[:, b % 2, g, h * P:(h + 1) * P], ident[:, :])
                        ins.then_inc(s_ktr, 1)
                    if b >= 1:
                        d = b - 1
                        if d == 0:
                            pe.wait_ge(s_sns, c + 1)
                        pe.wait_ge(s_kte, c * DECB + (d + 3))
                        for h in range(2):
                            ins = pe.matmul(PS[:, 4, :], qsel(d, h), kts[:, d % 2, h, :],
                                            start=(d == 0 and h == 0), stop=(d == DECB - 1 and h == 1))
                        ins.then_inc(s_kmm, 1)
            pe.wait_ge(s_ws, 1)
            for g in range(4):
                for j in range(4):
                    t = 4 * g + j
                    ins = pe.transpose(PS[:, g, j * P:(j + 1) * P], sS[:, t * P:(t + 1) * P], ident[:, :])
                ins.then_inc(s_wtr, 1)
            pe.wait_ge(s_sns, 6)
            pe.transpose(PS[0:DECT, 5, 0:P], sS[:, PAST:PAST + DECT], ident[:, :]).then_inc(s_wtr, 1)
            pe.sem_inc(s_vuse, 2)
            pe.wait_ge(s_wte, 5)
            pe.wait_ge(s_vnat, 2)
            with pe.Fori(0, DECB) as b:
                for c in range(4):
                    pe.wait_ge(s_vin[c % 2], b * 128 + 64 * (c // 2 + 1))
                    for g in range(4):
                        for h in range(2):
                            ins = pe.matmul(PS[:, 6 + h, bass.ds(b * 8, 8)], vpg[:, c % 2, g, h * P:(h + 1) * P],
                                            wtS[:, 4 * c + g, bass.ds(b * 16 + 8 * h, 8)],
                                            start=(c == 0 and g == 0), stop=False)
                    ins.then_inc(s_vuse, 1)
                pe.wait_ge(s_vnin, b * 16 + 16)
                for h in range(2):
                    ins = pe.matmul(PS[:, 6 + h, bass.ds(b * 8, 8)], vnew[:, h * P:(h + 1) * P],
                                    wtN[:, bass.ds(b * 16 + 8 * h, 8)], start=False, stop=True)
                ins.then_inc(s_vnuse, 1)
            pe.wait_ge(s_yse, 4)

            with pe.Fori(0, 2) as hp:
                pe.wait_ge(s_qkv, hp * 48 + 48)
                for g in range(4):
                    for j in range(4):
                        t = 4 * g + j
                        ins = pe.transpose(PS[:, 4 + g, j * P:(j + 1) * P], vT[:, t * P:(t + 1) * P], ident[:, :])
                    ins.then_inc(s_vtr, 1)
                pe.wait_ge(s_vnp, hp * 4 + 4)
                cc = tg = 0

                def scores(n):
                    nonlocal cc
                    hl_, qt = divmod(n, QT)
                    rows = slice(HD * hl_, HD * hl_ + HD)
                    W = (qt + 1) * P
                    for a in range(0, W, CHW):
                        w = min(CHW, W - a)
                        if cc >= 4:
                            pe.wait_ge(s_sn, hp * 80 + (cc - 3))
                        pe.matmul(PS[:, cc % 4, 0:w], qT[rows, qt * P:(qt + 1) * P], kT[rows, a:a + w],
                                  start=True, stop=True).then_inc(s_z, 1)
                        cc += 1

                scores(0)
                for n in range(2 * QT):
                    if n + 1 < 2 * QT:
                        scores(n + 1)
                    hl_, qt = divmod(n, QT)
                    pe.wait_ge(s_w, hp * 32 + (n + 2))
                    if n >= 2:
                        pe.wait_ge(s_yc, hp * 32 + (n - 1))
                    groups = [list(range(a, min(a + 4, qt + 1))) for a in range(0, qt + 1, 4)]

                    def values(g, at):
                        pe.wait_ge(s_wt, hp * 80 + (at + 1))
                        for j, t in enumerate(groups[g]):
                            ins = pe.matmul(PS[HD * hl_:HD * hl_ + HD, 6 + n % 2, 0:P], vN[:, t, HD * hl_:HD * hl_ + HD],
                                            wtP[:, at % 2, j * P:(j + 1) * P], start=(t == 0), stop=(t == qt))
                        ins.then_inc(s_av, 1)

                    for g, ts in enumerate(groups):
                        if tg >= 2:
                            pe.wait_ge(s_wt, hp * 80 + (tg - 1))
                        for j, t in enumerate(ts):
                            ins = pe.transpose(PS[:, 4 + tg % 2, j * P:(j + 1) * P], sP[:, n % 2, t * P:(t + 1) * P], ident[:, :])
                        ins.then_inc(s_tr, 1)
                        if g:
                            values(g - 1, tg - 1)
                        tg += 1
                    values(len(groups) - 1, tg - 1)
                pe.wait_ge(s_yc, hp * 32 + 32)
                pe.sem_inc(s_pair, 1)

            def weights(n):
                pe.wait_ge(s_wh, n + (NC_IN + 1))
                pe.wait_ge(s_wl, n + (NC_IN + 1))

            a_parts = lambda k: (ah[:, k, :], al[:, k, :])

            def out_proj(n, blk, before_first):
                pe.wait_ge(s_yh, blk * 2 + 2)
                pe.wait_ge(s_yl, blk * 2 + 2)
                for s in range(KT):
                    weights(n + s)
                    if s < 4:
                        before_first(s)
                    else:
                        pe.wait_ge(s_oev, blk * KT + (s - 3))
                    step(s % 2, PS[:, s % 4, 0:BLK], a_parts, True, True).then_inc(s_step, 1)

            def ffn1(n, f, u):
                weights(n)
                pe.wait_ge(s_r, f + 1)
                step(u % 2, PS[:, u % 4, 0:BLK], a_parts, True, True).then_inc(s_step, 1)

            def ffn2(n, o, h, u, free, before=lambda q: None):
                for q in range(2):
                    before(q)
                    weights(n + q)
                    pe.wait_ge(s_hh, h + KT * (q + 1))
                    pe.wait_ge(s_hl, h + (KT * (q + 1) + 1))
                    if q == 0:
                        pe.wait_ge(s_fev, o + 1)
                        free()
                    step(q, PS[:, u % 4, 0:BLK], lambda k: (hh[:, KT * q + k, :], hl[:, KT * q + k, :]),
                         q == 0, q == 1).then_inc(s_step, 1)

            def forward(src, lnb, j):
                pe.wait_ge(s_nat, lnb + (NATB + j - 1))
                for k in range(KT):
                    bank = 4 + 2 * (j % 2) + k // 4
                    ins = pe.transpose(PS[0:ROW, bank, (k % 4) * P:(k % 4 + 1) * P], src[:, k, j * ROW:(j + 1) * ROW], ident[:, :])
                ins.then_inc(s_ft, 1)

            def back1(blk, lnb, q):
                if q == 0:
                    pe.wait_ge(s_nat, lnb + (NATB + NR))
                back(blk, NB * KT, nat3, range(2 * q, 2 * q + 2))

            def split_x1(blk):
                pe.wait_ge(s_xh, blk * KT + (NB * KT + KT))
                wait_apart(pe, s_xl, blk * KT + (NB * KT + KT))

            def ffn_body(b, n):
                with pe.Fori(0, (HF - NN) // 4) as i:
                    for u in range(4):
                        ffn1(n + i * 4 + u, b * FT + i * 4 + (NN + u), u)
                with pe.Fori(0, 2) as i:
                    for u in range(4):
                        ffn2(n + i * 8 + (SB_ + 2 * u), b * (2 * KT) + i * 4 + u, b * FT, u,
                             lambda: pe.wait_ge(s_r, b * FT + (HF + u + 1)))
                with pe.Fori(0, HF // 4) as i:
                    for u in range(4):
                        pe.wait_ge(s_fev, b * (2 * KT) + (KT + u + 1))
                        ffn1(n + i * 4 + (SC_ + u), b * FT + i * 4 + (HF + u), u)

            def iteration_tail(b, n):
                ln1, ln2 = b * 8 + 4, b * 8 + 8

                def output(o, free, before=lambda q: None):
                    at = SD_ if o < D1 // 2 else SD2 - D1
                    ffn2(n + (at + 2 * o), b * (2 * KT) + (KT + o), b * FT + HF, o, free, before)

                for o in range(D1 // 2):
                    output(o, lambda: pe.wait_ge(s_r, b * FT + (FT + o + 1)))

                def bank_free(s):
                    if s < D1 // 2:
                        pe.wait_ge(s_fev, b * (2 * KT) + (KT + s + 5))
                    else:
                        pe.wait_ge(s_r, b * FT + (FT + s + 1))

                out_proj(n + SE_, b + 1, bank_free)

                def norm1(d):
                    if d == 1:
                        pe.wait_ge(s_oev, b * KT + 2 * KT)
                    if 1 <= d <= NR:
                        forward(xr, ln1, d - 1)
                    if 6 <= d < 10:
                        back1(b + 1, ln1, d - 6)

                for o in range(D1 // 2, KT):
                    output(o, lambda: pe.wait_ge(s_oev, b * KT + (KT + min(o + 5, KT))),
                           lambda q: norm1(2 * o - D1 + q))
                split_x1(b + 1)
                for a in range(NN):
                    if a == 1:
                        pe.wait_ge(s_fev, b * (2 * KT) + (2 * KT + 4))
                    if 1 <= a <= NR:
                        forward(acc, ln2, a - 1)
                    if a < 4:
                        pe.wait_ge(s_fev, b * (2 * KT) + (KT + a + 9))
                    ffn1(n + (SN_ + a), b * FT + (FT + a), a)

            out_proj(0, 0, lambda s: None)
            pe.wait_ge(s_oev, KT)
            for j in range(NR):
                forward(xr, 0, j)
            for q in range(4):
                back1(0, 0, q)
            split_x1(0)
            for a in range(NN):
                ffn1(KT + a, a, a)
            with pe.Fori(0, NB - 1) as b:
                n = b * STEPS + PRO
                ffn_body(b, n)
                iteration_tail(b, n)
            b, n = NB - 1, (NB - 1) * STEPS + PRO
            ffn_body(b, n)
            with pe.Fori(0, 2) as i:
                for u in range(4):
                    ffn2(n + (SD_ + 2 * u) + i * 8, b * (2 * KT) + KT + u + i * 4, b * FT + HF, u,
                         lambda: pe.wait_ge(s_r, b * FT + (FT + u + 1)))
            pe.wait_ge(s_fev, NB * 2 * KT + 4)
            for j in range(NR):
                forward(acc, 8 * b + 4, j)

        @block.scalar
        def _(act):
            own = Tally(act, s_act)

            def split_hi(slot, uses):
                act.wait_ge(s_raw[slot], uses * 16)
                act.activation(wh[:, slot, :], raw[:, slot, :], ACT.Copy).then_inc(s_wh, 1)

            def norm(src, dst, j, col):
                act.activation(dst, src, ACT.Identity, bias=nmr[0:ROW, col:col + 1], scale=rstd[0:ROW, col:col + 1]).then_inc(s_nat, 1)

            def back_hi(b, base, full, hi, ks=range(KT)):
                for k in ks:
                    wait_apart(act, s_xf, b * KT + (base + k + 1))
                    act.activation(hi(k), full[:, k, :], ACT.Copy).then_inc(s_xh, 1)

            act.wait_ge(s_const, 32)
            split_hi(0, 1)
            split_hi(1, 1)
            with act.Fori(0, NB) as b:
                act.wait_ge(s_ve, b + 1)
                act.activation(std[0:ROW, :], var[0:ROW, :], ACT.Sqrt).then_inc(s_std, 1)
                act.wait_ge(s_nmr, b + 1)
                for j in range(NR):
                    norm(xin[0:ROW, j, :], nat1[0:ROW, j, :], j, j)
                back_hi(b, 0, t1, lambda k: xh[:, k, bass.ds(b * BLK, BLK)])
                act.wait_ge(s_xf, b * KT + KT)
                act.dma_start(x1_d[:, :, bass.ds(b * BLK, BLK)].rearrange("k p t -> p k t"), t1[:, :, :]).then_inc(s_t1st, 16)
            act.sem_inc(s_ev1, 5)
            act.sem_inc(s_stg[0], 16)
            act.sem_inc(s_stg[1], 16)
            act.wait_ge(s_t1st, 16 * NB + 16)
            with act.Fori(0, NC_IN // 2) as i:
                for u in range(2):
                    act.wait_ge(s_stg[u], i * 16 + 16)
                    for b in range(NB):
                        act.wait_ge(s_grp, i * 10 + (5 * u + b + 1))
                        act.activation(stage[:, u, b * BLK:(b + 1) * BLK], PS[:, b, 0:BLK], ACT.Copy).then_inc(s_ev1, 1)
                    split_hi(u, i + 2)

            def gates(n0, c, dst, func, bias, scale=1.0):
                n = n0
                for a in range(0, TOK, CHW):
                    w = min(CHW, TOK - a)
                    act.wait_ge(s_gps, n + 1)
                    act.activation(dst[:, a:a + w], PS[:, n % 4, 0:w], func, bias=bias, scale=scale).then_inc(s_gev, 1)
                    n += 1
                return n

            n = 0
            act.wait_ge(s_const, CONST_ALL)
            act.wait_ge(s_lam, 1)
            own.up(act.activation(lam[:, :, 1], lam[:, :, 0], ACT.Exp, scale=-1.0))
            act.wait_ge(s_lam, 2)
            own.up(act.activation(lam[:, :, 3], lam[:, :, 2], ACT.Ln))
            for c in range(2):
                act.wait_ge(s_lam, 3)
                act.wait_ge(s_mst[1], 16 * c)
                n = gates(n, c, mx[3], ACT.Sigmoid, pv[:, c, PBA:PBA + 1])
                n = gates(n, c, mx[4], ACT.Sigmoid, pv[:, c, PBX:PBX + 1])
                act.wait_ge(s_gev, n)
                own.up(act.activation(mx[3][:, 0:TOK], mx[3][:, 0:TOK], ACT.Tanh, scale=lam[:, c, 7:8]))
                own.sync()
                own.up(act.activation(mx[5][:, 0:TOK], mx[3][:, 0:TOK], ACT.Sqrt))
                act.wait_ge(s_mld[0], (c + 1) * 96)
                own.up(act.activation(mx[1][:, 0:TOK], mx[1][:, 0:TOK], ACT.Gelu_apprx_tanh))
                act.wait_ge(s_mst[0], 16 * (c + 1))
                n = gates(n, c, mx[6], ACT.Copy, 0.0, pv[:, c, PSC:PSC + 1])
                act.wait_ge(s_gev, n)
                act.sem_inc(s_mxa, 1)

            act.wait_ge(s_vnt, 2)
            for c in range(2):
                act.activation(vnat[:, c * P:(c + 1) * P], PS[0:SMP, 6 + c, 0:P], ACT.Copy).then_inc(s_vnat, 1)
            act.sem_inc(s_kte, 2)
            with act.Fori(0, NPG // 4) as c:
                for b in range(DECB):
                    act.wait_ge(s_ktr, c * DECB + (b + 3))
                    act.wait_ge(s_kmm, c * DECB + (b + 1))
                    act.activation(kts[:, b % 2, :, :], PS[:, 2 * (b % 2):2 * (b % 2) + 2, :], ACT.Copy).then_inc(s_kte, 1)
                wait_apart(act, s_kmm, c * DECB + (DECB + 2))
                own_c = bass.ds(c * CHW, CHW)
                act.activation(sS[:, own_c], PS[:, 4, :], ACT.Sigmoid, bias=bias_h[:, NH:NH + 1], scale=HD ** -0.5)
                act.activation(nS[:, own_c], PS[:, 4, :], ACT.Sigmoid, bias=nbias_h[:, NH:NH + 1], scale=-HD ** -0.5).then_inc(s_sns, 1)
            act.wait_ge(s_zn, 1)
            act.activation(sS[:, PAST:PAST + DECT], PS[:, 5, 0:DECT], ACT.Sigmoid, bias=bias_h[:, NH:NH + 1], scale=HD ** -0.5)
            act.activation(nS[:, PAST:PAST + DECT], PS[:, 5, 0:DECT], ACT.Sigmoid, bias=nbias_h[:, NH:NH + 1],
                           scale=-HD ** -0.5).then_inc(s_sns, 1)
            for g in range(4):
                act.wait_ge(s_wtr, g + 1)
                act.activation(wtS[:, 4 * g:4 * g + 4, :].rearrange("p a b -> p (a b)"), PS[:, g, :], ACT.Copy).then_inc(s_wte, 1)
            act.wait_ge(s_wtr, 5)
            act.activation(wtN[:, :], PS[0:DECT, 5, 0:P], ACT.Copy).then_inc(s_wte, 1)

            with act.Fori(0, 2) as hp:
                for g in range(4):
                    act.wait_ge(s_vtr, hp * 4 + (g + 1))
                    act.activation(vN[:, 4 * g:4 * g + 4, :].rearrange("p a b -> p (a b)"), PS[:, 4 + g, :], ACT.Copy).then_inc(s_vnp, 1)
                cc = tg = 0

                def sig(n):
                    nonlocal cc
                    hl_, qt = divmod(n, QT)
                    W = (qt + 1) * P
                    if n >= 2:
                        act.wait_ge(s_tr, hp * 80 + groups_until(n - 1))
                    for a in range(0, W, CHW):
                        w = min(CHW, W - a)
                        wait_apart(act, s_z, hp * 80 + (cc + 1))
                        act.activation(sP[:, n % 2, a:a + w], PS[:, cc % 4, 0:w], ACT.Sigmoid, scale=HD ** -0.5,
                                       bias=bias_h[:, bass.ds(hp * 2 + hl_, 1)])
                        act.activation(nP[:, n % 2, a:a + w], PS[:, cc % 4, 0:w], ACT.Sigmoid, scale=-HD ** -0.5,
                                       bias=nbias_h[:, bass.ds(hp * 2 + hl_, 1)]).then_inc(s_sn, 1)
                        cc += 1

                sig(0)
                for n in range(2 * QT):
                    if n + 1 < 2 * QT:
                        sig(n + 1)
                    qt = n % QT
                    for a in range(0, qt + 1, 4):
                        w = min(4, qt + 1 - a) * P
                        act.wait_ge(s_tr, hp * 80 + (tg + 1))
                        if tg >= 2:
                            act.wait_ge(s_av, hp * 80 + (tg - 1))
                        act.activation(wtP[:, tg % 2, 0:w], PS[:, 4 + tg % 2, 0:w], ACT.Copy).then_inc(s_wt, 1)
                        tg += 1

            act.wait_ge(s_pair, 3)
            act.wait_ge(s_ycs, 48)
            act.wait_ge(s_yst, 32)
            for m in s_mst:
                act.wait_ge(m, 32)
            act.sem_inc(s_r, 4)
            act.sem_inc(s_rowfree, 1)

            def hi_after(n, u):
                act.wait_ge(s_step, n + 1)
                act.wait_ge(s_raw[u], n * 8 + (NC_IN + 4 - u) * 8)
                act.activation(wh[:, u, :], raw[:, u, :], ACT.Copy).then_inc(s_wh, 1)

            def cols(blk):
                return bass.ds(blk * BLK, BLK)

            def load_y(blk):
                act.dma_start(yin[:, :, :], y_d[:, :, cols(blk)].rearrange("k p t -> p k t")).then_inc(s_yin, 16)

            def load_x1(blk):
                act.dma_start(xr[:, :, :], x1_d[:, :, cols(blk)].rearrange("k p t -> p k t")).then_inc(s_x1in, 16)

            def split_y(blk):
                act.wait_ge(s_yin, blk * 16 + 16)
                for g in range(2):
                    act.activation(ah[:, 4 * g:4 * g + 4, :], yin[:, 4 * g:4 * g + 4, :], ACT.Copy).then_inc(s_yh, 1)

            def ln_std(lnb, j):
                act.wait_ge(s_ve, lnb + (NB + j + 1))
                act.activation(std[0:ROW, j:j + 1], var[0:ROW, j:j + 1], ACT.Sqrt).then_inc(s_std, 1)

            def ln_norm(lnb, j):
                act.wait_ge(s_nmr, lnb + (NB + j + 1))
                bank = 4 + 2 * (j % 2)
                norm(PS[0:ROW, bank:bank + 2, :].rearrange("p a b -> p (a b)"), nat3[0:ROW, j, :], j, j)

            def hidden_hi(f, at, u):
                act.wait_ge(s_hf, f + 1)
                act.activation(rbuf[:, u % 2, :], PS[:, u % 4, 0:BLK], ACT.Relu).then_inc(s_r, 1)
                wait_apart(act, s_r, f + 5)
                act.activation(tile_of(hh, at), rbuf[:, u % 2, :], ACT.Square).then_inc(s_hh, 1)

            def back_hi1(blk, q):
                back_hi(blk, NB * KT, xr, lambda k: ah[:, k, :], range(2 * q, 2 * q + 2))

            def norm1_task(blk, lnb, d):
                if 0 < d <= NR:
                    ln_norm(lnb, d - 1)
                if d < NR:
                    ln_std(lnb, d)
                if 5 <= d < 9:
                    back_hi1(blk, d - 5)

            load_y(0)
            load_x1(0)
            split_y(0)
            for s in range(KT):
                hi_after(s, s % 2)
            for d in range(9):
                norm1_task(0, 0, d)
            for a in range(NN):
                hi_after(KT + a, a % 2)
                hidden_hi(a, a, a)

            def ffn_body(b, n):
                with act.Fori(0, (HF - NN) // 4) as i:
                    for u in range(4):
                        hi_after(n + i * 4 + u, u % 2)
                        hidden_hi(b * FT + i * 4 + (NN + u), i * 4 + (NN + u), u)
                with act.Fori(0, HF // 4) as i:
                    for u in range(4):
                        hi_after(n + i * 4 + (SB_ + u), u % 2)
                yield
                with act.Fori(0, HF // 4) as i:
                    for u in range(4):
                        hi_after(n + i * 4 + (SC_ + u), u % 2)
                        hidden_hi(b * FT + i * 4 + (HF + u), i * 4 + u, u)

            with act.Fori(0, NB - 1) as b:
                n = b * STEPS + PRO
                act.wait_ge(s_yl, b * 2 + 2)
                load_y(b + 1)
                part = ffn_body(b, n)
                next(part)
                act.wait_ge(s_fev, b * (2 * KT) + (KT + 4))
                load_x1(b + 1)
                next(part, None)
                split_y(b + 1)
                for s in range(SD_, SD2):
                    hi_after(n + s, s % 2)
                for d in range(SN_ - SD2):
                    hi_after(n + (SD2 + d), d % 2)
                    if d == 1:
                        act.wait_ge(s_rowfree, b + 1)
                    norm1_task(b + 1, b * 8 + 4, d)
                for a in range(NN):
                    hi_after(n + (SN_ + a), a % 2)
                    hidden_hi(b * FT + (FT + a), a, a)
                    if 0 < a <= NR:
                        ln_norm(b * 8 + 8, a - 1)
                    if a < NR:
                        ln_std(b * 8 + 8, a)
            b, n = NB - 1, (NB - 1) * STEPS + PRO
            for _ in ffn_body(b, n):
                pass
            with act.Fori(0, (HF - 2) // 2) as i:
                for u in range(2):
                    hi_after(n + i * 2 + (SD_ + u), u)
            act.wait_ge(s_rowfree, NB)
            for j in range(NR + 1):
                if j:
                    ln_norm(b * 8 + 4, j - 1)
                if j < NR:
                    ln_std(b * 8 + 4, j)

        @block.vector
        def _(dve):
            own = Tally(dve, s_dve)

            def split_lo(slot, n_hi):
                dve.wait_ge(s_wh, n_hi)
                dve.tensor_tensor(wl[:, slot, :], raw[:, slot, :], wh[:, slot, :].bitcast(F32), ALU.subtract).then_inc(s_wl, 1)

            def moments(srcs, width, seq):
                for j, src in enumerate(srcs):
                    for h in range(2):
                        ins = dve.bn_stats(bn[0:ROW, j, h, :], src[:, h * 512:(h + 1) * 512])
                own.up(ins)
                own.sync()
                for j in range(width):
                    ins = dve.bn_aggr(mv[0:ROW, j, :], bn[0:ROW, j, :, :])
                own.up(ins)
                own.sync()
                dve.tensor_scalar(var[0:ROW, 0:width], mv[0:ROW, 0:width, 1], EPS, None, ALU.add).then_inc(s_ve, 1)
                dve.wait_ge(s_std, seq + 1)
                own.up(dve.reciprocal(rstd[0:ROW, 0:width], std[0:ROW, 0:width]))
                own.sync()
                dve.scalar_tensor_tensor(out=nmr[0:ROW, 0:width], in0=mv[0:ROW, 0:width, 0], scalar=-1.0,
                                         in1=rstd[0:ROW, 0:width], op0=ALU.mult, op1=ALU.mult).then_inc(s_nmr, 1)

            def back_lo(b, base, full, hi, lo, which, ks=range(KT)):
                ks = list(ks)
                for n in range(len(ks) + 1):
                    if n < len(ks):
                        k = ks[n]
                        dve.wait_ge(s_bt, b * KT + (base + k + 1))
                        dve.tensor_scalar(full(k), PS[:, 4 + k % 4, 0:BLK], ln_gb[:, which, k:k + 1], ln_gb[:, which + 1, k:k + 1],
                                          ALU.mult, ALU.add).then_inc(s_xf, 1)
                    if n:
                        k = ks[n - 1]
                        dve.wait_ge(s_xf, b * KT + (base + k + 1))
                        dve.wait_ge(s_xh, b * KT + (base + k + 1))
                        dve.tensor_tensor(lo(k), full(k), hi(k).bitcast(F32), ALU.subtract).then_inc(s_xl, 1)

            dve.memset(gsel[:, :, :, :], 0.0).then_inc(s_mzero, 1)
            dve.sem_inc(s_t1st, 16)
            dve.wait_ge(s_const, 32)
            split_lo(0, 1)
            split_lo(1, 2)
            with own.loop(NB, 3) as b:
                dve.wait_ge(s_xin, b * 16 + 16)
                moments([xin[0:ROW, j, :] for j in range(NR)], NR, b)
                dve.wait_ge(s_t1st, b * 16 + 16)
                cols = bass.ds(b * BLK, BLK)
                back_lo(b, 0, lambda k: t1[:, k, :], lambda k: xh[:, k, cols], lambda k: xl[:, k, cols], 0)
            with dve.Fori(0, NC_IN // 2) as i:
                for u in range(2):
                    dve.wait_ge(s_grp, i * 10 + (5 * u + 5))
                    split_lo(u, i * 2 + (u + 3))

            def op(ins):
                own.up(ins)
                own.sync()

            def conv(dst, src, c, col, taps, halo, bias):
                ext = ext_of(src, halo)
                dst_s = dst[:, SEQ:TOK].rearrange("p (b t) -> p b t", b=DECB)
                for j in range(taps):
                    for d_, s_ in ((dst[:, 0:SEQ], src[:, j:j + SEQ]), (dst_s, ext[:, :, j:j + DECT])):
                        if j == 0:
                            own.up(dve.tensor_scalar(d_, s_, pv[:, c, col:col + 1], bias, ALU.mult, ALU.add))
                        else:
                            own.up(dve.scalar_tensor_tensor(out=d_, in0=s_, scalar=pv[:, c, col + j:col + j + 1], in1=d_,
                                                            op0=ALU.mult, op1=ALU.add))
                    own.sync()

            dve.wait_ge(s_const, CONST_ALL)
            op(dve.tensor_scalar(nbias_h[:, :], bias_h[:, :], -1.0, None, ALU.mult))
            L = lambda n: lam[:, :, n]
            lamv = pv[:, :, PLAM]
            op(dve.tensor_scalar(L(4), lamv, -1.0, None, ALU.mult))
            dve.tensor_tensor(L(0), lamv, L(4), ALU.max).then_inc(s_lam, 1)
            dve.wait_ge(s_act, 1)
            dve.tensor_scalar(L(2), L(1), 1.0, None, ALU.add).then_inc(s_lam, 1)
            dve.wait_ge(s_lam, 2)
            op(dve.tensor_scalar(L(5), L(2), -1.0, None, ALU.add))
            op(dve.tensor_scalar(L(6), L(5), 0.0, None, ALU.is_equal))
            op(dve.tensor_tensor(L(5), L(5), L(6), ALU.add))
            op(dve.reciprocal(L(5), L(5)))
            dve.wait_ge(s_act, 2)
            op(dve.tensor_tensor(L(5), L(5), L(3), ALU.mult))
            op(dve.tensor_tensor(L(5), L(5), L(6), ALU.add))
            op(dve.tensor_tensor(L(5), L(5), L(1), ALU.mult))
            op(dve.scalar_tensor_tensor(out=L(5), in0=L(4), scalar=0.0, in1=L(5), op0=ALU.max, op1=ALU.add))
            dve.tensor_scalar(L(7), L(5), RC / 2, None, ALU.mult).then_inc(s_lam, 1)

            for c in range(2):
                dve.wait_ge(s_mld[0], (c + 1) * 96)
                op(dve.memset(mx[0][:, 0:BUFA], 0.0))
                conv(mx[2], mx[0], c, PCW, 4, BUFA, pv[:, c, PCB:PCB + 1])
                dve.sem_inc(s_xc, 1)
                nb = 1 + DECB
                own.up(dve.tensor_copy(so[:, c, SO_A:SO_A + BUFA], mx[0][:, SEQ:SEQ + BUFA]))
                op(dve.tensor_copy(so[:, c, SO_A + BUFA:SO_A + BUFA * nb].rearrange("p (b t) -> p b t", b=DECB),
                                   ext_of(mx[0], BUFA)[:, :, DECT:]))
                dve.wait_ge(s_act, 4 + 3 * c)
                T = lambda n: mx[n][:, 0:TOK]
                op(dve.tensor_scalar(T(7), T(3), 1.0, None, ALU.add))
                op(dve.reciprocal(T(7), T(7)))
                own.up(dve.tensor_scalar(T(3), T(7), 2.0, -1.0, ALU.mult, ALU.add))
                own.up(dve.scalar_tensor_tensor(out=T(5), in0=T(5), scalar=2.0, in1=T(7), op0=ALU.mult, op1=ALU.mult))
                op(dve.tensor_tensor(T(4), T(4), T(2), ALU.mult))
                op(dve.tensor_tensor(T(5), T(5), T(4), ALU.mult))
                dve.wait_ge(s_mst[2], 16 * c)
                own.up(dve.tensor_tensor_scan(mx[6][:, 0:SEQ], mx[3][:, 0:SEQ], mx[5][:, 0:SEQ], 0.0, ALU.mult, ALU.add))
                for b in range(DECB):
                    ts = slice(SEQ + b * DECT, SEQ + (b + 1) * DECT)
                    own.up(dve.tensor_tensor_scan(mx[6][:, ts], mx[3][:, ts], mx[5][:, ts], hs[:, c, b:b + 1], ALU.mult, ALU.add))
                own.sync()
                own.up(dve.tensor_copy(so[:, c, SO_H:SO_H + 1], mx[6][:, SEQ - 1:SEQ]))
                op(dve.tensor_copy(so[:, c, SO_H + 1:SO_H + nb], mx[6][:, SEQ:TOK].rearrange("p (b t) -> p b t", b=DECB)[:, :, DECT - 1]))
                dve.wait_ge(s_act, 5 + 3 * c)
                dve.tensor_tensor(T(6), T(6), T(1), ALU.mult).then_inc(s_mxv, 1)
                dve.wait_ge(s_mxv, 2 * c + 1)
                dve.sem_inc(s_mfree, 1)
                dve.wait_ge(s_mld[1], (c + 1) * 64)
                u_s = ext_of(mx[3], BUFB)
                own.up(dve.memset(mx[3][:, 0:BUFB], 0.0))
                own.up(dve.tensor_tensor(mx[3][:, BUFB:BUFB + SEQ], mx[0][:, 0:SEQ], mx[1][:, 0:SEQ], ALU.mult))
                s3 = lambda t: t[:, SEQ:TOK].rearrange("p (b t) -> p b t", b=DECB)
                op(dve.tensor_tensor(u_s[:, :, BUFB:], s3(mx[0]), s3(mx[1]), ALU.mult))
                own.up(dve.tensor_copy(so[:, c, SO_B:SO_B + BUFB], mx[3][:, SEQ:SEQ + BUFB]))
                own.up(dve.tensor_copy(so[:, c, SO_B + BUFB:SO_B + BUFB * nb].rearrange("p (b t) -> p b t", b=DECB), u_s[:, :, DECT:]))
                conv(mx[4], mx[3], c, PBW, 3, BUFB, 0.0)
                dve.tensor_tensor(T(4), T(4), T(2), ALU.mult).then_inc(s_mxv, 1)
                dve.wait_ge(s_mxv, 2 * c + 2)
                dve.sem_inc(s_mfree, 1)
                dve.wait_ge(s_mld[2], (c + 1) * 48)
                own.up(dve.memset(mx[0][:, 0:BUFP], 0.0))
                ext = ext_of(mx[0], BUFP)
                own.sync()
                own.up(dve.tensor_copy(so[:, c, SO_P:SO_P + BUFP], mx[0][:, SEQ:SEQ + BUFP]))
                own.up(dve.tensor_copy(so[:, c, SO_P + BUFP:SO_P + BUFP * nb].rearrange("p (b t) -> p b t", b=DECB), ext[:, :, DECT:]))

                def wider(dst, src, half, rows):
                    a = 2 * half - 1
                    own.up(dve.tensor_tensor(dst[rows, a:BUFP + SEQ], src[rows, a:BUFP + SEQ],
                                             src[rows, a - half:BUFP + SEQ - half], ALU.add))
                    d_, s_ = ext_of(dst, BUFP)[rows], ext_of(src, BUFP)[rows]
                    op(dve.tensor_tensor(d_[:, :, a:], s_[:, :, a:], s_[:, :, a - half:BUFP + DECT - half], ALU.add))

                every, low, high = slice(0, P), slice(0, HD), slice(HD, P)
                wider(mx[1], mx[0], 1, every)
                if c == 0:
                    wider(mx[2], mx[1], 2, high)
                    lo_t, hi_t = mx[1], mx[2]
                else:
                    wider(mx[2], mx[1], 2, every)
                    wider(mx[1], mx[2], 4, every)
                    wider(mx[2], mx[1], 8, high)
                    lo_t, hi_t = mx[1], mx[2]
                for rows, t in ((low, lo_t), (high, hi_t)):
                    own.up(dve.scalar_tensor_tensor(out=mx[5][rows, 0:SEQ], in0=t[rows, BUFP:BUFP + SEQ], scalar=pv[rows, c, PINV:PINV + 1],
                                                    in1=mx[0][rows, BUFP:BUFP + SEQ], op0=ALU.mult, op1=ALU.subtract))
                    own.up(dve.scalar_tensor_tensor(out=s3(mx[5])[rows], in0=ext_of(t, BUFP)[rows][:, :, BUFP:], scalar=pv[rows, c, PINV:PINV + 1],
                                                    in1=ext[rows][:, :, BUFP:], op0=ALU.mult, op1=ALU.subtract))
                own.sync()
                cnt = lambda rows: mask[rows, DECT + 16 * c:DECT + 16 * c + 16]
                for rows, t in ((low, lo_t), (high, hi_t)):
                    own.up(dve.tensor_tensor(mx[5][rows, 0:16], t[rows, BUFP:BUFP + 16], cnt(rows), ALU.mult))
                own.sync()
                op(dve.tensor_tensor(mx[5][:, 0:16], mx[5][:, 0:16], mx[0][:, BUFP:BUFP + 16], ALU.subtract))
                dve.sem_inc(s_xc, 1)
                dve.sem_inc(s_mfree, 1)

            op(dve.memset(qbd[:, :], 0.0))
            dve.wait_ge(s_kqs, 96)
            for h in range(NH):
                rows = slice(HD * (h % 2), HD * (h % 2) + HD)
                a = (h // 2) * P + h * DECT
                dst = qbd[rows, a:a + DECB * 272].rearrange("p (b s) -> p b s", s=272)[:, :, 0:DECT]
                dve.tensor_copy(dst, kqs[rows, h // 2, :].rearrange("p (b t) -> p b t", b=DECB)).then_inc(s_qbd, 1)
            dve.wait_ge(s_sns, 6)
            new = slice(PAST, PAST + DECT)
            own.up(dve.tensor_tensor(sS[:, new], sS[:, new], mask[:, 0:DECT], ALU.mult))
            op(dve.scalar_tensor_tensor(out=nS[:, new], in0=nS[:, new], scalar=-1.0, in1=mask[:, 0:DECT], op0=ALU.add, op1=ALU.mult))
            op(dve.tensor_scalar(nS[:, new], nS[:, new], 1.0, None, ALU.add))
            W = PAST + DECT
            own.up(dve.memset(pS[:, W:W + 1], 1.0))
            op(dve.tensor_tensor_scan(rev(pS[:, 0:W]), rev(nS[:, :]), rev(nS[:, :]), 1.0, ALU.mult, ALU.bypass))
            dve.tensor_tensor(sS[:, :], sS[:, :], pS[:, 1:W + 1], ALU.mult).then_inc(s_ws, 1)
            dve.wait_ge(s_vnuse, DECB + 1)
            for h in range(NH):
                rows = slice(HD * (h % 2), HD * (h % 2) + HD)
                src = PS[rows, 6 + h // 2, 0:DECB * 8].rearrange("p (b s) -> p b s", s=8)[:, :, DECT * (h % 2):DECT * (h % 2) + DECT]
                dve.tensor_copy(ycs[rows, h // 2, :].rearrange("p (b t) -> p b t", b=DECB), src).then_inc(s_yse, 1)

            dve.wait_ge(s_yst, 32)
            for m in s_mst:
                dve.wait_ge(m, 32)
            op(dve.memset(pP[:, SEQ:SEQ + 1], 1.0))
            dve.sem_inc(s_ycs, 16)
            dve.sem_inc(s_w, 1)
            with dve.Fori(0, 2) as hp:
                def result(n):
                    hl_, qt = divmod(n, QT)
                    rows = slice(HD * hl_, HD * hl_ + HD)
                    if n == 0:
                        dve.wait_ge(s_ycs, hp * 16 + 16)
                    dve.wait_ge(s_av, hp * 80 + groups_until(n + 1))
                    dve.tensor_copy(ycT[rows, qt * P:(qt + 1) * P], PS[rows, 6 + n % 2, 0:P]).then_inc(s_yc, 1)

                for n in range(2 * QT):
                    W = (n % QT + 1) * P
                    dve.wait_ge(s_msk, hp * 32 + (n + 1))
                    dve.wait_ge(s_w, hp * 32 + (n + 1))
                    dve.tensor_tensor_scan(rev(pP[:, SEQ - W:SEQ]), rev(nP[:, n % 2, 0:W]), rev(nP[:, n % 2, 0:W]), 1.0,
                                           ALU.mult, ALU.bypass).then_inc(s_scan, 1)
                    dve.wait_ge(s_scan, hp * 32 + (n + 1))
                    dve.tensor_tensor(sP[:, n % 2, 0:W], sP[:, n % 2, 0:W], pP[:, SEQ - W + 1:SEQ + 1], ALU.mult).then_inc(s_w, 1)
                    if n >= 1:
                        result(n - 1)
                result(2 * QT - 1)

            dve.wait_ge(s_pair, 3)
            dve.wait_ge(s_ycs, 48)
            dve.sem_inc(s_hf, 2)
            dve.sem_inc(s_fev, 4)
            dve.sem_inc(s_hl, 1)

            def lo_after(n, u):
                dve.wait_ge(s_step, n + 1)
                split_lo(u, n + (NC_IN + 3))

            def split_y(blk):
                dve.wait_ge(s_yin, blk * 16 + 16)
                for g in range(2):
                    dve.wait_ge(s_yh, blk * 2 + (g + 1))
                    dve.tensor_tensor(al[:, 4 * g:4 * g + 4, :], yin[:, 4 * g:4 * g + 4, :], ah[:, 4 * g:4 * g + 4, :].bitcast(F32),
                                      ALU.subtract).then_inc(s_yl, 1)

            def out_proj(n, blk):
                dve.wait_ge(s_x1in, blk * 16 + 16)
                for s in range(KT):
                    lo_after(n + s, s % 2)
                    dve.scalar_tensor_tensor(out=xr[:, s, :], in0=xr[:, s, :], scalar=ALPHA, in1=PS[:, s % 4, 0:BLK],
                                             op0=ALU.mult, op1=ALU.add).then_inc(s_oev, 1)

            def hidden_lo(f, at, u):
                dve.wait_ge(s_r, f + 5)
                dve.wait_ge(s_hl, f + 1)
                dve.tensor_tensor(hf[:, :], rbuf[:, u % 2, :], rbuf[:, u % 2, :], ALU.mult).then_inc(s_hf, 1)
                dve.wait_ge(s_hf, f + 3)
                dve.wait_ge(s_hh, f + 1)
                dve.tensor_tensor(tile_of(hl, at), hf[:, :], tile_of(hh, at).bitcast(F32), ALU.subtract).then_inc(s_hl, 1)

            def ln_var(lnb, j):
                dve.wait_ge(s_ft, lnb + (j + 1))
                bank = 4 + 2 * (j % 2)
                for h in range(2):
                    ins = dve.bn_stats(bn[0:ROW, j, h, :], PS[0:ROW, bank + h, :])
                own.up(ins)
                own.sync()
                own.up(dve.bn_aggr(mv[0:ROW, j, :], bn[0:ROW, j, :, :]))
                own.sync()
                dve.tensor_scalar(var[0:ROW, j:j + 1], mv[0:ROW, j, 1:2], EPS, None, ALU.add).then_inc(s_ve, 1)

            def ln_nmr(lnb, j):
                dve.wait_ge(s_std, lnb + (NB + j + 1))
                own.up(dve.reciprocal(rstd[0:ROW, j:j + 1], std[0:ROW, j:j + 1]))
                own.sync()
                dve.scalar_tensor_tensor(out=nmr[0:ROW, j:j + 1], in0=mv[0:ROW, j, 0:1], scalar=-1.0,
                                         in1=rstd[0:ROW, j:j + 1], op0=ALU.mult, op1=ALU.mult).then_inc(s_nmr, 1)

            def norm_task(lnb, d):
                if 0 < d <= NR:
                    ln_nmr(lnb, d - 1)
                if d < NR:
                    ln_var(lnb, d)

            def back_task(blk, d):
                if 5 <= d < 9:
                    back_lo(blk, NB * KT, lambda k: xr[:, k, :], lambda k: ah[:, k, :], lambda k: al[:, k, :], 2,
                            range(2 * d - 10, 2 * d - 8))

            def output(o, u, half):
                dst, ps = tile_of(acc, o), PS[:, u % 4, 0:BLK]
                if half == 0:
                    dve.scalar_tensor_tensor(out=dst, in0=tile_of(xr, o), scalar=ALPHA, in1=ps, op0=ALU.mult,
                                             op1=ALU.add).then_inc(s_fev, 1)
                else:
                    dve.tensor_tensor(dst, dst, ps, ALU.add).then_inc(s_fev, 1)

            def ffn_body(b, n):
                with dve.Fori(0, (HF - NN) // 4) as i:
                    for u in range(4):
                        lo_after(n + i * 4 + u, u % 2)
                        hidden_lo(b * FT + i * 4 + (NN + u), i * 4 + (NN + u), u)
                with dve.Fori(0, 2) as i:
                    for u in range(4):
                        for q in range(2):
                            lo_after(n + i * 8 + (SB_ + 2 * u + q), q)
                        output(i * 4 + u, u, 0)
                with dve.Fori(0, HF // 4) as i:
                    for u in range(4):
                        lo_after(n + i * 4 + (SC_ + u), u % 2)
                        hidden_lo(b * FT + i * 4 + (HF + u), i * 4 + u, u)
                dve.wait_ge(s_fev, b * (2 * KT) + (KT + 4))

            split_y(0)
            out_proj(0, 0)
            for d in range(9):
                norm_task(0, d)
                back_task(0, d)
            for a in range(NN):
                lo_after(KT + a, a % 2)
                hidden_lo(a, a, a)
            with own.loop(NB - 1, 24) as b:
                n = b * STEPS + PRO
                ffn_body(b, n)
                split_y(b + 1)
                for s in range(D1):
                    lo_after(n + (SD_ + s), s % 2)
                    if s % 2:
                        output(s // 2, s // 2, 1)
                out_proj(n + SE_, b + 1)
                for d in range(SN_ - SD2):
                    lo_after(n + (SD2 + d), d % 2)
                    if d % 2:
                        output((D1 + d) // 2, (D1 + d) // 2, 1)
                    norm_task(b * 8 + 4, d)
                    back_task(b + 1, d)
                for a in range(NN):
                    lo_after(n + (SN_ + a), a % 2)
                    hidden_lo(b * FT + (FT + a), a, a)
                    norm_task(b * 8 + 8, a)
            b, n = NB - 1, (NB - 1) * STEPS + PRO
            ffn_body(b, n)
            for o in range(KT):
                if o < KT - 1:
                    for q in range(2):
                        lo_after(n + (SD_ + 2 * o + q), q)
                else:
                    dve.wait_ge(s_step, TOTAL)
                output(o, o, 1)
            for d in range(NR + 1):
                norm_task(b * 8 + 4, d)

        @block.gpsimd
        def _(pool):
            own = Tally(pool, s_pool)
            with pool.Fori(0, 2) as hp:
                for n in range(2 * QT):
                    W = (n % QT + 1) * P
                    wait_apart(pool, s_sn, hp * 80 + groups_until(n + 1))
                    for t, fill in ((sP, 0.0), (nP, 1.0)):
                        diag = t[:, n % 2, W - P:W]
                        ins = pool.affine_select(out=diag, in_=diag, compare_op=ALU.is_gt, fill=fill, base=0,
                                                 pattern=[[-1, P]], channel_multiplier=1)
                    ins.then_inc(s_msk, 1)
            pool.wait_ge(s_const, CONST_ALL + 16)

            def store_rows(b, lnb):
                for j in range(NR):
                    pool.wait_ge(s_nat, lnb + (NATB + j + 1))
                    row = nat3[0:ROW, j, :]
                    own.op(pool.tensor_tensor(row, row, gb2[0:ROW, 0, :], ALU.mult))
                    pool.tensor_tensor(row, row, gb2[0:ROW, 1, :], ALU.add).then_inc(s_row, 1)
                    pool.wait_ge(s_row, b * NR + (j + 1))
                    pool.dma_start(y_out[bass.ds(b * BLK + j * ROW, ROW)], row).then_inc(s_out, 16)
                pool.wait_ge(s_out, b * (16 * NR) + 16 * NR)
                pool.sem_inc(s_rowfree, 1)

            with own.loop(NB - 1, NR) as b:
                store_rows(b, b * 8 + 8)
            store_rows(NB - 1, (NB - 1) * 8 + 4)


def _tiles(w, rows, cols):
    a = w.reshape(rows, KT, P, cols, P)
    return a.transpose(3, 0, 2, 1, 4).reshape(cols * rows, P, KT * P)


def _channels(a):
    a = np.moveaxis(a, -1, 0)
    return np.ascontiguousarray(a.reshape((2, P) + a.shape[1:]))


def kernel(**inputs):
    import concourse.bacc as bacc
    from concourse.bass_utils import run_bass_kernel_spmd

    f = {k: np.asarray(v) for k, v in inputs.items()}
    w_in = _tiles(f["w_in"][0], 1, NC_IN)[[2 * g + c for g, c in ORDER]]
    w_o, w_1 = _tiles(f["w_out"][0], 1, KT), _tiles(f["w_ff1"][0], 1, FT)
    w_2 = _tiles(f["w_ff2"][0], 4, KT).reshape(KT, 4, P, KT * P)
    w_2 = [w_2[:, 2 * h:2 * h + 2].reshape(HF, P, KT * P) for h in range(2)]
    iteration = [w_1[NN:HF], w_2[0], w_1[HF:], w_2[1][:D1], w_o, w_2[1][D1:], w_1[:NN]]
    w_all = np.concatenate([w_in, w_o, w_1[:NN]] + iteration)
    per_channel = [f["conv_a_w"][0].T, f["conv_a_b"][0][:, None], f["lru_ba"][0][:, None], f["lru_bx"][0][:, None],
                   f["lru_lambda"][0][:, None], f["conv_b_w"][0].T, f["pool_scale"][0][:, None],
                   np.repeat(np.float32(1.0) / np.array(WINDOWS, np.float32), HD)[:, None]]
    pvec = np.concatenate(per_channel, 1).reshape(2, P, NPV).transpose(1, 0, 2)
    lnp = np.stack([f[k].reshape(KT, P) for k in ("ln_in_g", "ln_in_b", "ln1_g", "ln1_b")]).transpose(2, 0, 1)
    rows2 = np.broadcast_to(np.stack([f["ln2_g"][0], f["ln2_b"][0]]), (P, 2, D))
    masks = np.zeros((P, DECT + 32), np.float32)
    masks[:, :DECT] = np.arange(DECT)[None] < (np.arange(P) % DECT)[:, None]
    for c in range(2):
        w = np.repeat(WINDOWS[2 * c:2 * c + 2], HD)[:, None]
        masks[:, DECT + 16 * c:DECT + 16 * c + 16] = 1.0 / np.minimum(w, np.arange(16)[None] + 1)
    n_pool = f["cache_k"].shape[1]
    arrays = {
        "x_all": np.concatenate([f["x_prompt"].reshape(SEQ, D), f["x_sample"].reshape(SMP, D)]),
        "w_all": w_all, "pvec": pvec, "lnp": lnp, "rows2": rows2,
        "gates_a": f["lru_wa"][0], "gates_x": f["lru_wx"][0], "poolw": f["pool_w"][0],
        "sbh": np.broadcast_to(f["sb_bias"][0], (P, NH)),
        "sbr": np.tile(np.repeat(f["sb_bias"][0], DECT), DECB)[:, None],
        "masks": masks, "ident_d": np.eye(P, dtype=np.float32),
        "ck": f["cache_k"].reshape(n_pool, PAGE, 2 * P), "cv": f["cache_v"].reshape(n_pool, PAGE, 2 * P),
        "ptab": f["page_table"].reshape(1, DECB * NPG),
        "st_h": _channels(f["state_rglru_h"][0]), "st_a": _channels(f["state_conv_a"][0]),
        "st_b": _channels(f["state_conv_b"][0]), "st_p": _channels(f["state_pool"][0]),
    }
    arrays = {k: np.ascontiguousarray(v) for k, v in arrays.items()}
    outs = {"y_out": (TOK, D), "kv_out": (4, P, TOK), "so_out": (P, 2, SO_N)}
    nc = bacc.Bacc("TRN2", target_bir_lowering=False, num_devices=1)
    args = [nc.dram_tensor(k, a.shape, mybir.dt.from_np(a.dtype), kind="ExternalInput").ap() for k, a in arrays.items()]
    args += [nc.dram_tensor(k, s, F32, kind="ExternalOutput").ap() for k, s in outs.items()]
    build(nc, *args)
    got = run_bass_kernel_spmd(nc, [arrays], core_ids=[0]).results[0]
    y, kv, so = got["y_out"], got["kv_out"], got["so_out"]
    kv = kv.reshape(2, 2 * P, TOK).transpose(0, 2, 1)

    def prompt(a):
        return np.ascontiguousarray(a[:SEQ].reshape(1, 1, SEQ, NH, HD))

    def sample(a):
        return np.ascontiguousarray(a[SEQ:].reshape(1, DECB, DECT, NH, HD))

    so = so.transpose(1, 0, 2).reshape(2 * P, SO_N).T

    def state(at, rows):
        return (np.ascontiguousarray(so[at:at + rows].reshape(1, 1, rows, 2 * P)),
                np.ascontiguousarray(so[at + rows:at + rows * (1 + DECB)].reshape(1, DECB, rows, 2 * P)))

    h_p, h_s = state(SO_H, 1)
    a_p, a_s = state(SO_A, BUFA)
    b_p, b_s = state(SO_B, BUFB)
    p_p, p_s = state(SO_P, BUFP)
    return (y[:SEQ].reshape(1, SEQ, D), y[SEQ:].reshape(DECB, DECT, D), prompt(kv[0]), prompt(kv[1]), sample(kv[0]), sample(kv[1]),
            h_p.reshape(1, 1, 2 * P), h_s.reshape(1, DECB, 2 * P), a_p, a_s, b_p, b_s, p_p, p_s)
```

```python
from contextlib import ExitStack, contextmanager

import numpy as np
import concourse.bass as bass
from concourse import mybir

F32 = mybir.dt.float32
F32R = mybir.dt.float32r
I32 = mybir.dt.int32
ACT = mybir.ActivationFunctionType
ALU = mybir.AluOpType

P = 128
D = 1024
KT = D // P
SEQ = 2048
DECB, DECT = 8, 4
SMP = DECB * DECT
TOK = SEQ + SMP
BLK = 416
NB = TOK // BLK
ROW = 104
NR = BLK // ROW
NC_IN = 18
FT = 32
HF = FT // 2
NN = 8
D1 = 4
PRO = KT + NN
SA_, SB_ = 0, HF - NN
SC_ = SB_ + HF
SD_ = SC_ + HF
SE_ = SD_ + D1
SD2 = SE_ + KT
SN_ = SD2 + HF - D1
STEPS = SN_ + NN
LAST = STEPS - KT - NN
TOTAL = PRO + (NB - 1) * STEPS + LAST
HD = 64
NH = 4
PAGE = 128
NPG = 16
PAST = NPG * PAGE
RING = 4
QT = SEQ // P
AHEAD = 2
ZB = 3
CHW = 512
ALPHA = 2.0 ** 0.25
EPS = 1e-5
RC = 8.0
BUFA, BUFB, BUFP = 3, 2, 15
WINDOWS = (2, 4, 8, 16)
BEHIND_PA = 6656
XA, GA, XB, GB, GC, Q, K, V, XP = range(9)
ORDER = [(g, c) for g in (XA, GA, XB, GC, GB, XP, K, V, Q) for c in (0, 1)]
AT = {gc: n for n, gc in enumerate(ORDER)}
K0 = AT[K, 0]
PCW, PCB, PBA, PBX, PLAM, PBW, PSC, PINV, NPV = 0, 4, 5, 6, 7, 8, 11, 12, 13
SO_H, SO_A, SO_B, SO_P = 0, 1 + DECB, 1 + DECB + BUFA * (1 + DECB), 1 + DECB + (BUFA + BUFB) * (1 + DECB)
SO_N = (1 + DECB) * (1 + BUFA + BUFB + BUFP)


NAT0 = NR
NATB = NAT0 + NR * NB
CONST_ALL = 16 * 18


def ext_of(tile, halo):
    a = SEQ + halo
    return tile[:, a:a + DECB * (halo + DECT)].rearrange("p (b t) -> p b t", b=DECB)


def new_of(tile):
    return tile[:, SEQ:TOK].rearrange("p (b t) -> p b t", b=DECB)


def tile_of(t, k):
    return t[:, bass.ds(k, 1), :].rearrange("p o t -> p (o t)")


def rev(ap):
    return ap[:, ::-1]


def groups_until(n):
    return sum(-(-(m % QT + 1) // 4) for m in range(n))


def build(nc, x_all, w_all, pvec, lnp, rows2, gates_a, gates_x, poolw, sbh, sbr, masks, ident_d, ck, cv, ptab,
          st_h, st_a, st_b, st_p, y_out, kv_out, so_out):
    ctx = ExitStack()
    with ctx:
        def sb(name, shape, dt=F32, stack=ctx):
            return stack.enter_context(nc.sbuf_tensor(name, shape, dt))

        def sem(name):
            return ctx.enter_context(nc.semaphore(name))

        proj_d = nc.dram_tensor("proj_scratch", (NC_IN, P, TOK), F32, kind="Internal").ap()
        x1_d = nc.dram_tensor("x1_scratch", (KT, P, TOK), F32, kind="Internal").ap()
        y_d = nc.dram_tensor("mixed_scratch", (KT, P, TOK), F32, kind="Internal").ap()
        vn_d = nc.dram_tensor("vnew_scratch", (SMP, 2 * P), F32, kind="Internal").ap()

        PS = ctx.enter_context(nc.psum_tensor("PS", [P, 8, 512], F32))

        ident = sb("ident", [P, P])
        raw = sb("w_raw", [P, 2, KT * P])
        wh = sb("w_hi", [P, 2, KT * P], F32R)
        wl = sb("w_lo", [P, 2, KT * P], F32R)
        pv = sb("pv", [P, 2, NPV])
        ln_gb = sb("ln_gb", [P, 4, KT])
        mask = sb("mask", [P, DECT + 32])
        hs = sb("hs", [P, 2, DECB])
        bias_h = sb("bias_h", [P, NH + 1])
        nbias_h = sb("nbias_h", [P, NH + 1])
        bn = sb("bn", [P, 4, 2, 6])
        mv = sb("mv", [P, 4, 2])
        var = sb("var", [P, 4])
        std = sb("std", [P, 4])
        rstd = sb("rstd", [P, 4])
        nmr = sb("nmr", [P, 4])
        gsel = sb("gsel", [P, 2, 3, P])
        lam = sb("lam", [P, 2, 8])
        so = sb("so", [P, 2, SO_N])

        with ExitStack() as e1:
            xh = sb("x_hi", [P, KT, TOK], F32R, e1)
            xl = sb("x_lo", [P, KT, TOK], F32R, e1)
            with ExitStack() as e:
                xin = sb("xin", [P, NR, D], F32, e)
                nat1 = sb("nat1", [P, NR, D], F32, e)
                t1 = sb("t1", [P, KT, BLK], F32, e)
            with ExitStack() as e:
                stage = sb("stage", [P, 2, TOK], F32, e)
        with ExitStack() as e2:
            vpg = sb("vpg", [P, RING, 4, 2 * P], F32, e2)
            vnew = sb("vnew", [DECT, 2, 2 * P], F32, e2)
            wtS = sb("wtS", [P, NPG, P], F32, e2)
            wtN = sb("wtN", [DECT, P], F32, e2)
            ycs = sb("ycs", [P, 2, SMP], F32, e2)
            ptb = sb("ptb", [1, DECB * NPG], I32, e2)
            with ExitStack() as e:
                MW = SEQ + BUFP + DECB * (BUFP + DECT)
                mx = [sb(f"mx{n}", [P, MW], F32, e) for n in range(8)]
                qbd = sb("qbd", [P, 2368], F32, e)
                kqs = sb("kqs", [P, 6, SMP], F32, e)
                kpg = sb("kpg", [P, RING, 4, 2 * P], F32, e)
                kts = sb("kts", [P, 2, 2, CHW], F32, e)
                vnat = sb("vnat", [SMP, 2 * P], F32, e)
                sS = sb("sS", [P, PAST + DECT], F32, e)
                nS = sb("nS", [P, PAST + DECT], F32, e)
                pS = sb("pS", [P, PAST + DECT + 1], F32, e)
            with ExitStack() as e:
                qT = sb("qT", [P, SEQ], F32, e)
                kT = sb("kT", [P, SEQ], F32, e)
                vN = sb("vN", [P, QT, P], F32, e)
                sP = sb("sP", [P, AHEAD + 1, SEQ], F32, e)
                nP = sb("nP", [P, AHEAD + 1, SEQ], F32, e)
                pP = sb("pP", [P, SEQ + 1], F32, e)
                wtP = sb("wtP", [P, 2, CHW], F32, e)
                ycT = sb("ycT", [P, SEQ], F32, e)
                vT = sP[:, AHEAD, :]
        with ExitStack() as e:
            hh = sb("h_hi", [P, HF, BLK], F32R, e)
            hl = sb("h_lo", [P, HF, BLK], F32R, e)
            acc = sb("mlp_sum", [P, KT, BLK], F32, e)
            nat3 = sb("nat3", [P, NR, D], F32, e)
            rbuf = sb("rbuf", [P, 2, BLK], F32, e)
            hf = sb("hf", [P, BLK], F32, e)
            gb2 = sb("gb2", [P, 2, D], F32, e)
            sb("behind_pa", [P, BEHIND_PA], F32, e)
            ah = sb("a_hi", [P, KT, BLK], F32R, e)
            al = sb("a_lo", [P, KT, BLK], F32R, e)
            xr = sb("x_residual", [P, KT, BLK], F32, e)
            yin = sb("y_block", [P, KT, BLK], F32, e)

        s_const = sem("const_in")
        s_raw = [sem("raw_in0"), sem("raw_in1")]
        s_wh, s_wl = sem("w_hi_made"), sem("w_lo_made")
        s_xin, s_t1st = sem("xin_in"), sem("x1_stored")
        s_ve, s_std, s_nmr = sem("var_made"), sem("std_made"), sem("nmr_made")
        s_nat = sem("tile_normalised")
        s_bt = sem("back_transposed")
        s_xh, s_xf, s_xl = sem("x_hi_made"), sem("x_full_made"), sem("x_lo_made")
        s_grp, s_ev1 = sem("proj_group_done"), sem("proj_evacuated")
        s_stg = [sem("stage_stored0"), sem("stage_stored1")]
        s_act, s_dve, s_pool = sem("act_own"), sem("dve_own"), sem("pool_own")
        s_mld = [sem("mix_loaded_a"), sem("mix_loaded_b"), sem("mix_loaded_d")]
        s_mzero = sem("mix_halo_zeroed")
        s_xc, s_gps, s_gev = sem("xc_made"), sem("gate_product_done"), sem("gate_evacuated")
        s_mxa, s_mxv = sem("mix_act_made"), sem("mix_dve_made")
        s_mst = [sem("ya_stored"), sem("yb_stored"), sem("yd_stored")]
        s_scan = sem("scan_done")
        s_lam = sem("lambda_step")
        s_mfree = sem("mix_tiles_free")
        s_qz, s_qbd, s_kqs = sem("qbd_zeroed"), sem("qbd_made"), sem("kqs_in")
        s_pt = sem("page_table_in")
        s_kin = [sem(f"k_pages_in{n}") for n in range(RING)]
        s_ktr, s_kte, s_kmm = sem("k_transposed"), sem("kT_evacuated"), sem("k_product_done")
        s_zs, s_sns, s_zn = sem("z_sample_done"), sem("sn_sample_made"), sem("z_new_done")
        s_ws, s_wtr, s_wte = sem("w_sample_made"), sem("w_sample_transposed"), sem("wT_sample_made")
        s_vin = [sem(f"v_pages_in{n}") for n in range(RING)]
        s_vuse, s_vnuse = sem("v_pages_used"), sem("v_new_used")
        s_vnin = [sem("v_new_in0"), sem("v_new_in1")]
        s_vnt, s_vnat, s_vnst = sem("v_new_transposed"), sem("v_new_natural"), sem("v_new_stored")
        s_yse, s_yst = sem("yc_sample_made"), sem("yc_stored")
        s_qkv, s_pair, s_vtr, s_vnp = sem("qkv_in"), sem("pair_done"), sem("v_transposed"), sem("v_natural")
        s_z, s_sn, s_msk, s_w = sem("z_done"), sem("sn_made"), sem("diag_masked"), sem("w_made")
        s_tr, s_wt, s_av, s_yc = sem("w_transposed"), sem("wT_made"), sem("av_group_done"), sem("yc_made")
        s_yc0, s_ycs = sem("yc_first_columns_stored"), sem("yc_prompt_stored")
        s_yin, s_x1in = sem("y_in"), sem("x1_in")
        s_yin0, s_x1in0 = sem("y_in_block0"), sem("x1_in_block0")
        s_yh, s_yl = sem("y_hi_made"), sem("y_lo_made")
        s_step, s_oev, s_ft = sem("step_done"), sem("outproj_evacuated"), sem("forward_transposed")
        s_r, s_hh, s_hf, s_hl = sem("relu_made"), sem("h_hi_made"), sem("h_full_made"), sem("h_lo_made")
        s_fev = sem("mlp_evacuated")
        s_row, s_out, s_so = sem("row_scaled"), sem("y_stored"), sem("state_stored")
        s_rowfree = sem("nat3_free")

        def wait_apart(eng, sem, value):
            eng.wait_ge(sem, value)
            eng.nop(nofuse=True)

        class Tally:

            def __init__(self, eng, sem):
                self.eng, self.sem, self.base, self.n = eng, sem, 0, 0

            def up(self, ins):
                ins.then_inc(self.sem, 1)
                self.n += 1

            def sync(self):
                wait_apart(self.eng, self.sem, self.base + self.n)

            def op(self, ins):
                self.up(ins)
                self.sync()

            @contextmanager
            def loop(self, count, per):
                base, n = self.base, self.n
                with self.eng.Fori(0, count) as i:
                    self.base, self.n = base + n + i * per, 0
                    yield i
                    assert self.n == per, (self.n, per)
                self.base, self.n = base, n + count * per

        def value_pages(eng, b, gs):
            for c in range(NPG // 4):
                ids = [eng.value_load(ptb[0:1, bass.ds(b * NPG + (c * 4 + g), 1)], min_val=0, max_val=cv.shape[0] - 1) for g in gs]
                eng.wait_ge(s_vuse, b * 4 + (c + 1))
                for g, page in zip(gs, ids):
                    eng.dma_start(vpg[:, c % RING, g, :], cv[bass.ds(page, 1)].rearrange("o p n -> p (o n)")).then_inc(
                        s_vin[c % RING], 16)

        block = ctx.enter_context(nc.Block())

        @block.sync
        def _(sp):
            n_const = [0]

            def const(dst, src):
                sp.dma_start(dst, src).then_inc(s_const, 16)
                n_const[0] += 16

            def load_raw(slot, tile):
                sp.dma_start(raw[:, slot, :], w_all[bass.ds(tile, 1)].rearrange("o p n -> p (o n)")).then_inc(
                    s_raw[slot], 16)

            sp.sem_inc(s_nat, NAT0)
            sp.sem_inc(s_vnuse, 2)
            sp.sem_inc(s_pair, 1)
            const(ident[:, :], ident_d)
            const(ln_gb[:, :, :], lnp)
            load_raw(0, 0)
            load_raw(1, 1)
            with sp.Fori(0, NB) as b:
                sp.wait_ge(s_nat, b * NR + NAT0)
                sp.dma_start(xin[0:ROW], x_all[bass.ds(b * BLK, BLK)].rearrange("(j p) d -> p j d", p=ROW)).then_inc(
                    s_xin, 16)
            const(pv[:, :, :], pvec)
            const(mask[:, :], masks)
            const(bias_h[:, 0:NH], sbh)
            const(bias_h[:, NH:NH + 1], sbr)
            sp.wait_ge(s_mzero, 1)
            for c in range(2):
                for n, src in enumerate((gates_a, gates_x, poolw)):
                    for h in range(2):
                        const(gsel[HD * h:HD * h + HD, c, n, HD * h:HD * h + HD], src[2 * c + h])
            assert n_const[0] == CONST_ALL

            def proj_steps(first, last, dst):
                with sp.Fori(first // 2, last // 2) as i:
                    for u in range(2):
                        sp.wait_ge(s_wl, i * 2 + (u + 1))
                        load_raw(u, i * 2 + (u + 2))
                        sp.wait_ge(s_ev1, i * 10 + (5 * u + 10))
                        sp.dma_start(dst[bass.ds(i * 2 + (u - (first if dst is kv_out else 0)), 1)].rearrange(
                            "o p t -> p (o t)"), stage[:, u, :]).then_inc(s_stg[u], 16)

            proj_steps(0, K0, proj_d)
            proj_steps(K0, K0 + 4, kv_out)
            proj_steps(K0 + 4, NC_IN, proj_d)
            for u in range(2):
                sp.wait_ge(s_stg[u], 16 * (NC_IN // 2) + 16)

            sp.dma_start(ptb[:, :], ptab).then_inc(s_pt, 16)
            for c in range(2):
                for n, (src, t) in enumerate(((proj_d, AT[Q, 0]), (kv_out, 0), (kv_out, 2))):
                    sp.dma_start(kqs[:, 2 * n + c, :], src[t + c, :, SEQ:TOK]).then_inc(s_kqs, 16)
            sp.wait_ge(s_pt, 16)
            with sp.Fori(0, NPG // 4) as c:
                for b in range(DECB):
                    ids = [sp.value_load(ptb[0:1, bass.ds(c * 4 + (b * NPG + g), 1)], min_val=0, max_val=ck.shape[0] - 1)
                           for g in range(4)]
                    sp.wait_ge(s_ktr, c * DECB + (b + 1))
                    for g in range(4):
                        sp.dma_start(kpg[:, b % RING, g, :], ck[bass.ds(ids[g], 1)].rearrange("o p n -> p (o n)")).then_inc(
                            s_kin[b % RING], 16)
            sp.wait_ge(s_vnat, 2)
            sp.dma_start(vn_d, vnat[:, :]).then_inc(s_vnst, 16)
            sp.wait_ge(s_vnst, 16)
            for m in s_mst:
                sp.wait_ge(m, 32)
            sp.wait_ge(s_so, 16)
            sp.wait_ge(s_wte, 5)

            with sp.Fori(0, 2) as hp:
                sp.wait_ge(s_pair, hp + 1)
                sp.dma_start(vT, kv_out[bass.ds(hp + 2, 1), :, 0:SEQ].rearrange("o p t -> p (o t)")).then_inc(s_qkv, 16)
                sp.dma_start(qT[:, :], proj_d[bass.ds(hp + AT[Q, 0], 1), :, 0:SEQ].rearrange("o p t -> p (o t)")).then_inc(s_qkv, 16)
                sp.dma_start(kT[:, :], kv_out[bass.ds(hp, 1), :, 0:SEQ].rearrange("o p t -> p (o t)")).then_inc(s_qkv, 16)
                with sp.Fori(0, DECB // 4) as i:
                    for u in range(2):
                        b = hp * (DECB // 2) + i * 2 + u
                        sp.wait_ge(s_vnuse, b + 1)
                        sp.dma_start(vnew[:, u, :], vn_d[bass.ds(b * DECT, DECT)]).then_inc(s_vnin[u], 16)
                        value_pages(sp, b, range(4))
                y_pair = y_d[bass.ds(hp + 4, 1)].rearrange("o p t -> p (o t)")
                sp.wait_ge(s_yc, hp * 32 + (QT + 4))
                sp.dma_start(y_pair[:, 0:CHW], ycT[:, 0:CHW]).then_inc(s_yc0, 16)
                sp.wait_ge(s_yc, hp * 32 + 32)
                sp.dma_start(y_pair[:, CHW:SEQ], ycT[:, CHW:SEQ]).then_inc(s_ycs, 16)
            sp.wait_ge(s_yse, 4)
            for c in range(2):
                sp.dma_start(y_d[4 + c, :, SEQ:TOK], ycs[:, c, :]).then_inc(s_yst, 16)

            sp.wait_ge(s_pair, 3)
            sp.wait_ge(s_ycs, 48)
            const(gb2[:, :, :], rows2)

            def load_step(n, tile, u):
                sp.wait_ge(s_wl, n + (NC_IN - 1))
                load_raw(u, tile)

            W0 = NC_IN + PRO
            with sp.Fori(1, PRO // 2) as i:
                for u in range(2):
                    load_step(i * 2 + u, i * 2 + (NC_IN + u), u)
            with sp.Fori(0, NB - 1) as b:
                with sp.Fori(0, STEPS // 2) as i:
                    for u in range(2):
                        load_step(b * STEPS + i * 2 + (PRO + u), i * 2 + (W0 + u), u)
            for first, count, skip in ((0, SE_, 0), (SE_, LAST - SE_, KT)):
                with sp.Fori(0, count // 2) as i:
                    for u in range(2):
                        load_step(i * 2 + (PRO + (NB - 1) * STEPS + first + u), i * 2 + (W0 + first + skip + u), u)
            sp.wait_ge(s_out, 16 * NR * NB)

        @block.tensor
        def _(pe):
            def back(b, base, nat, ks=range(KT)):
                for k in ks:
                    if k >= 4:
                        pe.wait_ge(s_xf, b * KT + (base + k - 3))
                    for j in range(NR):
                        ins = pe.transpose(PS[:, 4 + k % 4, j * ROW:(j + 1) * ROW], nat[0:ROW, j, k * P:(k + 1) * P],
                                           ident[0:ROW, 0:ROW])
                    ins.then_inc(s_bt, 1)

            def step(slot, out, moving, first, last):
                for k in range(KT):
                    mh, ml = moving(k)
                    w_h, w_l = wh[:, slot, k * P:(k + 1) * P], wl[:, slot, k * P:(k + 1) * P]
                    pe.matmul(out, w_h, mh, start=(first and k == 0), stop=False)
                    pe.matmul(out, w_h, ml, start=False, stop=False)
                    ins = pe.matmul(out, w_l, mh, start=False, stop=(last and k == KT - 1))
                return ins

            pe.wait_ge(s_const, 32)
            with pe.Fori(0, NB) as b:
                pe.wait_ge(s_nat, b * NR + (NAT0 + NR))
                back(b, 0, nat1)
            pe.wait_ge(s_xh, NB * KT)
            pe.wait_ge(s_xl, NB * KT)
            with pe.Fori(0, NC_IN // 2) as i:
                for u in range(2):
                    pe.wait_ge(s_wh, i * 2 + (u + 1))
                    pe.wait_ge(s_wl, i * 2 + (u + 1))
                    for b in range(NB):
                        pe.wait_ge(s_ev1, i * 10 + (5 * u + b + 1))
                        cols = slice(b * BLK, (b + 1) * BLK)
                        step(u, PS[:, b, 0:BLK], lambda k: (xh[:, k, cols], xl[:, k, cols]), True, True).then_inc(s_grp, 1)

            pe.wait_ge(s_const, CONST_ALL)
            pe.wait_ge(s_ev1, NB * NC_IN + NB)
            mixed = 0

            def mixer_product(c, what):
                nonlocal mixed
                pe.wait_ge(s_xc, 2 * c + (1 if what < 2 else 2))
                src = mx[2] if what < 2 else mx[5]
                for a in range(0, TOK, CHW):
                    w = min(CHW, TOK - a)
                    if mixed >= 2:
                        pe.wait_ge(s_gev, mixed - 1)
                    pe.matmul(PS[:, 6 + mixed % 2, 0:w], gsel[:, c, what, :], src[:, a:a + w], start=True, stop=True).then_inc(s_gps, 1)
                    mixed += 1

            def qsel(b, h):
                return qbd[:, (2 * b + h) * P:(2 * b + h + 1) * P]

            def keys(c):
                for b in range(DECB + 1):
                    if b < DECB:
                        pe.wait_ge(s_kin[b % RING], c * (64 * DECB // RING) + 64 * (b // RING + 1))
                        pe.wait_ge(s_kte, c * DECB + (b + 1))
                        for h in range(2):
                            for g in range(4):
                                ins = pe.transpose(PS[:, 2 * (b % 2) + h, g * P:(g + 1) * P],
                                                   kpg[:, b % RING, g, h * P:(h + 1) * P], ident[:, :])
                        ins.then_inc(s_ktr, 1)
                    if b >= 1:
                        d = b - 1
                        if d == 0:
                            pe.wait_ge(s_sns, c + 1)
                        pe.wait_ge(s_kte, c * DECB + (d + 3))
                        for h in range(2):
                            ins = pe.matmul(PS[:, 4, :], qsel(d, h), kts[:, d % 2, h, :],
                                            start=(d == 0 and h == 0), stop=(d == DECB - 1 and h == 1))
                        ins.then_inc(s_kmm, 1)

            pe.wait_ge(s_kqs, 96)
            for c in range(2):
                pe.transpose(PS[0:SMP, 6 + c, 0:P], kqs[:, 4 + c, :], ident[:, :]).then_inc(s_vnt, 1)
            pe.wait_ge(s_qbd, 4)
            pe.sem_inc(s_ktr, RING)
            pe.sem_inc(s_vuse, RING)
            pe.sem_inc(s_kmm, 2)
            pe.sem_inc(s_sns, 1)
            for b in range(DECB):
                for h in range(2):
                    ins = pe.matmul(PS[:, 5, 0:DECT], qsel(b, h), kqs[:, 2 + h, b * DECT:(b + 1) * DECT],
                                    start=(b == 0 and h == 0), stop=(b == DECB - 1 and h == 1))
            ins.then_inc(s_zn, 1)
            pe.wait_ge(s_vnat, 2)
            for what in (0, 1):
                mixer_product(0, what)
            with pe.Fori(0, 2) as c:
                keys(c)
            mixer_product(0, 2)
            keys(2)
            for what in (0, 1):
                mixer_product(1, what)
            keys(3)
            pe.wait_ge(s_ws, 1)
            for g in range(4):
                for j in range(4):
                    t = 4 * g + j
                    ins = pe.transpose(PS[:, g, j * P:(j + 1) * P], sS[:, t * P:(t + 1) * P], ident[:, :])
                ins.then_inc(s_wtr, 1)
            pe.wait_ge(s_sns, 6)
            pe.transpose(PS[0:DECT, 5, 0:P], sS[:, PAST:PAST + DECT], ident[:, :]).then_inc(s_wtr, 1)
            pe.wait_ge(s_wte, 5)
            mixer_product(1, 2)
            pe.wait_ge(s_gev, mixed)

            def sample_values(hp, m):
                k, c = divmod(m, 4)
                out = lambda h: PS[:, ZB, bass.ds(hp * 32 + (64 * h + 8 * k), 8)]
                col = lambda h: bass.ds(hp * 64 + (16 * k + 8 * h), 8)
                pe.wait_ge(s_vin[c], hp * 256 + 64 * (k + 1))
                for g in range(4):
                    for h in range(2):
                        ins = pe.matmul(out(h), vpg[:, c, g, h * P:(h + 1) * P], wtS[:, 4 * c + g, col(h)],
                                        start=(c == 0 and g == 0 and h == 0), stop=False)
                ins.then_inc(s_vuse, 1)
                if c == 3:
                    pe.wait_ge(s_vnin[k % 2], hp * 32 + 16 * (k // 2 + 1))
                    for h in range(2):
                        ins = pe.matmul(out(h), vnew[:, k % 2, h * P:(h + 1) * P], wtN[:, col(h)], start=False, stop=(h == 1))
                    ins.then_inc(s_vnuse, 1)

            with pe.Fori(0, 2) as hp:
                pe.wait_ge(s_qkv, hp * 48 + 48)
                for g in range(4):
                    for j in range(4):
                        t = 4 * g + j
                        ins = pe.transpose(PS[:, 4 + g, j * P:(j + 1) * P], vT[:, t * P:(t + 1) * P], ident[:, :])
                    ins.then_inc(s_vtr, 1)
                pe.wait_ge(s_vnp, hp * 4 + 4)
                cc = tg = 0

                def chunks(n):
                    W = (n % QT + 1) * P
                    return [(a, min(CHW, W - a)) for a in range(0, W, CHW)] if n < 2 * QT else []

                def scores(n, a, w):
                    nonlocal cc
                    hl_, qt = divmod(n, QT)
                    rows = slice(HD * hl_, HD * hl_ + HD)
                    if cc >= ZB:
                        pe.wait_ge(s_sn, hp * 80 + (cc - ZB + 1))
                    pe.matmul(PS[:, cc % ZB, 0:w], qT[rows, qt * P:(qt + 1) * P], kT[rows, a:a + w],
                              start=True, stop=True).then_inc(s_z, 1)
                    cc += 1

                for n in range(AHEAD):
                    for a, w in chunks(n):
                        scores(n, a, w)
                for n in range(2 * QT):
                    hl_, qt = divmod(n, QT)
                    pe.wait_ge(s_w, hp * 32 + (n + 2))
                    if n >= 2:
                        pe.wait_ge(s_yc, hp * 32 + (n - 1))
                    groups = [list(range(a, min(a + 4, qt + 1))) for a in range(0, qt + 1, 4)]
                    ahead = chunks(n + AHEAD)

                    def values(g, at):
                        pe.wait_ge(s_wt, hp * 80 + (at + 1))
                        for j, t in enumerate(groups[g]):
                            ins = pe.matmul(PS[HD * hl_:HD * hl_ + HD, 6 + n % 2, 0:P], vN[:, t, HD * hl_:HD * hl_ + HD],
                                            wtP[:, at % 2, j * P:(j + 1) * P], start=(t == 0), stop=(t == qt))
                        ins.then_inc(s_av, 1)

                    for g in range(max(len(groups), len(ahead))):
                        if g < len(groups):
                            if tg >= 2:
                                pe.wait_ge(s_wt, hp * 80 + (tg - 1))
                            for j, t in enumerate(groups[g]):
                                ins = pe.transpose(PS[:, 4 + tg % 2, j * P:(j + 1) * P], sP[:, n % (AHEAD + 1), t * P:(t + 1) * P],
                                                   ident[:, :])
                            ins.then_inc(s_tr, 1)
                            tg += 1
                        if g < len(ahead):
                            scores(n + AHEAD, *ahead[g])
                        if 0 < g < len(groups):
                            values(g - 1, tg - 2)
                    if n % 2 == 0:
                        sample_values(hp, n // 2)
                    values(len(groups) - 1, tg - 1)
                pe.wait_ge(s_yc, hp * 32 + 32)
                pe.sem_inc(s_pair, 1)

            def weights(n):
                pe.wait_ge(s_wh, n + (NC_IN + 1))
                pe.wait_ge(s_wl, n + (NC_IN + 1))

            a_parts = lambda k: (ah[:, k, :], al[:, k, :])

            def out_proj(n, blk, before_first):
                pe.wait_ge(s_yh, blk * 2 + 2)
                pe.wait_ge(s_yl, blk * 2 + 2)
                for s in range(KT):
                    weights(n + s)
                    if s < 4:
                        before_first(s)
                    else:
                        pe.wait_ge(s_oev, blk * KT + (s - 3))
                    step(s % 2, PS[:, s % 4, 0:BLK], a_parts, True, True).then_inc(s_step, 1)

            def ffn1(n, f, u):
                weights(n)
                pe.wait_ge(s_r, f + 1)
                step(u % 2, PS[:, u % 4, 0:BLK], a_parts, True, True).then_inc(s_step, 1)

            def ffn2(n, o, h, u, free, before=lambda q: None):
                for q in range(2):
                    before(q)
                    weights(n + q)
                    pe.wait_ge(s_hh, h + KT * (q + 1))
                    pe.wait_ge(s_hl, h + (KT * (q + 1) + 1))
                    if q == 0:
                        pe.wait_ge(s_fev, o + 1)
                        free()
                    step(q, PS[:, u % 4, 0:BLK], lambda k: (hh[:, KT * q + k, :], hl[:, KT * q + k, :]),
                         q == 0, q == 1).then_inc(s_step, 1)

            def forward(src, lnb, j):
                pe.wait_ge(s_nat, lnb + (NATB + j - 1))
                for k in range(KT):
                    bank = 4 + 2 * (j % 2) + k // 4
                    ins = pe.transpose(PS[0:ROW, bank, (k % 4) * P:(k % 4 + 1) * P], src[:, k, j * ROW:(j + 1) * ROW], ident[:, :])
                ins.then_inc(s_ft, 1)

            def back1(blk, lnb, q):
                if q == 0:
                    pe.wait_ge(s_nat, lnb + (NATB + NR))
                back(blk, NB * KT, nat3, range(2 * q, 2 * q + 2))

            def split_x1(blk):
                pe.wait_ge(s_xh, blk * KT + (NB * KT + KT))
                wait_apart(pe, s_xl, blk * KT + (NB * KT + KT))

            def ffn_body(b, n):
                with pe.Fori(0, (HF - NN) // 4) as i:
                    for u in range(4):
                        ffn1(n + i * 4 + u, b * FT + i * 4 + (NN + u), u)
                with pe.Fori(0, 2) as i:
                    for u in range(4):
                        ffn2(n + i * 8 + (SB_ + 2 * u), b * (2 * KT) + i * 4 + u, b * FT, u,
                             lambda: pe.wait_ge(s_r, b * FT + (HF + u + 1)))
                with pe.Fori(0, HF // 4) as i:
                    for u in range(4):
                        pe.wait_ge(s_fev, b * (2 * KT) + (KT + u + 1))
                        ffn1(n + i * 4 + (SC_ + u), b * FT + i * 4 + (HF + u), u)

            def iteration_tail(b, n):
                ln1, ln2 = b * 8 + 4, b * 8 + 8

                def output(o, free, before=lambda q: None):
                    at = SD_ if o < D1 // 2 else SD2 - D1
                    ffn2(n + (at + 2 * o), b * (2 * KT) + (KT + o), b * FT + HF, o, free, before)

                for o in range(D1 // 2):
                    output(o, lambda: pe.wait_ge(s_r, b * FT + (FT + o + 1)))

                def bank_free(s):
                    if s < D1 // 2:
                        pe.wait_ge(s_fev, b * (2 * KT) + (KT + s + 5))
                    else:
                        pe.wait_ge(s_r, b * FT + (FT + s + 1))

                out_proj(n + SE_, b + 1, bank_free)

                def norm1(d):
                    if d == 1:
                        pe.wait_ge(s_oev, b * KT + 2 * KT)
                    if 1 <= d <= NR:
                        forward(xr, ln1, d - 1)
                    if 6 <= d < 10:
                        back1(b + 1, ln1, d - 6)

                for o in range(D1 // 2, KT):
                    output(o, lambda: pe.wait_ge(s_oev, b * KT + (KT + min(o + 5, KT))),
                           lambda q: norm1(2 * o - D1 + q))
                split_x1(b + 1)
                for a in range(NN):
                    if a == 1:
                        pe.wait_ge(s_fev, b * (2 * KT) + (2 * KT + 4))
                    if 1 <= a <= NR:
                        forward(acc, ln2, a - 1)
                    if a < 4:
                        pe.wait_ge(s_fev, b * (2 * KT) + (KT + a + 9))
                    ffn1(n + (SN_ + a), b * FT + (FT + a), a)

            pe.wait_ge(s_yse, 4)
            out_proj(0, 0, lambda s: None)
            pe.wait_ge(s_oev, KT)
            for j in range(NR):
                forward(xr, 0, j)
            for q in range(4):
                back1(0, 0, q)
            split_x1(0)
            for a in range(NN):
                ffn1(KT + a, a, a)
            with pe.Fori(0, NB - 1) as b:
                n = b * STEPS + PRO
                ffn_body(b, n)
                iteration_tail(b, n)
            b, n = NB - 1, (NB - 1) * STEPS + PRO
            ffn_body(b, n)
            with pe.Fori(0, 2) as i:
                for u in range(4):
                    ffn2(n + (SD_ + 2 * u) + i * 8, b * (2 * KT) + KT + u + i * 4, b * FT + HF, u,
                         lambda: pe.wait_ge(s_r, b * FT + (FT + u + 1)))
            pe.wait_ge(s_fev, NB * 2 * KT + 4)
            for j in range(NR):
                forward(acc, 8 * b + 4, j)

        @block.scalar
        def _(act):
            own = Tally(act, s_act)

            def split_hi(slot, uses):
                act.wait_ge(s_raw[slot], uses * 16)
                act.activation(wh[:, slot, :], raw[:, slot, :], ACT.Copy).then_inc(s_wh, 1)

            def norm(src, dst, j, col):
                act.activation(dst, src, ACT.Identity, bias=nmr[0:ROW, col:col + 1], scale=rstd[0:ROW, col:col + 1]).then_inc(s_nat, 1)

            def back_hi(b, base, full, hi, ks=range(KT)):
                for k in ks:
                    wait_apart(act, s_xf, b * KT + (base + k + 1))
                    act.activation(hi(k), full[:, k, :], ACT.Copy).then_inc(s_xh, 1)

            act.wait_ge(s_const, 32)
            split_hi(0, 1)
            split_hi(1, 1)
            with act.Fori(0, NB) as b:
                act.wait_ge(s_ve, b + 1)
                act.activation(std[0:ROW, :], var[0:ROW, :], ACT.Sqrt).then_inc(s_std, 1)
                act.wait_ge(s_nmr, b + 1)
                for j in range(NR):
                    norm(xin[0:ROW, j, :], nat1[0:ROW, j, :], j, j)
                back_hi(b, 0, t1, lambda k: xh[:, k, bass.ds(b * BLK, BLK)])
                act.wait_ge(s_xf, b * KT + KT)
                act.dma_start(x1_d[:, :, bass.ds(b * BLK, BLK)].rearrange("k p t -> p k t"), t1[:, :, :]).then_inc(s_t1st, 16)
            act.sem_inc(s_ev1, 5)
            act.sem_inc(s_stg[0], 16)
            act.sem_inc(s_stg[1], 16)
            act.wait_ge(s_t1st, 16 * NB + 16)
            with act.Fori(0, NC_IN // 2) as i:
                for u in range(2):
                    act.wait_ge(s_stg[u], i * 16 + 16)
                    for b in range(NB):
                        act.wait_ge(s_grp, i * 10 + (5 * u + b + 1))
                        act.activation(stage[:, u, b * BLK:(b + 1) * BLK], PS[:, b, 0:BLK], ACT.Copy).then_inc(s_ev1, 1)
                    split_hi(u, i + 2)

            def gates(n0, c, dst, func, bias, scale=1.0):
                n = n0
                for a in range(0, TOK, CHW):
                    w = min(CHW, TOK - a)
                    act.wait_ge(s_gps, n + 1)
                    act.activation(dst[:, a:a + w], PS[:, 6 + n % 2, 0:w], func, bias=bias, scale=scale).then_inc(s_gev, 1)
                    n += 1
                return n

            act.wait_ge(s_vnt, 2)
            for c in range(2):
                act.activation(vnat[:, c * P:(c + 1) * P], PS[0:SMP, 6 + c, 0:P], ACT.Copy).then_inc(s_vnat, 1)
            act.sem_inc(s_kte, 2)
            n = 0
            act.wait_ge(s_const, CONST_ALL)
            act.wait_ge(s_lam, 1)
            own.up(act.activation(lam[:, :, 1], lam[:, :, 0], ACT.Exp, scale=-1.0))
            act.wait_ge(s_lam, 2)
            own.up(act.activation(lam[:, :, 3], lam[:, :, 2], ACT.Ln))

            def lru_gates(c):
                nonlocal n
                act.wait_ge(s_lam, 3)
                act.wait_ge(s_mst[1], 16 * c)
                n = gates(n, c, mx[3], ACT.Sigmoid, pv[:, c, PBA:PBA + 1])
                n = gates(n, c, mx[4], ACT.Sigmoid, pv[:, c, PBX:PBX + 1])
                act.wait_ge(s_gev, n)
                own.up(act.activation(mx[3][:, 0:TOK], mx[3][:, 0:TOK], ACT.Tanh, scale=lam[:, c, 7:8]))
                own.sync()
                own.up(act.activation(mx[5][:, 0:TOK], mx[3][:, 0:TOK], ACT.Sqrt))
                act.wait_ge(s_mld[0], (c + 1) * 96)
                own.up(act.activation(mx[1][:, 0:TOK], mx[1][:, 0:TOK], ACT.Gelu_apprx_tanh))

            def pooled(c):
                nonlocal n
                act.wait_ge(s_mst[0], 16 * (c + 1))
                n = gates(n, c, mx[6], ACT.Copy, 0.0, pv[:, c, PSC:PSC + 1])
                act.wait_ge(s_gev, n)
                act.sem_inc(s_mxa, 1)

            def new_scores():
                act.wait_ge(s_zn, 1)
                act.activation(sS[:, PAST:PAST + DECT], PS[:, 5, 0:DECT], ACT.Sigmoid, bias=bias_h[:, NH:NH + 1], scale=HD ** -0.5)
                act.activation(nS[:, PAST:PAST + DECT], PS[:, 5, 0:DECT], ACT.Sigmoid, bias=nbias_h[:, NH:NH + 1],
                               scale=-HD ** -0.5).then_inc(s_sns, 1)

            def keys(c):
                for b in range(DECB):
                    act.wait_ge(s_ktr, c * DECB + (b + RING + 1))
                    act.wait_ge(s_kmm, c * DECB + (b + 1))
                    act.activation(kts[:, b % 2, :, :], PS[:, 2 * (b % 2):2 * (b % 2) + 2, :], ACT.Copy).then_inc(s_kte, 1)
                wait_apart(act, s_kmm, c * DECB + (DECB + 2))
                own_c = bass.ds(c * CHW, CHW)
                act.activation(sS[:, own_c], PS[:, 4, :], ACT.Sigmoid, bias=bias_h[:, NH:NH + 1], scale=HD ** -0.5)
                act.activation(nS[:, own_c], PS[:, 4, :], ACT.Sigmoid, bias=nbias_h[:, NH:NH + 1], scale=-HD ** -0.5).then_inc(s_sns, 1)

            lru_gates(0)
            with act.Fori(0, 2) as c:
                keys(c)
            pooled(0)
            keys(2)
            lru_gates(1)
            keys(3)
            new_scores()
            for g in range(4):
                act.wait_ge(s_wtr, g + 1)
                act.activation(wtS[:, 4 * g:4 * g + 4, :].rearrange("p a b -> p (a b)"), PS[:, g, :], ACT.Copy).then_inc(s_wte, 1)
            act.wait_ge(s_wtr, 5)
            act.activation(wtN[:, :], PS[0:DECT, 5, 0:P], ACT.Copy).then_inc(s_wte, 1)
            pooled(1)

            with act.Fori(0, 2) as hp:
                for g in range(4):
                    act.wait_ge(s_vtr, hp * 4 + (g + 1))
                    act.activation(vN[:, 4 * g:4 * g + 4, :].rearrange("p a b -> p (a b)"), PS[:, 4 + g, :], ACT.Copy).then_inc(s_vnp, 1)
                cc = tg = 0

                def chunks(n):
                    W = (n % QT + 1) * P
                    return [(a, min(CHW, W - a)) for a in range(0, W, CHW)] if n < 2 * QT else []

                def sig(n, a, w):
                    nonlocal cc
                    if n > AHEAD and a == 0:
                        act.wait_ge(s_tr, hp * 80 + groups_until(n - AHEAD))
                    wait_apart(act, s_z, hp * 80 + (cc + 1))
                    act.activation(sP[:, n % (AHEAD + 1), a:a + w], PS[:, cc % ZB, 0:w], ACT.Sigmoid, scale=HD ** -0.5,
                                   bias=bias_h[:, bass.ds(hp * 2 + n // QT, 1)])
                    act.activation(nP[:, n % (AHEAD + 1), a:a + w], PS[:, cc % ZB, 0:w], ACT.Sigmoid, scale=-HD ** -0.5,
                                   bias=nbias_h[:, bass.ds(hp * 2 + n // QT, 1)]).then_inc(s_sn, 1)
                    cc += 1

                for n in range(AHEAD):
                    for a, w in chunks(n):
                        sig(n, a, w)
                for n in range(2 * QT):
                    qt = n % QT
                    ahead = chunks(n + AHEAD)
                    for g in range(max(qt // 4 + 1, len(ahead))):
                        if g <= qt // 4:
                            w = min(4, qt + 1 - 4 * g) * P
                            act.wait_ge(s_tr, hp * 80 + (tg + 1))
                            if tg >= 2:
                                act.wait_ge(s_av, hp * 80 + (tg - 1))
                            act.activation(wtP[:, tg % 2, 0:w], PS[:, 4 + tg % 2, 0:w], ACT.Copy).then_inc(s_wt, 1)
                            tg += 1
                        if g < len(ahead):
                            sig(n + AHEAD, *ahead[g])

            act.sem_inc(s_r, 4)
            act.sem_inc(s_rowfree, 1)

            def hi_after(n, u):
                act.wait_ge(s_step, n + 1)
                act.wait_ge(s_raw[u], n * 8 + (NC_IN + 4 - u) * 8)
                act.activation(wh[:, u, :], raw[:, u, :], ACT.Copy).then_inc(s_wh, 1)

            def cols(blk):
                return bass.ds(blk * BLK, BLK)

            def load_y(blk):
                act.dma_start(yin[:, :, :], y_d[:, :, cols(blk)].rearrange("k p t -> p k t")).then_inc(s_yin, 16)

            def load_x1(blk):
                act.dma_start(xr[:, :, :], x1_d[:, :, cols(blk)].rearrange("k p t -> p k t")).then_inc(s_x1in, 16)

            def split_y(blk):
                for g in range(2):
                    act.activation(ah[:, 4 * g:4 * g + 4, :], yin[:, 4 * g:4 * g + 4, :], ACT.Copy).then_inc(s_yh, 1)

            def ln_std(lnb, j):
                act.wait_ge(s_ve, lnb + (NB + j + 1))
                act.activation(std[0:ROW, j:j + 1], var[0:ROW, j:j + 1], ACT.Sqrt).then_inc(s_std, 1)

            def ln_norm(lnb, j):
                act.wait_ge(s_nmr, lnb + (NB + j + 1))
                bank = 4 + 2 * (j % 2)
                norm(PS[0:ROW, bank:bank + 2, :].rearrange("p a b -> p (a b)"), nat3[0:ROW, j, :], j, j)

            def hidden_hi(f, at, u):
                act.wait_ge(s_hf, f + 1)
                act.activation(rbuf[:, u % 2, :], PS[:, u % 4, 0:BLK], ACT.Relu).then_inc(s_r, 1)
                wait_apart(act, s_r, f + 5)
                act.activation(tile_of(hh, at), rbuf[:, u % 2, :], ACT.Square).then_inc(s_hh, 1)

            def back_hi1(blk, q):
                back_hi(blk, NB * KT, xr, lambda k: ah[:, k, :], range(2 * q, 2 * q + 2))

            def norm1_task(blk, lnb, d):
                if 0 < d <= NR:
                    ln_norm(lnb, d - 1)
                if d < NR:
                    ln_std(lnb, d)
                if 5 <= d < 9:
                    back_hi1(blk, d - 5)

            act.wait_ge(s_yin0, 16)
            split_y(0)
            act.wait_ge(s_pair, 3)
            act.wait_ge(s_ycs, 48)
            act.wait_ge(s_yst, 32)
            for m in s_mst:
                act.wait_ge(m, 32)
            for s in range(KT):
                hi_after(s, s % 2)
            for d in range(9):
                norm1_task(0, 0, d)
            for a in range(NN):
                hi_after(KT + a, a % 2)
                hidden_hi(a, a, a)

            def ffn_body(b, n):
                with act.Fori(0, (HF - NN) // 4) as i:
                    for u in range(4):
                        hi_after(n + i * 4 + u, u % 2)
                        hidden_hi(b * FT + i * 4 + (NN + u), i * 4 + (NN + u), u)
                with act.Fori(0, HF // 4) as i:
                    for u in range(4):
                        hi_after(n + i * 4 + (SB_ + u), u % 2)
                yield
                with act.Fori(0, HF // 4) as i:
                    for u in range(4):
                        hi_after(n + i * 4 + (SC_ + u), u % 2)
                        hidden_hi(b * FT + i * 4 + (HF + u), i * 4 + u, u)

            with act.Fori(0, NB - 1) as b:
                n = b * STEPS + PRO
                act.wait_ge(s_yl, b * 2 + 2)
                load_y(b + 1)
                part = ffn_body(b, n)
                next(part)
                act.wait_ge(s_fev, b * (2 * KT) + (KT + 4))
                load_x1(b + 1)
                next(part, None)
                act.wait_ge(s_yin, b * 16 + 16)
                split_y(b + 1)
                for s in range(SD_, SD2):
                    hi_after(n + s, s % 2)
                for d in range(SN_ - SD2):
                    hi_after(n + (SD2 + d), d % 2)
                    if d == 1:
                        act.wait_ge(s_rowfree, b + 1)
                    norm1_task(b + 1, b * 8 + 4, d)
                for a in range(NN):
                    hi_after(n + (SN_ + a), a % 2)
                    hidden_hi(b * FT + (FT + a), a, a)
                    if 0 < a <= NR:
                        ln_norm(b * 8 + 8, a - 1)
                    if a < NR:
                        ln_std(b * 8 + 8, a)
            b, n = NB - 1, (NB - 1) * STEPS + PRO
            for _ in ffn_body(b, n):
                pass
            with act.Fori(0, (HF - 2) // 2) as i:
                for u in range(2):
                    hi_after(n + i * 2 + (SD_ + u), u)
            act.wait_ge(s_rowfree, NB)
            for j in range(NR + 1):
                if j:
                    ln_norm(b * 8 + 4, j - 1)
                if j < NR:
                    ln_std(b * 8 + 4, j)

        @block.vector
        def _(dve):
            own = Tally(dve, s_dve)

            def split_lo(slot, n_hi):
                dve.wait_ge(s_wh, n_hi)
                dve.tensor_tensor(wl[:, slot, :], raw[:, slot, :], wh[:, slot, :].bitcast(F32), ALU.subtract).then_inc(s_wl, 1)

            def moments(srcs, width, seq):
                for j, src in enumerate(srcs):
                    for h in range(2):
                        ins = dve.bn_stats(bn[0:ROW, j, h, :], src[:, h * 512:(h + 1) * 512])
                own.up(ins)
                own.sync()
                for j in range(width):
                    ins = dve.bn_aggr(mv[0:ROW, j, :], bn[0:ROW, j, :, :])
                own.up(ins)
                own.sync()
                dve.tensor_scalar(var[0:ROW, 0:width], mv[0:ROW, 0:width, 1], EPS, None, ALU.add).then_inc(s_ve, 1)
                dve.wait_ge(s_std, seq + 1)
                own.up(dve.reciprocal(rstd[0:ROW, 0:width], std[0:ROW, 0:width]))
                own.sync()
                dve.scalar_tensor_tensor(out=nmr[0:ROW, 0:width], in0=mv[0:ROW, 0:width, 0], scalar=-1.0,
                                         in1=rstd[0:ROW, 0:width], op0=ALU.mult, op1=ALU.mult).then_inc(s_nmr, 1)

            def back_lo(b, base, full, hi, lo, which, ks=range(KT)):
                ks = list(ks)
                for n in range(len(ks) + 1):
                    if n < len(ks):
                        k = ks[n]
                        dve.wait_ge(s_bt, b * KT + (base + k + 1))
                        dve.tensor_scalar(full(k), PS[:, 4 + k % 4, 0:BLK], ln_gb[:, which, k:k + 1], ln_gb[:, which + 1, k:k + 1],
                                          ALU.mult, ALU.add).then_inc(s_xf, 1)
                    if n:
                        k = ks[n - 1]
                        dve.wait_ge(s_xf, b * KT + (base + k + 1))
                        dve.wait_ge(s_xh, b * KT + (base + k + 1))
                        dve.tensor_tensor(lo(k), full(k), hi(k).bitcast(F32), ALU.subtract).then_inc(s_xl, 1)

            dve.memset(gsel[:, :, :, :], 0.0).then_inc(s_mzero, 1)
            dve.sem_inc(s_t1st, 16)
            dve.wait_ge(s_const, 32)
            split_lo(0, 1)
            split_lo(1, 2)
            with own.loop(NB, 3) as b:
                dve.wait_ge(s_xin, b * 16 + 16)
                moments([xin[0:ROW, j, :] for j in range(NR)], NR, b)
                dve.wait_ge(s_t1st, b * 16 + 16)
                cols = bass.ds(b * BLK, BLK)
                back_lo(b, 0, lambda k: t1[:, k, :], lambda k: xh[:, k, cols], lambda k: xl[:, k, cols], 0)
            with dve.Fori(0, NC_IN // 2) as i:
                for u in range(2):
                    dve.wait_ge(s_grp, i * 10 + (5 * u + 5))
                    split_lo(u, i * 2 + (u + 3))

            def op(ins):
                own.up(ins)
                own.sync()

            def conv(dst, src, c, col, taps, halo, bias):
                ext = ext_of(src, halo)
                dst_s = dst[:, SEQ:TOK].rearrange("p (b t) -> p b t", b=DECB)
                for j in range(taps):
                    for d_, s_ in ((dst[:, 0:SEQ], src[:, j:j + SEQ]), (dst_s, ext[:, :, j:j + DECT])):
                        if j == 0:
                            own.up(dve.tensor_scalar(d_, s_, pv[:, c, col:col + 1], bias, ALU.mult, ALU.add))
                        else:
                            own.up(dve.scalar_tensor_tensor(out=d_, in0=s_, scalar=pv[:, c, col + j:col + j + 1], in1=d_,
                                                            op0=ALU.mult, op1=ALU.add))
                    own.sync()

            dve.wait_ge(s_const, CONST_ALL)
            op(dve.tensor_scalar(nbias_h[:, :], bias_h[:, :], -1.0, None, ALU.mult))
            L = lambda n: lam[:, :, n]
            lamv = pv[:, :, PLAM]
            op(dve.tensor_scalar(L(4), lamv, -1.0, None, ALU.mult))
            dve.tensor_tensor(L(0), lamv, L(4), ALU.max).then_inc(s_lam, 1)
            dve.wait_ge(s_act, 1)
            dve.tensor_scalar(L(2), L(1), 1.0, None, ALU.add).then_inc(s_lam, 1)
            dve.wait_ge(s_lam, 2)
            op(dve.tensor_scalar(L(5), L(2), -1.0, None, ALU.add))
            op(dve.tensor_scalar(L(6), L(5), 0.0, None, ALU.is_equal))
            op(dve.tensor_tensor(L(5), L(5), L(6), ALU.add))
            op(dve.reciprocal(L(5), L(5)))
            dve.wait_ge(s_act, 2)
            op(dve.tensor_tensor(L(5), L(5), L(3), ALU.mult))
            op(dve.tensor_tensor(L(5), L(5), L(6), ALU.add))
            op(dve.tensor_tensor(L(5), L(5), L(1), ALU.mult))
            op(dve.scalar_tensor_tensor(out=L(5), in0=L(4), scalar=0.0, in1=L(5), op0=ALU.max, op1=ALU.add))
            dve.tensor_scalar(L(7), L(5), RC / 2, None, ALU.mult).then_inc(s_lam, 1)

            op(dve.memset(qbd[:, :], 0.0))
            dve.wait_ge(s_kqs, 96)
            for h in range(NH):
                rows = slice(HD * (h % 2), HD * (h % 2) + HD)
                a = (h // 2) * P + h * DECT
                dst = qbd[rows, a:a + DECB * 272].rearrange("p (b s) -> p b s", s=272)[:, :, 0:DECT]
                dve.tensor_copy(dst, kqs[rows, h // 2, :].rearrange("p (b t) -> p b t", b=DECB)).then_inc(s_qbd, 1)

            def sample_weights():
                dve.wait_ge(s_sns, 6)
                new = slice(PAST, PAST + DECT)
                own.up(dve.tensor_tensor(sS[:, new], sS[:, new], mask[:, 0:DECT], ALU.mult))
                op(dve.scalar_tensor_tensor(out=nS[:, new], in0=nS[:, new], scalar=-1.0, in1=mask[:, 0:DECT], op0=ALU.add, op1=ALU.mult))
                op(dve.tensor_scalar(nS[:, new], nS[:, new], 1.0, None, ALU.add))
                W = PAST + DECT
                own.up(dve.memset(pS[:, W:W + 1], 1.0))
                op(dve.tensor_tensor_scan(rev(pS[:, 0:W]), rev(nS[:, :]), rev(nS[:, :]), 1.0, ALU.mult, ALU.bypass))
                dve.tensor_tensor(sS[:, :], sS[:, :], pS[:, 1:W + 1], ALU.mult).then_inc(s_ws, 1)

            for c in range(2):
                dve.wait_ge(s_mld[0], (c + 1) * 96)
                op(dve.memset(mx[0][:, 0:BUFA], 0.0))
                conv(mx[2], mx[0], c, PCW, 4, BUFA, pv[:, c, PCB:PCB + 1])
                dve.sem_inc(s_xc, 1)
                nb = 1 + DECB
                own.up(dve.tensor_copy(so[:, c, SO_A:SO_A + BUFA], mx[0][:, SEQ:SEQ + BUFA]))
                op(dve.tensor_copy(so[:, c, SO_A + BUFA:SO_A + BUFA * nb].rearrange("p (b t) -> p b t", b=DECB),
                                   ext_of(mx[0], BUFA)[:, :, DECT:]))
                dve.wait_ge(s_act, 4 + 3 * c)
                T = lambda n: mx[n][:, 0:TOK]
                op(dve.tensor_scalar(T(7), T(3), 1.0, None, ALU.add))
                op(dve.reciprocal(T(7), T(7)))
                own.up(dve.tensor_scalar(T(3), T(7), 2.0, -1.0, ALU.mult, ALU.add))
                own.up(dve.scalar_tensor_tensor(out=T(5), in0=T(5), scalar=2.0, in1=T(7), op0=ALU.mult, op1=ALU.mult))
                op(dve.tensor_tensor(T(4), T(4), T(2), ALU.mult))
                op(dve.tensor_tensor(T(5), T(5), T(4), ALU.mult))
                dve.wait_ge(s_mst[2], 16 * c)
                own.up(dve.tensor_tensor_scan(mx[6][:, 0:SEQ], mx[3][:, 0:SEQ], mx[5][:, 0:SEQ], 0.0, ALU.mult, ALU.add))
                for b in range(DECB):
                    ts = slice(SEQ + b * DECT, SEQ + (b + 1) * DECT)
                    own.up(dve.tensor_tensor_scan(mx[6][:, ts], mx[3][:, ts], mx[5][:, ts], hs[:, c, b:b + 1], ALU.mult, ALU.add))
                own.sync()
                own.up(dve.tensor_copy(so[:, c, SO_H:SO_H + 1], mx[6][:, SEQ - 1:SEQ]))
                op(dve.tensor_copy(so[:, c, SO_H + 1:SO_H + nb], mx[6][:, SEQ:TOK].rearrange("p (b t) -> p b t", b=DECB)[:, :, DECT - 1]))
                dve.wait_ge(s_act, 5 + 3 * c)
                dve.tensor_tensor(T(6), T(6), T(1), ALU.mult).then_inc(s_mxv, 1)
                dve.wait_ge(s_mxv, 2 * c + 1)
                dve.sem_inc(s_mfree, 1)
                if c == 1:
                    sample_weights()
                dve.wait_ge(s_mld[1], (c + 1) * 64)
                u_s = ext_of(mx[3], BUFB)
                own.up(dve.memset(mx[3][:, 0:BUFB], 0.0))
                own.up(dve.tensor_tensor(mx[3][:, BUFB:BUFB + SEQ], mx[0][:, 0:SEQ], mx[1][:, 0:SEQ], ALU.mult))
                s3 = lambda t: t[:, SEQ:TOK].rearrange("p (b t) -> p b t", b=DECB)
                op(dve.tensor_tensor(u_s[:, :, BUFB:], s3(mx[0]), s3(mx[1]), ALU.mult))
                own.up(dve.tensor_copy(so[:, c, SO_B:SO_B + BUFB], mx[3][:, SEQ:SEQ + BUFB]))
                own.up(dve.tensor_copy(so[:, c, SO_B + BUFB:SO_B + BUFB * nb].rearrange("p (b t) -> p b t", b=DECB), u_s[:, :, DECT:]))
                conv(mx[4], mx[3], c, PBW, 3, BUFB, 0.0)
                dve.tensor_tensor(T(4), T(4), T(2), ALU.mult).then_inc(s_mxv, 1)
                dve.wait_ge(s_mxv, 2 * c + 2)
                dve.sem_inc(s_mfree, 1)
                dve.wait_ge(s_mld[2], (c + 1) * 48)
                own.up(dve.memset(mx[0][:, 0:BUFP], 0.0))
                ext = ext_of(mx[0], BUFP)
                own.sync()
                own.up(dve.tensor_copy(so[:, c, SO_P:SO_P + BUFP], mx[0][:, SEQ:SEQ + BUFP]))
                own.up(dve.tensor_copy(so[:, c, SO_P + BUFP:SO_P + BUFP * nb].rearrange("p (b t) -> p b t", b=DECB), ext[:, :, DECT:]))

                def wider(dst, src, half, rows):
                    a = 2 * half - 1
                    own.up(dve.tensor_tensor(dst[rows, a:BUFP + SEQ], src[rows, a:BUFP + SEQ],
                                             src[rows, a - half:BUFP + SEQ - half], ALU.add))
                    d_, s_ = ext_of(dst, BUFP)[rows], ext_of(src, BUFP)[rows]
                    op(dve.tensor_tensor(d_[:, :, a:], s_[:, :, a:], s_[:, :, a - half:BUFP + DECT - half], ALU.add))

                every, low, high = slice(0, P), slice(0, HD), slice(HD, P)
                wider(mx[1], mx[0], 1, every)
                if c == 0:
                    wider(mx[2], mx[1], 2, high)
                    lo_t, hi_t = mx[1], mx[2]
                else:
                    wider(mx[2], mx[1], 2, every)
                    wider(mx[1], mx[2], 4, every)
                    wider(mx[2], mx[1], 8, high)
                    lo_t, hi_t = mx[1], mx[2]
                for rows, t in ((low, lo_t), (high, hi_t)):
                    own.up(dve.scalar_tensor_tensor(out=mx[5][rows, 0:SEQ], in0=t[rows, BUFP:BUFP + SEQ], scalar=pv[rows, c, PINV:PINV + 1],
                                                    in1=mx[0][rows, BUFP:BUFP + SEQ], op0=ALU.mult, op1=ALU.subtract))
                    own.up(dve.scalar_tensor_tensor(out=s3(mx[5])[rows], in0=ext_of(t, BUFP)[rows][:, :, BUFP:], scalar=pv[rows, c, PINV:PINV + 1],
                                                    in1=ext[rows][:, :, BUFP:], op0=ALU.mult, op1=ALU.subtract))
                own.sync()
                cnt = lambda rows: mask[rows, DECT + 16 * c:DECT + 16 * c + 16]
                for rows, t in ((low, lo_t), (high, hi_t)):
                    own.up(dve.tensor_tensor(mx[5][rows, 0:16], t[rows, BUFP:BUFP + 16], cnt(rows), ALU.mult))
                own.sync()
                op(dve.tensor_tensor(mx[5][:, 0:16], mx[5][:, 0:16], mx[0][:, BUFP:BUFP + 16], ALU.subtract))
                dve.sem_inc(s_xc, 1)
                dve.sem_inc(s_mfree, 1)

            dve.wait_ge(s_wte, 5)
            for m in s_mst:
                dve.wait_ge(m, 32)
            op(dve.memset(pP[:, SEQ:SEQ + 1], 1.0))
            dve.sem_inc(s_yc0, 16)
            dve.sem_inc(s_ycs, 16)
            dve.sem_inc(s_w, 1)
            with dve.Fori(0, 2) as hp:
                def result(n):
                    hl_, qt = divmod(n, QT)
                    rows = slice(HD * hl_, HD * hl_ + HD)
                    if n == 0:
                        dve.wait_ge(s_yc0, hp * 16 + 16)
                        dve.wait_ge(s_ycs, hp * 16 + 16)
                    dve.wait_ge(s_av, hp * 80 + groups_until(n + 1))
                    dve.tensor_copy(ycT[rows, qt * P:(qt + 1) * P], PS[rows, 6 + n % 2, 0:P]).then_inc(s_yc, 1)

                for n in range(2 * QT):
                    W = (n % QT + 1) * P
                    dve.wait_ge(s_msk, hp * 32 + (n + 1))
                    dve.wait_ge(s_w, hp * 32 + (n + 1))
                    dve.tensor_tensor_scan(rev(pP[:, SEQ - W:SEQ]), rev(nP[:, n % (AHEAD + 1), 0:W]), rev(nP[:, n % (AHEAD + 1), 0:W]), 1.0,
                                           ALU.mult, ALU.bypass).then_inc(s_scan, 1)
                    dve.wait_ge(s_scan, hp * 32 + (n + 1))
                    dve.tensor_tensor(sP[:, n % (AHEAD + 1), 0:W], sP[:, n % (AHEAD + 1), 0:W], pP[:, SEQ - W + 1:SEQ + 1], ALU.mult).then_inc(s_w, 1)
                    if n >= 1:
                        result(n - 1)
                result(2 * QT - 1)

            dve.wait_ge(s_vnuse, DECB + 2)
            for h in range(NH):
                rows = slice(HD * (h % 2), HD * (h % 2) + HD)
                src = PS[rows, ZB, 64 * (h // 2):64 * (h // 2) + DECB * 8].rearrange("p (b s) -> p b s", s=8)[:, :, DECT * (h % 2):DECT * (h % 2) + DECT]
                dve.tensor_copy(ycs[rows, h // 2, :].rearrange("p (b t) -> p b t", b=DECB), src).then_inc(s_yse, 1)


            dve.sem_inc(s_hf, 2)
            dve.sem_inc(s_fev, 4)
            dve.sem_inc(s_hl, 1)

            def lo_after(n, u):
                dve.wait_ge(s_step, n + 1)
                split_lo(u, n + (NC_IN + 3))

            def split_y(blk):
                for g in range(2):
                    dve.wait_ge(s_yh, blk * 2 + (g + 1))
                    dve.tensor_tensor(al[:, 4 * g:4 * g + 4, :], yin[:, 4 * g:4 * g + 4, :], ah[:, 4 * g:4 * g + 4, :].bitcast(F32),
                                      ALU.subtract).then_inc(s_yl, 1)

            def out_proj(n, blk):
                for s in range(KT):
                    lo_after(n + s, s % 2)
                    dve.scalar_tensor_tensor(out=xr[:, s, :], in0=xr[:, s, :], scalar=ALPHA, in1=PS[:, s % 4, 0:BLK],
                                             op0=ALU.mult, op1=ALU.add).then_inc(s_oev, 1)

            def hidden_lo(f, at, u):
                dve.wait_ge(s_r, f + 5)
                dve.wait_ge(s_hl, f + 1)
                dve.tensor_tensor(hf[:, :], rbuf[:, u % 2, :], rbuf[:, u % 2, :], ALU.mult).then_inc(s_hf, 1)
                dve.wait_ge(s_hf, f + 3)
                dve.wait_ge(s_hh, f + 1)
                dve.tensor_tensor(tile_of(hl, at), hf[:, :], tile_of(hh, at).bitcast(F32), ALU.subtract).then_inc(s_hl, 1)

            def ln_var(lnb, j):
                dve.wait_ge(s_ft, lnb + (j + 1))
                bank = 4 + 2 * (j % 2)
                for h in range(2):
                    ins = dve.bn_stats(bn[0:ROW, j, h, :], PS[0:ROW, bank + h, :])
                own.up(ins)
                own.sync()
                own.up(dve.bn_aggr(mv[0:ROW, j, :], bn[0:ROW, j, :, :]))
                own.sync()
                dve.tensor_scalar(var[0:ROW, j:j + 1], mv[0:ROW, j, 1:2], EPS, None, ALU.add).then_inc(s_ve, 1)

            def ln_nmr(lnb, j):
                dve.wait_ge(s_std, lnb + (NB + j + 1))
                own.up(dve.reciprocal(rstd[0:ROW, j:j + 1], std[0:ROW, j:j + 1]))
                own.sync()
                dve.scalar_tensor_tensor(out=nmr[0:ROW, j:j + 1], in0=mv[0:ROW, j, 0:1], scalar=-1.0,
                                         in1=rstd[0:ROW, j:j + 1], op0=ALU.mult, op1=ALU.mult).then_inc(s_nmr, 1)

            def norm_task(lnb, d):
                if 0 < d <= NR:
                    ln_nmr(lnb, d - 1)
                if d < NR:
                    ln_var(lnb, d)

            def back_task(blk, d):
                if 5 <= d < 9:
                    back_lo(blk, NB * KT, lambda k: xr[:, k, :], lambda k: ah[:, k, :], lambda k: al[:, k, :], 2,
                            range(2 * d - 10, 2 * d - 8))

            def output(o, u, half):
                dst, ps = tile_of(acc, o), PS[:, u % 4, 0:BLK]
                if half == 0:
                    dve.scalar_tensor_tensor(out=dst, in0=tile_of(xr, o), scalar=ALPHA, in1=ps, op0=ALU.mult,
                                             op1=ALU.add).then_inc(s_fev, 1)
                else:
                    dve.tensor_tensor(dst, dst, ps, ALU.add).then_inc(s_fev, 1)

            def ffn_body(b, n):
                with dve.Fori(0, (HF - NN) // 4) as i:
                    for u in range(4):
                        lo_after(n + i * 4 + u, u % 2)
                        hidden_lo(b * FT + i * 4 + (NN + u), i * 4 + (NN + u), u)
                with dve.Fori(0, 2) as i:
                    for u in range(4):
                        for q in range(2):
                            lo_after(n + i * 8 + (SB_ + 2 * u + q), q)
                        output(i * 4 + u, u, 0)
                with dve.Fori(0, HF // 4) as i:
                    for u in range(4):
                        lo_after(n + i * 4 + (SC_ + u), u % 2)
                        hidden_lo(b * FT + i * 4 + (HF + u), i * 4 + u, u)
                dve.wait_ge(s_fev, b * (2 * KT) + (KT + 4))

            dve.wait_ge(s_yin0, 16)
            split_y(0)
            dve.wait_ge(s_pair, 3)
            dve.wait_ge(s_ycs, 48)
            dve.wait_ge(s_x1in0, 16)
            out_proj(0, 0)
            for d in range(9):
                norm_task(0, d)
                back_task(0, d)
            for a in range(NN):
                lo_after(KT + a, a % 2)
                hidden_lo(a, a, a)
            with own.loop(NB - 1, 24) as b:
                n = b * STEPS + PRO
                ffn_body(b, n)
                dve.wait_ge(s_yin, b * 16 + 16)
                split_y(b + 1)
                for s in range(D1):
                    lo_after(n + (SD_ + s), s % 2)
                    if s % 2:
                        output(s // 2, s // 2, 1)
                dve.wait_ge(s_x1in, b * 16 + 16)
                out_proj(n + SE_, b + 1)
                for d in range(SN_ - SD2):
                    lo_after(n + (SD2 + d), d % 2)
                    if d % 2:
                        output((D1 + d) // 2, (D1 + d) // 2, 1)
                    norm_task(b * 8 + 4, d)
                    back_task(b + 1, d)
                for a in range(NN):
                    lo_after(n + (SN_ + a), a % 2)
                    hidden_lo(b * FT + (FT + a), a, a)
                    norm_task(b * 8 + 8, a)
            b, n = NB - 1, (NB - 1) * STEPS + PRO
            ffn_body(b, n)
            for o in range(KT):
                if o < KT - 1:
                    for q in range(2):
                        lo_after(n + (SD_ + 2 * o + q), q)
                else:
                    dve.wait_ge(s_step, TOTAL)
                output(o, o, 1)
            for d in range(NR + 1):
                norm_task(b * 8 + 4, d)

        @block.gpsimd
        def _(pool):
            own = Tally(pool, s_pool)
            for u in range(2):
                pool.wait_ge(s_stg[u], 16 * (NC_IN // 2) + 16)
            for c in range(2):
                if c:
                    pool.wait_ge(s_mfree, 3 * c)
                for dst, t in ((mx[0][:, BUFA:BUFA + SEQ], XA), (mx[1][:, 0:SEQ], GA)):
                    pool.dma_start(dst, proj_d[AT[t, c], :, 0:SEQ]).then_inc(s_mld[0], 16)
                pool.dma_start(ext_of(mx[0], BUFA)[:, :, BUFA:], new_of(proj_d[AT[XA, c]])).then_inc(s_mld[0], 16)
                pool.dma_start(ext_of(mx[0], BUFA)[:, :, 0:BUFA], st_a[c]).then_inc(s_mld[0], 16)
                pool.dma_start(mx[1][:, SEQ:TOK], proj_d[AT[GA, c], :, SEQ:TOK]).then_inc(s_mld[0], 16)
                pool.dma_start(hs[:, c, :], st_h[c]).then_inc(s_mld[0], 16)
                pool.wait_ge(s_mxv, 2 * c + 1)
                pool.dma_start(y_d[0 + c], mx[6][:, 0:TOK]).then_inc(s_mst[0], 16)
                pool.wait_ge(s_mfree, 3 * c + 1)
                pool.dma_start(mx[0][:, 0:TOK], proj_d[AT[XB, c]]).then_inc(s_mld[1], 16)
                pool.dma_start(mx[1][:, 0:TOK], proj_d[AT[GC, c]]).then_inc(s_mld[1], 16)
                pool.dma_start(mx[2][:, 0:TOK], proj_d[AT[GB, c]]).then_inc(s_mld[1], 16)
                pool.dma_start(ext_of(mx[3], BUFB)[:, :, 0:BUFB], st_b[c]).then_inc(s_mld[1], 16)
                pool.wait_ge(s_mxv, 2 * c + 2)
                pool.dma_start(y_d[2 + c], mx[4][:, 0:TOK]).then_inc(s_mst[1], 16)
                pool.wait_ge(s_mfree, 3 * c + 2)
                pool.dma_start(mx[0][:, BUFP:BUFP + SEQ], proj_d[AT[XP, c], :, 0:SEQ]).then_inc(s_mld[2], 16)
                pool.dma_start(ext_of(mx[0], BUFP)[:, :, BUFP:], new_of(proj_d[AT[XP, c]])).then_inc(s_mld[2], 16)
                pool.dma_start(ext_of(mx[0], BUFP)[:, :, 0:BUFP], st_p[c]).then_inc(s_mld[2], 16)
                pool.wait_ge(s_mxa, c + 1)
                pool.dma_start(y_d[6 + c], mx[6][:, 0:TOK]).then_inc(s_mst[2], 16)
            pool.wait_ge(s_mfree, 6)
            pool.dma_start(so_out, so[:, :, :]).then_inc(s_so, 16)


            with pool.Fori(0, 2) as hp:
                for n in range(2 * QT):
                    W = (n % QT + 1) * P
                    wait_apart(pool, s_sn, hp * 80 + groups_until(n + 1))
                    for t, fill in ((sP, 0.0), (nP, 1.0)):
                        diag = t[:, n % (AHEAD + 1), W - P:W]
                        ins = pool.affine_select(out=diag, in_=diag, compare_op=ALU.is_gt, fill=fill, base=0,
                                                 pattern=[[-1, P]], channel_multiplier=1)
                    ins.then_inc(s_msk, 1)
            pool.wait_ge(s_yc0, 48)
            for m in s_mst:
                pool.wait_ge(m, 32)
            pool.dma_start(yin[:, :, :], y_d[:, :, 0:BLK].rearrange("k p t -> p k t")).then_inc(s_yin0, 16)
            pool.dma_start(xr[:, :, :], x1_d[:, :, 0:BLK].rearrange("k p t -> p k t")).then_inc(s_x1in0, 16)
            pool.wait_ge(s_const, CONST_ALL + 16)

            def store_rows(b, lnb):
                for j in range(NR):
                    pool.wait_ge(s_nat, lnb + (NATB + j + 1))
                    row = nat3[0:ROW, j, :]
                    own.op(pool.tensor_tensor(row, row, gb2[0:ROW, 0, :], ALU.mult))
                    pool.tensor_tensor(row, row, gb2[0:ROW, 1, :], ALU.add).then_inc(s_row, 1)
                    pool.wait_ge(s_row, b * NR + (j + 1))
                    pool.dma_start(y_out[bass.ds(b * BLK + j * ROW, ROW)], row).then_inc(s_out, 16)
                pool.wait_ge(s_out, b * (16 * NR) + 16 * NR)
                pool.sem_inc(s_rowfree, 1)

            with own.loop(NB - 1, NR) as b:
                store_rows(b, b * 8 + 8)
            store_rows(NB - 1, (NB - 1) * 8 + 4)


def _tiles(w, rows, cols):
    a = w.reshape(rows, KT, P, cols, P)
    return a.transpose(3, 0, 2, 1, 4).reshape(cols * rows, P, KT * P)


def _channels(a):
    a = np.moveaxis(a, -1, 0)
    return np.ascontiguousarray(a.reshape((2, P) + a.shape[1:]))


def kernel(**inputs):
    import concourse.bacc as bacc
    from concourse.bass_utils import run_bass_kernel_spmd

    f = {k: np.asarray(v) for k, v in inputs.items()}
    w_in = _tiles(f["w_in"][0], 1, NC_IN)[[2 * g + c for g, c in ORDER]]
    w_o, w_1 = _tiles(f["w_out"][0], 1, KT), _tiles(f["w_ff1"][0], 1, FT)
    w_2 = _tiles(f["w_ff2"][0], 4, KT).reshape(KT, 4, P, KT * P)
    w_2 = [w_2[:, 2 * h:2 * h + 2].reshape(HF, P, KT * P) for h in range(2)]
    iteration = [w_1[NN:HF], w_2[0], w_1[HF:], w_2[1][:D1], w_o, w_2[1][D1:], w_1[:NN]]
    w_all = np.concatenate([w_in, w_o, w_1[:NN]] + iteration)
    per_channel = [f["conv_a_w"][0].T, f["conv_a_b"][0][:, None], f["lru_ba"][0][:, None], f["lru_bx"][0][:, None],
                   f["lru_lambda"][0][:, None], f["conv_b_w"][0].T, f["pool_scale"][0][:, None],
                   np.repeat(np.float32(1.0) / np.array(WINDOWS, np.float32), HD)[:, None]]
    pvec = np.concatenate(per_channel, 1).reshape(2, P, NPV).transpose(1, 0, 2)
    lnp = np.stack([f[k].reshape(KT, P) for k in ("ln_in_g", "ln_in_b", "ln1_g", "ln1_b")]).transpose(2, 0, 1)
    rows2 = np.broadcast_to(np.stack([f["ln2_g"][0], f["ln2_b"][0]]), (P, 2, D))
    masks = np.zeros((P, DECT + 32), np.float32)
    masks[:, :DECT] = np.arange(DECT)[None] < (np.arange(P) % DECT)[:, None]
    for c in range(2):
        w = np.repeat(WINDOWS[2 * c:2 * c + 2], HD)[:, None]
        masks[:, DECT + 16 * c:DECT + 16 * c + 16] = 1.0 / np.minimum(w, np.arange(16)[None] + 1)
    n_pool = f["cache_k"].shape[1]
    arrays = {
        "x_all": np.concatenate([f["x_prompt"].reshape(SEQ, D), f["x_sample"].reshape(SMP, D)]),
        "w_all": w_all, "pvec": pvec, "lnp": lnp, "rows2": rows2,
        "gates_a": f["lru_wa"][0], "gates_x": f["lru_wx"][0], "poolw": f["pool_w"][0],
        "sbh": np.broadcast_to(f["sb_bias"][0], (P, NH)),
        "sbr": np.tile(np.repeat(f["sb_bias"][0], DECT), DECB)[:, None],
        "masks": masks, "ident_d": np.eye(P, dtype=np.float32),
        "ck": f["cache_k"].reshape(n_pool, PAGE, 2 * P), "cv": f["cache_v"].reshape(n_pool, PAGE, 2 * P),
        "ptab": f["page_table"].reshape(1, DECB * NPG),
        "st_h": _channels(f["state_rglru_h"][0]), "st_a": _channels(f["state_conv_a"][0]),
        "st_b": _channels(f["state_conv_b"][0]), "st_p": _channels(f["state_pool"][0]),
    }
    arrays = {k: np.ascontiguousarray(v) for k, v in arrays.items()}
    outs = {"y_out": (TOK, D), "kv_out": (4, P, TOK), "so_out": (P, 2, SO_N)}
    nc = bacc.Bacc("TRN2", target_bir_lowering=False, num_devices=1)
    args = [nc.dram_tensor(k, a.shape, mybir.dt.from_np(a.dtype), kind="ExternalInput").ap() for k, a in arrays.items()]
    args += [nc.dram_tensor(k, s, F32, kind="ExternalOutput").ap() for k, s in outs.items()]
    build(nc, *args)
    got = run_bass_kernel_spmd(nc, [arrays], core_ids=[0]).results[0]
    y, kv, so = got["y_out"], got["kv_out"], got["so_out"]
    kv = kv.reshape(2, 2 * P, TOK).transpose(0, 2, 1)

    def prompt(a):
        return np.ascontiguousarray(a[:SEQ].reshape(1, 1, SEQ, NH, HD))

    def sample(a):
        return np.ascontiguousarray(a[SEQ:].reshape(1, DECB, DECT, NH, HD))

    so = so.transpose(1, 0, 2).reshape(2 * P, SO_N).T

    def state(at, rows):
        return (np.ascontiguousarray(so[at:at + rows].reshape(1, 1, rows, 2 * P)),
                np.ascontiguousarray(so[at + rows:at + rows * (1 + DECB)].reshape(1, DECB, rows, 2 * P)))

    h_p, h_s = state(SO_H, 1)
    a_p, a_s = state(SO_A, BUFA)
    b_p, b_s = state(SO_B, BUFB)
    p_p, p_s = state(SO_P, BUFP)
    return (y[:SEQ].reshape(1, SEQ, D), y[SEQ:].reshape(DECB, DECT, D), prompt(kv[0]), prompt(kv[1]), sample(kv[0]), sample(kv[1]),
            h_p.reshape(1, 1, 2 * P), h_s.reshape(1, DECB, 2 * P), a_p, a_s, b_p, b_s, p_p, p_s)
```
